# Optimizing a Trainium2 kernel written in Bass

```python
import math
import jax, jax.numpy as jnp
from jax import lax
import numpy as np

D_MODEL = 1024
BATCH = 1
SEQ = 2048
DEPTH = 1

D_MIX = D_MODEL
D_LRU = D_MIX // 2
D_HY = D_MIX - D_LRU
LRU_HEADS = 8
LRU_HEAD_DIM = D_LRU // LRU_HEADS
LRU_CONV = 4
LRU_C = 8.0
HY_ORDER = 2
HY_CONV = 3
HY_BANDS = 16
HY_EMB = 2 * HY_BANDS + 1
HY_FFN = 64
HY_FAST_DECAY_PCT = 0.3
HY_SLOW_DECAY_PCT = 1.5
HY_DECAY_TARGET = 1e-2
D_IN = 2 * D_LRU + (HY_ORDER + 1) * D_HY
N_GROUPS = 4
EXPERTS_PER_GROUP = 8
N_EXPERTS = N_GROUPS * EXPERTS_PER_GROUP
TOP_K = 2
D_EXPERT = D_MODEL // 2
MOE_BLOCK = 128
EPS = 1e-6

kernel_name = "hybrid_lru_hyena_hmoe_encoder"

def _rmsnorm(x, g):
    x32 = x.astype(jnp.float32)
    y = x32 * lax.rsqrt(jnp.mean(x32 * x32, axis=-1, keepdims=True) + EPS)
    return (y * g.astype(jnp.float32)).astype(x.dtype)

def _dwconv(x, w, b, pad):
    c = x.shape[-1]
    y = lax.conv_general_dilated(x, w[:, None, :].astype(x.dtype), window_strides=(1,), padding=[pad], dimension_numbers=("NWC", "WIO", "NWC"), feature_group_count=c)
    return y + b.astype(x.dtype)

def _lin_combine(c1, c2):
    a1, b1 = c1
    a2, b2 = c2
    return a1 * a2, a2 * b1 + b2

def _rg_lru(xc, wr, br, wi, bi, lam, reverse):
    bsz, seq, c = xc.shape
    xh = xc.reshape(bsz, seq, LRU_HEADS, LRU_HEAD_DIM)
    r = jax.nn.sigmoid((jnp.einsum("bshi,hij->bshj", xh, wr).reshape(bsz, seq, c) + br).astype(jnp.float32))
    i = jax.nn.sigmoid((jnp.einsum("bshi,hij->bshj", xh, wi).reshape(bsz, seq, c) + bi).astype(jnp.float32))
    log_a = -LRU_C * r * jax.nn.softplus(-lam.astype(jnp.float32))
    a = jnp.exp(log_a)
    b = jnp.sqrt(-jnp.expm1(2.0 * log_a)) * (i * xc.astype(jnp.float32))
    _, h = lax.associative_scan(_lin_combine, (a, b), axis=1, reverse=reverse)
    return h

def _hyena_filters(seq, fw1, fb1, ff1, fw2, fb2, ff2, fw3):
    f32 = jnp.float32
    pos = jnp.arange(seq, dtype=f32)
    t = jnp.linspace(0.0, 1.0, seq, dtype=f32)
    w = (2.0 * math.pi / seq) * pos
    bands = jnp.linspace(1e-4, HY_BANDS - 1, HY_BANDS, dtype=f32)
    ang = w[:, None] * bands[None, :]
    feats = jnp.concatenate([t[:, None], jnp.cos(ang), jnp.sin(ang)], axis=-1)
    z = jnp.sin(ff1.astype(f32) * (feats @ fw1.astype(f32) + fb1.astype(f32)))
    z = jnp.sin(ff2.astype(f32) * (z @ fw2.astype(f32) + fb2.astype(f32)))
    h = (z @ fw3.astype(f32)).reshape(seq, 2, HY_ORDER, D_HY)
    deltas = jnp.abs(jnp.linspace(math.log(HY_DECAY_TARGET) / HY_SLOW_DECAY_PCT, math.log(HY_DECAY_TARGET) / HY_FAST_DECAY_PCT, D_HY, dtype=f32))
    h = h * jnp.exp(-t[:, None, None, None] * deltas)
    hf, hb = h[:, 0], h[:, 1]
    k = jnp.concatenate([hf, jnp.zeros((1, HY_ORDER, D_HY), f32), hb[1:][::-1]], axis=0)
    k = k / (jnp.sum(jnp.abs(k), axis=0, keepdims=True) + EPS)
    return jnp.fft.rfft(k, axis=0)

def _long_conv(z, kf, skip):
    seq = z.shape[1]
    zf = jnp.fft.rfft(z, n=2 * seq, axis=1)
    y = jnp.fft.irfft(zf * kf[None], n=2 * seq, axis=1)[:, :seq]
    return y + z * skip

def _hyena(u, conv_w, conv_b, kf, skip):
    uc = _dwconv(u, conv_w, conv_b, (1, 1)).astype(jnp.float32)
    v, x1, x2 = uc[..., :D_HY], uc[..., D_HY:2 * D_HY], uc[..., 2 * D_HY:]
    skip = skip.astype(jnp.float32)
    z = x1 * _long_conv(v, kf[:, 0], skip[0])
    z = x2 * _long_conv(z, kf[:, 1], skip[1])
    return z

def _hier_moe(h, wg, bg, we, be, w1, w3, w2):
    bsz, seq, d = h.shape
    n_tok = bsz * seq
    hf = h.reshape(n_tok, d)
    lg = (hf @ wg + bg).astype(jnp.float32)
    pg = jax.nn.softmax(lg, axis=-1)
    g_idx = jnp.argmax(lg, axis=-1)
    g_p = jnp.take_along_axis(pg, g_idx[:, None], axis=1)[:, 0]
    le = (hf @ we + be).astype(jnp.float32).reshape(n_tok, N_GROUPS, EXPERTS_PER_GROUP)
    le = jnp.take_along_axis(le, g_idx[:, None, None], axis=1)[:, 0]
    pe = jax.nn.softmax(le, axis=-1)
    top_p, top_i = lax.top_k(pe, TOP_K)
    gate = g_p[:, None] * top_p / jnp.sum(top_p, axis=-1, keepdims=True)
    eid = (g_idx[:, None] * EXPERTS_PER_GROUP + top_i).astype(jnp.int32)
    n_assign = n_tok * TOP_K
    flat_e = eid.reshape(n_assign)
    order = jnp.argsort(flat_e)
    sorted_e = flat_e[order]
    sorted_tok = (order // TOP_K).astype(jnp.int32)
    sorted_gate = gate.reshape(n_assign)[order]
    counts = jnp.bincount(flat_e, length=N_EXPERTS).astype(jnp.int32)
    padded = (counts + MOE_BLOCK - 1) // MOE_BLOCK * MOE_BLOCK
    raw_start = jnp.cumsum(counts) - counts
    pad_end = jnp.cumsum(padded)
    pad_start = pad_end - padded
    dest = pad_start[sorted_e] + jnp.arange(n_assign, dtype=jnp.int32) - raw_start[sorted_e]
    n_blocks = (n_assign + MOE_BLOCK - 1) // MOE_BLOCK + N_EXPERTS
    n_slots = n_blocks * MOE_BLOCK
    slot_tok = jnp.full((n_slots,), n_tok, jnp.int32).at[dest].set(sorted_tok)
    block_e = jnp.minimum(jnp.searchsorted(pad_end, jnp.arange(n_blocks, dtype=jnp.int32) * MOE_BLOCK, side="right"), N_EXPERTS - 1)
    h_pad = jnp.concatenate([hf, jnp.zeros((1, d), hf.dtype)], axis=0)
    xb = h_pad[slot_tok].reshape(n_blocks, MOE_BLOCK, d)

    def expert_block(args):
        xblk, e = args
        a = jax.nn.silu(xblk @ w1[e]) * (xblk @ w3[e])
        return a @ w2[e]

    yb = lax.map(expert_block, (xb, block_e)).reshape(n_slots, d)
    y = jnp.zeros((n_tok, d), h.dtype).at[sorted_tok].add(yb[dest] * sorted_gate[:, None].astype(h.dtype))
    return y.reshape(bsz, seq, d)

def setup_inputs(seed: int = 0) -> dict:
    key = jax.random.key(seed)
    ks = iter(jax.random.split(key, 48))

    def nrm(shape, scale):
        return jax.random.normal(next(ks), shape, jnp.float32) * scale

    def gain(shape):
        return 1.0 + nrm(shape, 0.02)

    def lam_init():
        u = jax.random.uniform(next(ks), (DEPTH, D_LRU), jnp.float32, minval=0.9, maxval=0.999)
        a = u ** (1.0 / LRU_C)
        return jnp.log(a) - jnp.log1p(-a)

    hd = LRU_HEAD_DIM
    return {
        "x": nrm((BATCH, SEQ, D_MODEL), 1.0),
        "norm_mix_g": gain((DEPTH, D_MODEL)),
        "w_in": nrm((DEPTH, D_MODEL, D_IN), D_MODEL ** -0.5),
        "lru_conv_w": nrm((DEPTH, LRU_CONV, D_LRU), LRU_CONV ** -0.5),
        "lru_conv_b": nrm((DEPTH, D_LRU), 0.01),
        "lru_wr_f": nrm((DEPTH, LRU_HEADS, hd, hd), hd ** -0.5),
        "lru_br_f": nrm((DEPTH, D_LRU), 0.01),
        "lru_wi_f": nrm((DEPTH, LRU_HEADS, hd, hd), hd ** -0.5),
        "lru_bi_f": nrm((DEPTH, D_LRU), 0.01),
        "lru_lambda_f": lam_init(),
        "lru_wr_b": nrm((DEPTH, LRU_HEADS, hd, hd), hd ** -0.5),
        "lru_br_b": nrm((DEPTH, D_LRU), 0.01),
        "lru_wi_b": nrm((DEPTH, LRU_HEADS, hd, hd), hd ** -0.5),
        "lru_bi_b": nrm((DEPTH, D_LRU), 0.01),
        "lru_lambda_b": lam_init(),
        "hy_conv_w": nrm((DEPTH, HY_CONV, (HY_ORDER + 1) * D_HY), HY_CONV ** -0.5),
        "hy_conv_b": nrm((DEPTH, (HY_ORDER + 1) * D_HY), 0.01),
        "hy_filt_w1": nrm((DEPTH, HY_EMB, HY_FFN), HY_EMB ** -0.5),
        "hy_filt_b1": nrm((DEPTH, HY_FFN), 0.1),
        "hy_filt_freq1": gain((DEPTH, HY_FFN)),
        "hy_filt_w2": nrm((DEPTH, HY_FFN, HY_FFN), HY_FFN ** -0.5),
        "hy_filt_b2": nrm((DEPTH, HY_FFN), 0.1),
        "hy_filt_freq2": gain((DEPTH, HY_FFN)),
        "hy_filt_w3": nrm((DEPTH, HY_FFN, 2 * HY_ORDER * D_HY), HY_FFN ** -0.5),
        "hy_skip": nrm((DEPTH, HY_ORDER, D_HY), 1.0),
        "grp_norm_lru_g": gain((DEPTH, D_LRU)),
        "grp_norm_hy_g": gain((DEPTH, D_HY)),
        "w_out": nrm((DEPTH, D_MIX, D_MODEL), D_MIX ** -0.5),
        "norm_ffn_g": gain((DEPTH, D_MODEL)),
        "router_group_w": nrm((DEPTH, D_MODEL, N_GROUPS), D_MODEL ** -0.5),
        "router_group_b": nrm((DEPTH, N_GROUPS), 0.01),
        "router_expert_w": nrm((DEPTH, D_MODEL, N_EXPERTS), D_MODEL ** -0.5),
        "router_expert_b": nrm((DEPTH, N_EXPERTS), 0.01),
        "exp_w1": nrm((DEPTH, N_EXPERTS, D_MODEL, D_EXPERT), D_MODEL ** -0.5),
        "exp_w3": nrm((DEPTH, N_EXPERTS, D_MODEL, D_EXPERT), D_MODEL ** -0.5),
        "exp_w2": nrm((DEPTH, N_EXPERTS, D_EXPERT, D_MODEL), D_EXPERT ** -0.5),
        "norm_final_g": gain((D_MODEL,)),
    }

def reference(x, norm_mix_g, w_in, lru_conv_w, lru_conv_b, lru_wr_f, lru_br_f, lru_wi_f, lru_bi_f, lru_lambda_f, lru_wr_b, lru_br_b, lru_wi_b, lru_bi_b, lru_lambda_b, hy_conv_w, hy_conv_b, hy_filt_w1, hy_filt_b1, hy_filt_freq1, hy_filt_w2, hy_filt_b2, hy_filt_freq2, hy_filt_w3, hy_skip, grp_norm_lru_g, grp_norm_hy_g, w_out, norm_ffn_g, router_group_w, router_group_b, router_expert_w, router_expert_b, exp_w1, exp_w3, exp_w2, norm_final_g):
    seq = x.shape[1]
    for l in range(DEPTH):
        hn = _rmsnorm(x, norm_mix_g[l])
        proj = hn @ w_in[l]
        lru_x = proj[..., :D_LRU]
        lru_gate = proj[..., D_LRU:2 * D_LRU]
        hy_u = proj[..., 2 * D_LRU:]
        xc = _dwconv(lru_x, lru_conv_w[l], lru_conv_b[l], (2, 1))
        h_lru = _rg_lru(xc, lru_wr_f[l], lru_br_f[l], lru_wi_f[l], lru_bi_f[l], lru_lambda_f[l], False) + _rg_lru(xc, lru_wr_b[l], lru_br_b[l], lru_wi_b[l], lru_bi_b[l], lru_lambda_b[l], True)
        y_lru = (h_lru * jax.nn.gelu(lru_gate.astype(jnp.float32))).astype(x.dtype)
        kf = _hyena_filters(seq, hy_filt_w1[l], hy_filt_b1[l], hy_filt_freq1[l], hy_filt_w2[l], hy_filt_b2[l], hy_filt_freq2[l], hy_filt_w3[l])
        y_hy = _hyena(hy_u, hy_conv_w[l], hy_conv_b[l], kf, hy_skip[l]).astype(x.dtype)
        y_cat = jnp.concatenate([_rmsnorm(y_lru, grp_norm_lru_g[l]), _rmsnorm(y_hy, grp_norm_hy_g[l])], axis=-1)
        x = x + y_cat @ w_out[l]
        x = x + _hier_moe(_rmsnorm(x, norm_ffn_g[l]), router_group_w[l], router_group_b[l], router_expert_w[l], router_expert_b[l], exp_w1[l], exp_w3[l], exp_w2[l])
    return _rmsnorm(x, norm_final_g)


_drawn_inputs = setup_inputs


def setup_inputs(seed=0):
    import zlib

    import numpy as np

    out = dict(_drawn_inputs(seed))
    spreads = {}
    factors = {'lru_br_f': 40.641,
     'lru_bi_f': 35.351,
     'lru_br_b': 40.024,
     'lru_bi_b': 33.133,
     'hy_conv_b': 3.439,
     'hy_filt_b1': 3.897,
     'hy_filt_freq1': 8.0,
     'hy_filt_b2': 4.73,
     'hy_filt_freq2': 64.0,
     'grp_norm_lru_g': 12.182,
     'grp_norm_hy_g': 12.93,
     'router_group_b': 28.667,
     'router_expert_b': 34.167,
     'norm_final_g': 7.222,
     'norm_ffn_g': 6.44}
    for name, (base, spread) in spreads.items():
        noise = np.random.default_rng([zlib.crc32(name.encode()), seed]).standard_normal(out[name].shape)
        drawn = base * np.exp(spread * noise) if base else spread * noise
        out[name] = __import__('jax').numpy.asarray(drawn.astype(out[name].dtype))
    for name, factor in factors.items():
        out[name] = (out[name] * factor).astype(out[name].dtype)
    return out
```

```python
import math
from contextlib import ExitStack

import numpy as np

import concourse.bass as bass
from concourse import mybir
from concourse.bass import ds

P = 128
SEQ, D = 2048, 1024
CH = 512
KC = D // P
CT = CH // P
NCHUNK = SEQ // 512
EPS = 1e-6

N = 2 * SEQ
R = 64
HALF = R // 2
NT = 16

N_GROUPS, PER_GROUP = 4, 8
N_EXP = N_GROUPS * PER_GROUP
D_EXP = 512
N_BLOCKS = SEQ * 2 // P + N_EXP
N_SLOTS = N_BLOCKS * P

F32, I32 = mybir.dt.float32, mybir.dt.int32
ALU, ACT = mybir.AluOpType, mybir.ActivationFunctionType
AX = mybir.AxisListType


class Steps:

    def __init__(self, eng, sem, base=0):
        self.eng, self.sem, self.base, self.n = eng, sem, base, 0

    def __call__(self, ins):
        self.n += 1
        ins.then_inc(self.sem, 1)
        self.eng.wait_ge(self.sem, self.base + self.n)


def phase_semaphores(nc, ctx, suffix=""):
    taken = []

    def sem(name):
        taken.append(nc.alloc_semaphore(name=name + suffix))
        return taken[-1]

    def give_back():
        with nc.Block() as block:
            @block.sync
            def _(sp):
                for s in taken:
                    sp.sem_clear(s)
        for s in taken:
            nc.release_semaphore(s)

    ctx.callback(give_back)
    return sem


def load_and_norm(nc, dram, hT, ident):
    GROUPS = 4
    with ExitStack() as ctx:
        sb = lambda name, shape, dt=F32: ctx.enter_context(nc.sbuf_tensor(name, shape, dt))
        sem = phase_semaphores(nc, ctx)
        X = sb("X", [P, NT, D])
        junk = sb("junk", [P, D])
        gain = sb("gain", [P, D])
        xn = sb("xn", [P, 2, D])
        ssq = sb("ssq", [P, NT])
        rstd = sb("rstd", [P, NT])
        tp = [[ctx.enter_context(nc.psum_tensor(f"tp{s}{b}", [P, 512], F32)) for b in range(2)] for s in range(2)]
        x_in = [sem(f"x_in{g}") for g in range(GROUPS)]
        gain_in, ident_in = sem("gain_in"), sem("ident_in")
        squares, steps, rstd_ready = sem("squares"), sem("n_steps"), sem("rstd_ready")
        ms_ready, xn_ready, tp_ready, evacuated = sem("ms_ready"), sem("xn_ready"), sem("tp_ready"), sem("evacuated")
        per = NT // GROUPS
        x_t = dram["x"].rearrange("o (i p) d -> p (o i) d", p=P)
        block = ctx.enter_context(nc.Block())

        @block.sync
        def _(sp):
            for g in range(GROUPS):
                sp.dma_start(X[:, g * per:(g + 1) * per, :], x_t[:, g * per:(g + 1) * per, :]).then_inc(x_in[g], 16)
            sp.dma_start(gain[:, :], dram["norm_mix_g"].rearrange("o d -> (o d)").partition_broadcast(P)).then_inc(gain_in, 16)
            sp.dma_start(ident[:, :], dram["ident"]).then_inc(ident_in, 16)

        @block.scalar
        def _(act):
            for g in range(GROUPS):
                act.wait_ge(x_in[g], 16)
                for i in range(g * per, (g + 1) * per):
                    if i:
                        act.wait_ge(squares, i)
                    act.activation(junk[:, :], X[:, i, :], ACT.Square, accum_out=ssq[:, i:i + 1]).then_inc(squares, 1)
            act.wait_ge(ms_ready, 1)
            act.activation(rstd[:, :], rstd[:, :], ACT.Sqrt).then_inc(rstd_ready, 1)
            with act.Fori(0, NT // 2) as it:
                for s in range(2):
                    i = it * 2 + s
                    act.wait_ge(tp_ready, i + 1)
                    for b in range(2):
                        last = act.activation(hT[:, 4 * b:4 * b + 4, ds(i * P, P)],
                                              tp[s][b].rearrange("p (k t) -> p k t", k=4), ACT.Copy)
                    last.then_inc(evacuated, 1)

        @block.vector
        def _(dve):
            step = Steps(dve, steps)
            dve.wait_ge(squares, NT)
            step(dve.tensor_scalar(ssq[:, :], ssq[:, :], 1.0 / D, EPS, ALU.mult, ALU.add))
            dve.reciprocal(rstd[:, :], ssq[:, :]).then_inc(ms_ready, 1)
            dve.wait_ge(rstd_ready, 1)
            dve.wait_ge(gain_in, 16)
            dve.sem_inc(evacuated, 2)
            with dve.Fori(0, NT // 2) as it:
                for s in range(2):
                    i = it * 2 + s
                    dve.wait_ge(evacuated, i + 1)
                    dve.scalar_tensor_tensor(out=xn[:, s, :], in0=X[:, ds(i, 1), :].rearrange("p a d -> p (a d)"),
                                             scalar=rstd[:, ds(i, 1)], in1=gain[:, :],
                                             op0=ALU.mult, op1=ALU.mult).then_inc(xn_ready, 1)

        @block.tensor
        def _(pe):
            pe.wait_ge(ident_in, 16)
            with pe.Fori(0, NT // 2) as it:
                for s in range(2):
                    i = it * 2 + s
                    pe.wait_ge(xn_ready, i + 1)
                    pe.wait_ge(evacuated, i + 1)
                    for k in range(KC):
                        last = pe.transpose(tp[s][k // 4][:, (k % 4) * P:(k % 4 + 1) * P],
                                            xn[:, s, k * P:(k + 1) * P], ident[:, :])
                    last.then_inc(tp_ready, 1)


Q_CONV_W, Q_CONV_B, Q_BR, Q_BI, Q_LAM = 0, 4, (5, 7), (6, 8), (9, 10)
Q_HW, Q_HB, Q_GA, N_Q = 11, 20, 23, 25


def project_and_lru(nc, dram, hT, ident):
    with ExitStack() as ctx:
        sb = lambda name, shape, dt=F32: ctx.enter_context(nc.sbuf_tensor(name, shape, dt))
        sem = phase_semaphores(nc, ctx)
        W = sb("W", [P, 4, KC, P])
        xraw = sb("xraw", [P, 2 + SEQ + 1])
        xc = sb("xc", [P, SEQ])
        hraw = sb("hraw", [P, 2, 1 + SEQ + 1])
        hc = sb("hc", [P, 2, SEQ])
        tst = sb("tst", [P, NT, P])
        T = [sb("Tf", [P, SEQ]), sb("Tb", [P, SEQ])]
        I = [sb("If", [P, SEQ]), sb("Ib", [P, SEQ])]
        Q = [sb("Qf", [P, SEQ]), sb("Qb", [P, SEQ])]
        G = I[0]
        WG = sb("WG", [P, 4, P])
        prow = sb("prow", [P, P])
        zero = sb("zero", [P, 256])
        PT = sb("PT", [P, N_Q, CT])
        par = sb("par", [P, N_Q])
        sp8 = sb("sp8", [P, 6, 8])
        pj = [ctx.enter_context(nc.psum_tensor(f"pj{n}", [P, 512], F32)) for n in range(4)]
        tp = [ctx.enter_context(nc.psum_tensor(f"tr{n}", [P, 512], F32)) for n in range(4)]
        w_in = [sem(f"w_in{k}") for k in range(5)]
        par_in, zeroed, pt_t, pt_ready, lam_exp = sem("par_in"), sem("zeroed"), sem("pt_t"), sem("pt_ready"), sem("lam_exp")
        wg_in, mm_done, evac, par_ready = sem("wg_in"), sem("mm_done"), sem("evac"), sem("par_ready")
        xc_ready, hc_ready, tr_done, tr_evac, tst_out = sem("xc_ready"), sem("hc_ready"), sem("tr_done"), sem("tr_evac"), sem("tst_out")
        tanh_ready, q1_ready, sqrt_ready, y_ready, y_out = sem("tanh_ready"), sem("q1_ready"), sem("sqrt_ready"), sem("y_ready"), sem("y_out")
        filled = sem("filled_yb")
        sp_passed = sem("sp_passed")
        steps, if_free, lam_ready = sem("p_steps"), sem("p_act"), sem("lam_ready")

        w_v = dram["w_in"].rearrange("o (k p) n -> p (o k) n", p=P)
        USES = 9
        U_X, U_V, U_R, U_I, U_X1, U_X2, U_G = 0, 1, (2, 4), (3, 5), 6, 7, 8
        tiles = [("x", 0, 0, U_X), ("v", 1024, 1, U_V), ("x1", 1536, 2, U_X1), ("x2", 2048, 0, U_X2), ("g", 512, 3, U_G)]
        gates = ["lru_wr_f", "lru_wi_f", "lru_wr_b", "lru_wi_b"]
        L_out = [dram["L"][w] for w in range(3)]
        FILL = (N_SLOTS - SEQ * 2) // CT

        block = ctx.enter_context(nc.Block())

        @block.sync
        def _(sp):
            rows = [("lru_conv_w", Q_CONV_W), ("lru_conv_b", Q_CONV_B), ("lru_br_f", 5), ("lru_bi_f", 6),
                    ("lru_br_b", 7), ("lru_bi_b", 8), ("lru_lambda_f", 9), ("lru_lambda_b", 10),
                    ("hy_conv_w", Q_HW), ("hy_conv_b", Q_HB), ("grp_norm_lru_g", Q_GA), ("grp_norm_hy_g", Q_GA + 1)]
            sp.wait_ge(zeroed, 1)
            for name, q in rows:
                a = dram[name]
                v = a.rearrange("o j (r p) -> (o j r) p", p=P) if len(a.shape) == 3 else a.rearrange("o (r p) -> (o r) p", p=P)
                sp.dma_start(prow[q * CT:q * CT + v.shape[0], :], v).then_inc(par_in, 16)

            def load_w(k, c):
                _, col, slot, _ = tiles[k]
                sp.dma_start(W[:, slot, :, :], w_v[:, :, ds(c * P + col, P)]).then_inc(w_in[k], 16)

            def load_gates(c):
                for g, name in enumerate(gates):
                    for h in range(2):
                        src = dram[name].rearrange("o h i j -> (o h) i j")[ds(c * 2 + h, 1), :, :]
                        sp.dma_start(WG[R * h:R * h + R, g, R * h:R * h + R], src.rearrange("a i j -> (a i) j")).then_inc(wg_in, 16)

            def mm_of(c, use):
                sp.wait_ge(mm_done, c * (4 * USES) + 4 * (use + 1))
                sp.sem_inc(sp_passed, 1)

            def store_tiles(c, which):
                sp.wait_ge(tr_evac, c * 12 + 4 * (which + 1) + 4)
                sp.sem_inc(sp_passed, 1)
                sp.dma_start(L_out[which][:, :, ds(c * P, P)], tst[:, :, :]).then_inc(tst_out, 16)

            for k in (0, 1, 2, 4):
                load_w(k, 0)
            load_gates(0)

            def iteration(c, more):
                mm_of(c, U_X)
                load_w(3, c)
                if more:
                    mm_of(c, U_V)
                    load_w(1, c + 1)
                    mm_of(c, U_I[1])
                    load_gates(c + 1)
                    mm_of(c, U_X1)
                    load_w(2, c + 1)
                store_tiles(c, 0)
                if more:
                    mm_of(c, U_X2)
                    load_w(0, c + 1)
                store_tiles(c, 1)
                if more:
                    mm_of(c, U_G)
                    load_w(4, c + 1)
                store_tiles(c, 2)
                sp.wait_ge(y_ready, c + 1)
                sp.dma_start(dram["YT"][:, :, ds(c, 1), :].rearrange("t p c n -> p t (c n)"),
                             T[1].rearrange("p (t n) -> p t n", n=P)).then_inc(y_out, 16)

            def fill(c):
                rows = dram["YB"][ds(c * FILL + SEQ * 2, FILL), :]
                sp.dma_start(rows.rearrange("(p b) (a n) -> p (b a) n", p=P, n=256),
                             zero[:, :].unsqueeze(1).broadcast_to([P, FILL // P * 4, 256])).then_inc(filled, 16)

            with sp.Fori(0, CT - 1) as c:
                iteration(c, True)
                fill(c)
            iteration(CT - 1, False)
            fill(CT - 1)
            sp.wait_ge(tst_out, 16 * 3 * CT)
            sp.wait_ge(y_out, 16 * CT)
            sp.wait_ge(filled, 16 * CT)

        @block.gpsimd
        def _(pool):
            pool.memset(prow[:, :], 0.0)
            pool.memset(zero[:, :], 0.0)
            pool.memset(WG[:, :, :], 0.0).then_inc(zeroed, 1)

        @block.tensor
        def _(pe):
            pe.wait_ge(par_in, 16 * 12)
            pe.transpose(tp[0][:, 0:P], prow[:, :], ident[:, :]).then_inc(pt_t, 1)
            pe.wait_ge(pt_ready, 1)

            def fill(c, use, lhs, rhs, n_k, need=None):
                for n in range(NCHUNK):
                    pe.wait_ge(evac, c * (4 * USES) + 4 * use + n + 1)
                    for k in range(n_k):
                        last = pe.matmul(pj[n][:, :], lhs(k), rhs(k, n), start=(k == 0), stop=(k == n_k - 1))
                    last.then_inc(mm_done, 1)

            def project(c, k):
                _, _, slot, use = tiles[k]
                pe.wait_ge(w_in[k], c * 16 + 16)
                fill(c, use, lambda j: W[:, slot, j, :], lambda j, n: hT[:, j, n * 512:(n + 1) * 512], KC)

            def transposes(c, which, slot):
                pe.wait_ge(hc_ready, c * 3 + which + 1)
                v = hc[:, slot, :].rearrange("p (q l) -> p l q", l=NT)
                for b in range(4):
                    pe.wait_ge(tr_evac, c * 12 + 4 * which + b + 1)
                    for q in range(4):
                        last = pe.transpose(tp[b][:, q * P:(q + 1) * P], v[:, 4 * b + q], ident[:, :])
                    last.then_inc(tr_done, 1)

            with pe.Fori(0, CT) as c:
                project(c, 0)
                project(c, 1)
                pe.wait_ge(xc_ready, c + 1)
                pe.wait_ge(wg_in, c * (16 * 8) + 16 * 8)
                for g in range(4):
                    fill(c, 2 + g, lambda j, g=g: WG[:, g, :], lambda j, n: xc[:, n * 512:(n + 1) * 512], 1)
                project(c, 2)
                transposes(c, 0, 0)
                project(c, 3)
                transposes(c, 1, 1)
                project(c, 4)
                transposes(c, 2, 0)

        @block.scalar
        def _(act):
            act.wait_ge(pt_ready, 1)
            act.activation(sp8[:, 0, :], sp8[:, 0, :], ACT.Exp, scale=-1.0).then_inc(lam_exp, 1)
            act.sem_inc(evac, 4)
            act.sem_inc(tr_evac, 4)
            act.wait_ge(lam_ready, 1)

            def evacuate(c, use, out, func=ACT.Copy, bias=None):
                for n in range(NCHUNK):
                    act.wait_ge(mm_done, c * (4 * USES) + 4 * use + n + 1)
                    if bias is None:
                        ins = act.activation(out(n), pj[n][:, :], func)
                    else:
                        ins = act.activation(out(n), pj[n][:, :], func, bias=bias)
                    ins.then_inc(evac, 1)

            def evacuate_transposes(c, which):
                act.wait_ge(tst_out, c * 48 + 16 * which)
                for b in range(4):
                    act.wait_ge(tr_done, c * 12 + 4 * which + b + 1)
                    act.activation(tst[:, 4 * b:4 * b + 4, :], tp[b].rearrange("p (t n) -> p t n", n=P), ACT.Copy).then_inc(tr_evac, 1)

            with act.Fori(0, CT) as c:
                act.wait_ge(xc_ready, c)
                evacuate(c, U_X, lambda n: xraw[:, 2 + 512 * n:2 + 512 * (n + 1)])
                act.wait_ge(hc_ready, c * 3)
                evacuate(c, U_V, lambda n: hraw[:, 0, 1 + 512 * n:1 + 512 * (n + 1)])
                act.wait_ge(par_ready, c + 1)
                act.wait_ge(y_ready, c)
                act.wait_ge(y_out, c * 16)
                for d in range(2):
                    evacuate(c, U_R[d], lambda n, d=d: T[d][:, 512 * n:512 * (n + 1)], ACT.Sigmoid, par[:, Q_BR[d]:Q_BR[d] + 1])
                    evacuate(c, U_I[d], lambda n, d=d: I[d][:, 512 * n:512 * (n + 1)], ACT.Sigmoid, par[:, Q_BI[d]:Q_BI[d] + 1])
                for d in range(2):
                    act.wait_ge(evac, c * (4 * USES) + 4 * (U_R[d] + 1) + 4)
                    act.activation(T[d][:, :], T[d][:, :], ACT.Tanh, scale=par[:, Q_LAM[d]:Q_LAM[d] + 1]).then_inc(tanh_ready, 1)
                for d in range(2):
                    act.wait_ge(q1_ready, c * 2 + d + 1)
                    act.activation(T[d][:, :], T[d][:, :], ACT.Sqrt).then_inc(sqrt_ready, 1)
                evacuate(c, U_X1, lambda n: hraw[:, 1, 1 + 512 * n:1 + 512 * (n + 1)])
                evacuate_transposes(c, 0)
                act.wait_ge(hc_ready, c * 3 + 1)
                evacuate(c, U_X2, lambda n: hraw[:, 0, 1 + 512 * n:1 + 512 * (n + 1)])
                evacuate_transposes(c, 1)
                act.wait_ge(q1_ready, c * 2 + 2)
                act.wait_ge(if_free, c + 1)
                evacuate(c, U_G, lambda n: G[:, 512 * n:512 * (n + 1)], ACT.Gelu_apprx_tanh)
                evacuate_transposes(c, 2)

        @block.vector
        def _(dve):
            step = Steps(dve, steps)
            dve.memset(xraw[:, :], 0.0)
            dve.memset(hraw[:, :, :], 0.0)
            dve.wait_ge(pt_t, 1)
            step(dve.tensor_copy(PT[:, :, :].rearrange("p q c -> p (q c)"), tp[0][:, 0:N_Q * CT]))
            lam = PT[:, Q_LAM[0]:Q_LAM[1] + 1, :].rearrange("p q c -> p (q c)")
            step(dve.tensor_scalar(sp8[:, 1, :], lam, -1.0, 0.0, ALU.mult, ALU.max))
            step(dve.tensor_scalar(sp8[:, 2, :], lam, 0.0, None, ALU.max))
            dve.tensor_tensor(sp8[:, 0, :], sp8[:, 1, :], sp8[:, 2, :], ALU.add).then_inc(pt_ready, 1)
            dve.wait_ge(lam_exp, 1)
            step(dve.tensor_scalar(sp8[:, 2, :], sp8[:, 0, :], 2.0, None, ALU.add))
            step(dve.reciprocal(sp8[:, 3, :], sp8[:, 2, :]))
            step(dve.tensor_tensor(sp8[:, 2, :], sp8[:, 0, :], sp8[:, 3, :], ALU.mult))
            step(dve.tensor_tensor(sp8[:, 3, :], sp8[:, 2, :], sp8[:, 2, :], ALU.mult))
            step(dve.memset(sp8[:, 4, :], 1.0 / 17))
            for odd in range(15, 0, -2):
                step(dve.tensor_tensor(sp8[:, 4, :], sp8[:, 4, :], sp8[:, 3, :], ALU.mult))
                step(dve.tensor_scalar(sp8[:, 4, :], sp8[:, 4, :], 1.0 / odd, None, ALU.add))
            step(dve.tensor_tensor(sp8[:, 4, :], sp8[:, 4, :], sp8[:, 2, :], ALU.mult))
            step(dve.scalar_tensor_tensor(out=sp8[:, 4, :], in0=sp8[:, 4, :], scalar=2.0, in1=sp8[:, 1, :], op0=ALU.mult, op1=ALU.add))
            step(dve.tensor_scalar(lam, sp8[:, 4, :], 4.0, None, ALU.mult))
            dve.tensor_copy(dram["gAB"][:, :, :], PT[:, Q_GA:Q_GA + 2, :]).then_inc(lam_ready, 1)
            PER_C = 22

            def conv(step, out, raw, taps, q_w, stride, q_b, done):
                step(dve.tensor_scalar(out, raw[:, 0:SEQ], par[:, q_w:q_w + 1], par[:, q_b:q_b + 1], ALU.mult, ALU.add))
                for j in range(1, taps):
                    q = q_w + j * stride
                    ins = dve.scalar_tensor_tensor(out=out, in0=raw[:, j:j + SEQ], scalar=par[:, q:q + 1], in1=out,
                                                   op0=ALU.mult, op1=ALU.add)
                    if j < taps - 1:
                        step(ins)
                ins.then_inc(done, 1)

            with dve.Fori(0, CT) as c:
                step = Steps(dve, steps, c * PER_C + 27)
                dve.wait_ge(hc_ready, c * 3)
                dve.tensor_copy(par[:, :], PT[:, :, ds(c, 1)].rearrange("p q c -> p (q c)")).then_inc(par_ready, 1)
                dve.wait_ge(par_ready, c + 1)

                def hyena_conv(which, slot, use):
                    dve.wait_ge(evac, c * (4 * USES) + 4 * (use + 1) + 4)
                    dve.wait_ge(tr_done, c * 12 + (4 if which == 2 else 0))
                    conv(step, hc[:, slot, :], hraw[:, slot, :], 3, Q_HW + which, 3, Q_HB + which, hc_ready)

                def lru(d):
                    step(dve.reciprocal(Q[d][:, :], Q[d][:, :]))
                    step(dve.tensor_tensor(I[d][:, :], I[d][:, :], xc[:, :], ALU.mult))
                    step(dve.tensor_tensor(I[d][:, :], I[d][:, :], Q[d][:, :], ALU.mult))
                    dve.wait_ge(sqrt_ready, c * 2 + d + 1)
                    step(dve.scalar_tensor_tensor(out=I[d][:, :], in0=T[d][:, :], scalar=2.0, in1=I[d][:, :], op0=ALU.mult, op1=ALU.mult))
                    step(dve.tensor_scalar(Q[d][:, :], Q[d][:, :], 2.0, -1.0, ALU.mult, ALU.add))
                    o = slice(None, None, -1) if d else slice(None)
                    step(dve.tensor_tensor_scan(T[d][:, o], Q[d][:, o], I[d][:, o], 0.0, ALU.mult, ALU.add))

                dve.wait_ge(evac, c * (4 * USES) + 8)
                conv(step, xc[:, :], xraw, 4, Q_CONV_W, 1, Q_CONV_B, xc_ready)
                hyena_conv(0, 0, U_V)
                for d in range(2):
                    dve.wait_ge(tanh_ready, c * 2 + d + 1)
                    dve.tensor_scalar(Q[d][:, :], T[d][:, :], 1.0, None, ALU.add).then_inc(q1_ready, 1)
                dve.wait_ge(xc_ready, c + 1)
                dve.wait_ge(q1_ready, c * 2 + 2)
                lru(0)
                dve.sem_inc(if_free, 1)
                hyena_conv(1, 1, U_X1)
                lru(1)
                step(dve.tensor_tensor(T[0][:, :], T[0][:, :], T[1][:, :], ALU.add))
                hyena_conv(2, 0, U_X2)
                dve.wait_ge(evac, c * (4 * USES) + 4 * (U_G + 1) + 4)
                dve.tensor_tensor(T[1].rearrange("p (l q) -> p q l", q=P), T[0].rearrange("p (q l) -> p q l", l=NT),
                                  G.rearrange("p (q l) -> p q l", l=NT), ALU.mult).then_inc(y_ready, 1)
                n_steps = step.n
            assert n_steps == PER_C, n_steps

def filters(nc, dram, invn):
    L = R // 2
    MAGIC = 1.5 * 2.0 ** 23
    C1 = 6.28125
    C2 = float(np.float32(np.round((2 * math.pi - C1) * 2 ** 21) / 2 ** 21))
    C3 = 2 * math.pi - C1 - C2
    with ExitStack() as ctx:
        sb = lambda name, shape, dt=F32: ctx.enter_context(nc.sbuf_tensor(name, shape, dt))
        sem = phase_semaphores(nc, ctx)
        feats = sb("feats", [33, SEQ])
        w1 = sb("w1", [33, P])
        w2 = sb("w2", [P, P])
        w3 = sb("w3", [P, 2, 512])
        vec = sb("vec", [P, 4])
        fa = sb("fa", [P, P])
        ones = sb("ones", [P, P])
        arg, rnd, z1, zz = sb("arg", [P, SEQ]), sb("rnd", [P, SEQ]), sb("zf1", [P, SEQ]), sb("zz", [P, SEQ])
        zb = sb("zb", [P, 4, P])
        mask = sb("mask", [P, 2, R])
        dec = sb("dec", [P, 4, 512])
        kt = sb("kt", [P, 4, 2, 512])
        acc = sb("acc", [P, 2, 512])
        ka = sb("ka", [P, 2, 2, 512])
        kst = sb("kst", [P, 2, 2, 2, 512])
        pk = [[ctx.enter_context(nc.psum_tensor(f"pk{s}{o}", [P, 512], F32)) for o in range(2)] for s in range(2)]
        pa = [[ctx.enter_context(nc.psum_tensor(f"pa{s}{o}", [P, 512], F32)) for o in range(2)] for s in range(2)]
        flat = [pk[0][0], pk[0][1], pk[1][0], pk[1][1]]
        par_in, w2_zero, mlp_mm, arg_ready, mlp_sin = sem("f_in"), sem("w2_zero"), sem("mlp_mm"), sem("arg_ready"), sem("mlp_sin")
        steps, dec_in, zb_ready, kgen, k_ready = sem("f_steps"), [sem(f"dec_in{s}") for s in range(4)], sem("zb_ready"), sem("kgen"), sem("k_ready")
        fa_done, kst_ready, kst_out, norm_mm, inv_ready = sem("fa_done"), sem("kst_ready"), [sem(f"kst_out{i}") for i in range(2)], sem("norm_mm"), sem("inv_ready")
        summed, mask_ready, abs_ready = sem("summed"), sem("mask_ready"), sem("abs_ready")
        N_PAR = 16
        block = ctx.enter_context(nc.Block())

        @block.sync
        def _(sp):
            load = lambda dst, src: sp.dma_start(dst, src).then_inc(par_in, 16)
            load(feats[:, :], dram["feats"])
            for h in range(2):
                load(w1[:, R * h:R * h + R], dram["hy_filt_w1"].rearrange("o i j -> (o i) j"))
                load(w3[R * h:R * h + R, :, :], dram["hy_filt_w3"].rearrange("o i (d r c) -> (o i) d r c", d=2, r=2)[:, h])
                for q, name in enumerate(("hy_filt_b1", "hy_filt_freq1", "hy_filt_b2", "hy_filt_freq2")):
                    load(vec[R * h:R * h + R, q:q + 1], dram[name].rearrange("o n -> n o"))
            load(fa[:, :], dram["fa_filter"])
            sp.wait_ge(w2_zero, 1)
            for h in range(2):
                load(w2[0:R, R * h:R * h + R], dram["hy_filt_w2"].rearrange("o i j -> (o i) j"))
            with sp.Fori(0, L // 4) as it:
                for s in range(4):
                    sp.wait_ge(k_ready, it * 8)
                    sp.dma_start(dec[:, s, :], dram["decay"][:, ds(it * 4 + s, 1), :].rearrange("p a c -> p (a c)")).then_inc(dec_in[s], 16)

        @block.gpsimd
        def _(pool):
            pool.memset(w2[:, :], 0.0).then_inc(w2_zero, 1)
            pool.memset(ones[:, :], 1.0)
            pool.wait_ge(mlp_sin, 3)
            pool.wait_ge(mask_ready, 1)
            pool.memset(acc[:, :, :], 0.0).then_inc(summed, 1)
            view = zz.rearrange("p (q l) -> p l q", l=L)
            with pool.Fori(0, L // 4) as it:
                for s in range(4):
                    pool.wait_ge(kgen, it * 8)
                    pool.tensor_tensor(zb[:, s, :].rearrange("p (h q) -> p h q", h=2),
                                       view[:, ds(it * 4 + s, 1), :].broadcast_to([P, 2, R]), mask[:, :, :], ALU.mult).then_inc(zb_ready, 1)
                for s in range(4):
                    for o in range(2):
                        pool.wait_ge(abs_ready, it * 8 + 2 * s + o + 1)
                        pool.wait_ge(summed, it * 8 + max(2 * s + o, 1))
                        pool.tensor_tensor(acc[:, o, :], acc[:, o, :], ka[:, s % 2, o, :], ALU.add).then_inc(summed, 1)

        @block.tensor
        def _(pe):
            pe.wait_ge(par_in, 16 * N_PAR)
            for n in range(4):
                last = pe.matmul(flat[n][:, :], w1[:, :], feats[:, n * 512:(n + 1) * 512], start=True, stop=True)
            last.then_inc(mlp_mm, 1)
            pe.wait_ge(mlp_sin, 1)
            for n in range(4):
                last = pe.matmul(flat[n][:, :], w2[:, :], z1[:, n * 512:(n + 1) * 512], start=True, stop=True)
            last.then_inc(mlp_mm, 1)
            pe.wait_ge(arg_ready, 2)
            with pe.Fori(0, L // 4) as it:
                for pair in range(2):
                    for s in (2 * pair, 2 * pair + 1):
                        pe.wait_ge(zb_ready, it * 4 + s + 1)
                        pe.wait_ge(k_ready, it * 8 + 4 * pair)
                        for o in range(2):
                            pe.matmul(pk[s % 2][o][:, :], zb[:, s, :], w3[:, o, :], start=True, stop=True).then_inc(kgen, 1)
                    for s in (2 * pair, 2 * pair + 1):
                        for o in range(2):
                            pe.wait_ge(k_ready, it * 8 + 2 * s + o + 1)
                            pe.wait_ge(kst_ready, it * 8 + 4 * pair)
                            pe.matmul(pa[s % 2][o][:, :], fa[:, :], kt[:, s, o, :], start=True, stop=True).then_inc(fa_done, 1)
            pe.wait_ge(summed, 1 + 8 * (L // 4))
            for o in range(2):
                last = pe.matmul(pk[0][o][:, :], ones[:, :], acc[:, o, :], start=True, stop=True)
            last.then_inc(norm_mm, 1)

        @block.scalar
        def _(act):
            act.wait_ge(arg_ready, 1)
            act.activation(z1[:, :], arg[:, :], ACT.Sin).then_inc(mlp_sin, 1)
            act.wait_ge(arg_ready, 2)
            act.activation(zz[0:R, :], arg[0:R, :], ACT.Sin).then_inc(mlp_sin, 1)
            act.activation(zz[R:P, 1:SEQ][:, ::-1], arg[R:P, 1:SEQ], ACT.Sin).then_inc(mlp_sin, 1)
            with act.Fori(0, L // 4) as it:
                for pair in range(2):
                    act.wait_ge(kst_out[pair], it * (16 * 4))
                    for s in (2 * pair, 2 * pair + 1):
                        for o in range(2):
                            act.wait_ge(fa_done, it * 8 + 2 * s + o + 1)
                            act.activation(kst[:, pair, o, s % 2, :], pa[s % 2][o][:, :], ACT.Copy).then_inc(kst_ready, 1)
                    act.wait_ge(kst_ready, it * 8 + 4 * pair + 4)
                    for o in range(2):
                        for g in range(2):
                            act.dma_start(dram["KA"][o][:, ds(it * 4 + 2 * pair + L * g, 2), :],
                                          kst[R * g:R * g + R, pair, o, :, :]).then_inc(kst_out[pair], 16)
            for pair in range(2):
                act.wait_ge(kst_out[pair], 16 * 4 * (L // 4))

        @block.vector
        def _(dve):
            step = Steps(dve, steps)

            def reduce_range(b, f):
                for n in range(4):
                    last = dve.tensor_scalar(arg[:, n * 512:(n + 1) * 512], flat[n][:, :], vec[:, b:b + 1], vec[:, f:f + 1], ALU.add, ALU.mult)
                step(last)
                step(dve.tensor_scalar(rnd[:, :], arg[:, :], 1.0 / (2 * math.pi), MAGIC, ALU.mult, ALU.add))
                step(dve.tensor_scalar(rnd[:, :], rnd[:, :], MAGIC, None, ALU.subtract))
                for part in (C1, C2, C3):
                    step(dve.scalar_tensor_tensor(out=arg[:, :], in0=rnd[:, :], scalar=-part, in1=arg[:, :], op0=ALU.mult, op1=ALU.add))
                dve.tensor_scalar(arg[:, :], arg[:, :], 3.1415925, -3.1415925, ALU.min, ALU.max).then_inc(arg_ready, 1)

            dve.memset(zz[R:P, 0:1], 0.0)
            step(dve.memset(mask[:, :, :], 0.0))
            for h in range(2):
                last = dve.memset(mask[R * h:R * h + R, h, :], 1.0)
            last.then_inc(mask_ready, 1)
            dve.wait_ge(par_in, 16 * N_PAR)
            dve.wait_ge(mlp_mm, 1)
            reduce_range(0, 1)
            dve.wait_ge(mlp_mm, 2)
            dve.wait_ge(mlp_sin, 1)
            reduce_range(2, 3)
            with dve.Fori(0, L // 4) as it:
                for s in range(4):
                    dve.wait_ge(dec_in[s], it * 16 + 16)
                    for o in range(2):
                        dve.wait_ge(kgen, it * 8 + 2 * s + o + 1)
                        dve.wait_ge(fa_done, it * 8)
                        dve.tensor_tensor(kt[:, s, o, :], pk[s % 2][o][:, :], dec[:, s, :], ALU.mult).then_inc(k_ready, 1)
                        dve.wait_ge(k_ready, it * 8 + 2 * s + o + 1)
                        dve.wait_ge(summed, it * 8 + (2 * s + o - 2 if s > 1 else 0))
                        dve.scalar_tensor_tensor(out=ka[:, s % 2, o, :], in0=kt[:, s, o, :], scalar=-1.0, in1=kt[:, s, o, :],
                                                 op0=ALU.mult, op1=ALU.max).then_inc(abs_ready, 1)
            dve.wait_ge(norm_mm, 1)
            for o in range(2):
                step(dve.tensor_scalar(acc[:, o, :], pk[0][o][:, :], EPS, None, ALU.add))
            dve.reciprocal(invn[:, :, :], acc[:, :, :]).then_inc(inv_ready, 1)


def conv_forward(nc, dram, o, cur, skip):
    with ExitStack() as ctx:
        sb = lambda name, shape, dt=F32: ctx.enter_context(nc.sbuf_tensor(f"{name}_{o}", shape, dt))
        sem = phase_semaphores(nc, ctx, f"_a{o}")
        fa = sb("faz", [P, 2, P])
        st = sb("st", [P, 2, 2, 2, 512])
        pa = [[ctx.enter_context(nc.psum_tensor(f"za_{o}_{s}{h}", [P, 512], F32)) for h in range(2)] for s in range(4)]
        cur_in, fa_in, skip_in, mm, evac = [sem(f"cur_in{g}") for g in range(4)], sem("fa_in"), sem("skip_in"), sem("mm"), sem("evac")
        stored = [sem(f"stored{i}") for i in range(2)]
        block = ctx.enter_context(nc.Block())

        @block.sync
        def _(sp):
            sp.dma_start(fa[:, :, :], dram["fa_signal"]).then_inc(fa_in, 16)
            if o == 0:
                for g in range(4):
                    sp.dma_start(cur[:, 4 * g:4 * g + 4, :], dram["L"][0][:, 4 * g:4 * g + 4, :]).then_inc(cur_in[g], 16)
            sp.dma_start(skip[:, :], dram["hy_skip"].rearrange("a o c -> (a o) c")[o].partition_broadcast(P)).then_inc(skip_in, 16)

        @block.tensor
        def _(pe):
            pe.wait_ge(fa_in, 16)
            if o == 0:
                for g in range(4):
                    pe.wait_ge(cur_in[g], 16)
            with pe.Fori(0, NT // 4) as it:
                for s in range(4):
                    pe.wait_ge(evac, it * 8 + 0)
                    for h in range(2):
                        pe.matmul(pa[s][h][:, :], fa[:, h, :], cur[:, ds(it * 4 + s, 1), :].rearrange("p a c -> p (a c)"),
                                  start=True, stop=True).then_inc(mm, 1)

        @block.scalar
        def _(act):
            with act.Fori(0, NT // 4) as it:
                for pair in range(2):
                    act.wait_ge(stored[pair], it * (16 * 4))
                    for s in (2 * pair, 2 * pair + 1):
                        for h in range(2):
                            act.wait_ge(mm, it * 8 + 2 * s + h + 1)
                            act.activation(st[:, pair, h, s % 2, :], pa[s][h][:, :], ACT.Copy).then_inc(evac, 1)
                    act.wait_ge(evac, it * 8 + 4 * pair + 4)
                    for h in range(2):
                        for g in range(2):
                            act.dma_start(dram["SA"][:, ds(it * 4 + 2 * pair + 32 * h + 16 * g, 2), :],
                                          st[R * g:R * g + R, pair, h, :, :]).then_inc(stored[pair], 16)
            for pair in range(2):
                act.wait_ge(stored[pair], 16 * 4 * (NT // 4))

        @block.gpsimd
        def _(pool):
            pool.wait_ge(skip_in, 16)
            with pool.Fori(0, NT) as t:
                pool.wait_ge(mm, t * 2 + 2)
                tile = cur[:, ds(t, 1), :].rearrange("p a c -> p (a c)")
                pool.tensor_tensor(tile, tile, skip[:, :], ALU.mult)


def conv_blocks(nc, dram, o):
    with ExitStack() as ctx:
        sb = lambda name, shape, dt=F32: ctx.enter_context(nc.sbuf_tensor(f"{name}_{o}", shape, dt))
        sem = phase_semaphores(nc, ctx, f"_b{o}")
        mats = sb("mats", [P, 4, 5, P])
        zin, kin, qo = sb("zin", [P, 4, 512]), sb("kin", [P, 4, 512]), sb("qo", [P, 4, 512])
        zs, u, v = sb("zs", [P, 2, 512]), sb("u", [P, 2, 512]), sb("v", [P, 2, 512])
        bank = lambda name: [ctx.enter_context(nc.psum_tensor(f"{name}_{o}_{i}", [P, 512], F32)) for i in range(2)]
        pz, pr, pi, pq = bank("pz"), bank("pr"), bank("pi"), bank("pq")
        landed = [sem(f"landed{s}") for s in range(4)]
        fwd, zs_ready, uv_ready, inv, q_evac = sem("fwd"), sem("zs_ready"), sem("uv_ready"), sem("inv"), sem("q_evac")
        stored = [sem(f"stored{s}") for s in range(4)]
        by_block = lambda a: a.rearrange("(r j) n c -> j r n c", r=2)
        SA, SI, KA = by_block(dram["SA"]), by_block(dram["SI"]), by_block(dram["KA"][o])
        block = ctx.enter_context(nc.Block())

        @block.sync
        def _(sp):
            with sp.Fori(0, HALF // 4) as it:
                for s in range(4):
                    j = it * 4 + s
                    sp.wait_ge(inv, it * 4)
                    sp.dma_start(mats[:, s, :, :], dram["mats"][ds(j, 1)].rearrange("a p m n -> (a p) m n")).then_inc(landed[s], 16)
                    for r in range(2):
                        for dst, src in ((zin, SA), (kin, KA)):
                            sp.dma_start(dst[R * r:R * r + R, s, :], src[ds(j, 1), r].rearrange("a n c -> (a n) c")).then_inc(landed[s], 16)

        @block.tensor
        def _(pe):
            with pe.Fori(0, HALF // 4) as it:
                def forward(s):
                    pe.wait_ge(landed[s], it * 80 + 80)
                    pe.wait_ge(zs_ready, it * 4 + max(s - 1, 0))
                    pe.wait_ge(uv_ready, it * 8 + 2 * max(s - 1, 0))
                    for bank_, m, rhs in ((pz, 0, zin), (pr, 1, kin), (pi, 2, kin)):
                        pe.matmul(bank_[s % 2][:, :], mats[:, s, m, :], rhs[:, s, :], start=True, stop=True).then_inc(fwd, 1)

                def inverse(s):
                    pe.wait_ge(uv_ready, it * 8 + 2 * s + 2)
                    pe.wait_ge(q_evac, it * 4 + max(s - 1, 0))
                    pe.matmul(pq[s % 2][:, :], mats[:, s, 3, :], u[:, s % 2, :], start=True, stop=False)
                    pe.matmul(pq[s % 2][:, :], mats[:, s, 4, :], v[:, s % 2, :], start=False, stop=True).then_inc(inv, 1)

                forward(0)
                for s in range(1, 4):
                    forward(s)
                    inverse(s - 1)
                inverse(3)

        @block.scalar
        def _(act):
            with act.Fori(0, HALF // 4) as it:
                def signal(s):
                    act.wait_ge(fwd, it * 12 + 3 * s + 1)
                    act.wait_ge(uv_ready, it * 8 + 2 * max(s - 1, 0))
                    act.activation(zs[:, s % 2, :], pz[s % 2][:, :], ACT.Copy).then_inc(zs_ready, 1)

                def result(s):
                    act.wait_ge(stored[s], it * 32)
                    act.wait_ge(inv, it * 4 + s + 1)
                    act.activation(qo[:, s, :], pq[s % 2][:, :], ACT.Copy).then_inc(q_evac, 1)
                    act.wait_ge(q_evac, it * 4 + s + 1)
                    for r in range(2):
                        act.dma_start(SI[ds(it * 4 + s, 1), r].rearrange("a n c -> (a n) c"), qo[R * r:R * r + R, s, :]).then_inc(stored[s], 16)

                signal(0)
                for s in range(1, 4):
                    signal(s)
                    result(s - 1)
                result(3)
            for s in range(4):
                act.wait_ge(stored[s], 32 * (HALF // 4))

        @block.vector
        def _(dve):
            with dve.Fori(0, HALF // 4) as it:
                for s in range(4):
                    dve.wait_ge(zs_ready, it * 4 + s + 1)
                    dve.wait_ge(inv, it * 4 + max(s - 1, 0))
                    for n, (dst, src) in enumerate(((u, pr), (v, pi))):
                        dve.wait_ge(fwd, it * 12 + 3 * s + 2 + n)
                        dve.tensor_tensor(dst[:, s % 2, :], src[s % 2][:, :], zs[:, s % 2, :], ALU.mult).then_inc(uv_ready, 1)


def conv_inverse(nc, dram, o, cur, invn, ident):
    with ExitStack() as ctx:
        sb = lambda name, shape, dt=F32: ctx.enter_context(nc.sbuf_tensor(f"{name}_{o}", shape, dt))
        sem = phase_semaphores(nc, ctx, f"_c{o}")
        ia = sb("ia", [P, 2, P])
        si = sb("si", [P, 4, 2, 512])
        gate = sb("gate", [P, 4, 512])
        y = sb("y", [P, 4, 512])
        junk = sb("junkz", [P, 512])
        ssq, rstd = sb("ssqz", [P, NT]), sb("rstdz", [P, NT])
        zn = sb("zn", [P, 2, 512])
        zt = sb("zt", [P, 2, 512])
        pq = [ctx.enter_context(nc.psum_tensor(f"py_{o}_{s}", [P, 512], F32)) for s in range(4)]
        tp = [ctx.enter_context(nc.psum_tensor(f"pt_{o}_{s}", [P, 512], F32)) for s in range(2)]
        ia_in, landed, mm, scaled, added, gated = sem("ia_in"), [sem(f"landed{s}") for s in range(4)], sem("mm"), sem("scaled"), sem("added"), sem("gated")
        squared, ms, rs, zn_ready, tr, zt_ready = sem("squared"), sem("ms"), sem("rs"), sem("zn_ready"), sem("tr"), sem("zt_ready")
        stored = [sem(f"stored{s}") for s in range(2)]
        tile = lambda t: cur[:, ds(t, 1), :].rearrange("p a c -> p (a c)")
        SI = dram["SI"].rearrange("k (h g l) c -> g l k h c", h=2, g=2)
        block = ctx.enter_context(nc.Block())

        @block.sync
        def _(sp):
            sp.dma_start(ia[:, :, :], dram["inv_a"]).then_inc(ia_in, 16)
            with sp.Fori(0, NT // 4) as it:
                for s in range(4):
                    sp.wait_ge(gated, it * 4)
                    for g in range(2):
                        sp.dma_start(si[R * g:R * g + R, s, :, :], SI[g, ds(it * 4 + s, 1)].rearrange("a k h c -> (a k) h c")).then_inc(landed[s], 16)
                    sp.dma_start(gate[:, s, :], dram["L"][1 + o][:, ds(it * 4 + s, 1), :].rearrange("p a c -> p (a c)")).then_inc(landed[s], 16)

        @block.tensor
        def _(pe):
            pe.wait_ge(ia_in, 16)
            with pe.Fori(0, NT // 4) as it:
                for s in range(4):
                    pe.wait_ge(landed[s], it * 48 + 48)
                    pe.wait_ge(scaled, it * 4)
                    pe.matmul(pq[s][:, :], ia[:, 0, :], si[:, s, 0, :], start=True, stop=False)
                    pe.matmul(pq[s][:, :], ia[:, 1, :], si[:, s, 1, :], start=False, stop=True).then_inc(mm, 1)
            if o == 1:
                with pe.Fori(0, NT // 2) as it:
                    for s in range(2):
                        t = it * 2 + s
                        pe.wait_ge(zn_ready, t + 1)
                        pe.wait_ge(zt_ready, it * 2)
                        for q in range(4):
                            last = pe.transpose(tp[s][:, q * P:(q + 1) * P], zn[:, s, q * P:(q + 1) * P], ident[:, :])
                        last.then_inc(tr, 1)

        @block.gpsimd
        def _(pool):
            with pool.Fori(0, NT // 4) as it:
                for s in range(4):
                    pool.wait_ge(scaled, it * 4 + s + 1)
                    pool.tensor_tensor(y[:, s, :], y[:, s, :], tile(it * 4 + s), ALU.add).then_inc(added, 1)

        @block.vector
        def _(dve):
            with dve.Fori(0, NT // 4) as it:
                for s in range(4):
                    dve.wait_ge(mm, it * 4 + s + 1)
                    dve.wait_ge(gated, it * 4)
                    dve.tensor_tensor(y[:, s, :], pq[s][:, :], invn[:, o, :], ALU.mult).then_inc(scaled, 1)
                for s in range(4):
                    dve.wait_ge(added, it * 4 + s + 1)
                    dve.wait_ge(landed[s], it * 48 + 48)
                    dve.tensor_tensor(tile(it * 4 + s), y[:, s, :], gate[:, s, :], ALU.mult).then_inc(gated, 1)
            if o == 1:
                dve.wait_ge(squared, NT)
                dve.tensor_scalar(ssq[:, :], ssq[:, :], 1.0 / CH, EPS, ALU.mult, ALU.add).then_inc(ms, 1)
                dve.wait_ge(ms, 1)
                dve.reciprocal(rstd[:, :], ssq[:, :]).then_inc(ms, 1)
                dve.wait_ge(rs, 1)
                with dve.Fori(0, NT // 2) as it:
                    for s in range(2):
                        t = it * 2 + s
                        dve.wait_ge(tr, it * 2)
                        dve.tensor_scalar(zn[:, s, :], tile(t), rstd[:, ds(t, 1)], None, ALU.mult).then_inc(zn_ready, 1)

        if o == 1:
            @block.scalar
            def _(act):
                with act.Fori(0, NT) as t:
                    act.wait_ge(gated, t + 1)
                    act.wait_ge(squared, t)
                    act.activation(junk[:, :], tile(t), ACT.Square, accum_out=ssq[:, ds(t, 1)]).then_inc(squared, 1)
                act.wait_ge(ms, 2)
                act.activation(rstd[:, :], rstd[:, :], ACT.Sqrt).then_inc(rs, 1)
                with act.Fori(0, NT // 2) as it:
                    for s in range(2):
                        t = it * 2 + s
                        act.wait_ge(tr, t + 1)
                        act.wait_ge(stored[s], it * 16)
                        act.activation(zt[:, s, :], tp[s][:, :], ACT.Copy).then_inc(zt_ready, 1)
                        act.wait_ge(zt_ready, t + 1)
                        act.dma_start(dram["YT"][ds(t, 1), :, 4:8, :].rearrange("a p c n -> (a p) (c n)"), zt[:, s, :]).then_inc(stored[s], 16)
                for s in range(2):
                    act.wait_ge(stored[s], 16 * (NT // 2))


def transform_tables():
    n = np.arange
    th1 = 2 * np.pi * np.outer(n(R), n(HALF + 1)) / R
    F = np.zeros((R, R))
    F[:, 0:HALF + 1] = np.cos(th1)
    F[:, HALF + 1:] = -np.sin(th1[:, 1:HALF])
    fa_filter = np.zeros((R, 2, 2, R))
    for g in range(2):
        fa_filter[:, g, g] = F
    fa_signal = np.zeros((HALF, 4, 2, 2, R))
    inv_a = np.zeros((2, R, 2, HALF, 4))
    G = np.zeros((R, HALF))
    n1 = n(HALF)
    G[0], G[HALF] = 1, (-1.0) ** n1
    for j in range(1, HALF):
        G[j], G[HALF + j] = 2 * np.cos(2 * np.pi * n1 * j / R), -2 * np.sin(2 * np.pi * n1 * j / R)
    for h in range(2):
        for g2 in range(2):
            fa_signal[:, 2 * h + g2, h, g2] = F[:HALF]
            inv_a[g2, :, h, :, 2 * h + g2] = G / N
    n2 = n(R)
    B, Inv = np.zeros((HALF, 2, R, 2, R)), np.zeros((HALF, 2, R, 2, R))
    for j in range(1, HALF):
        th = 2 * np.pi * np.outer(n2, j + R * n(R)) / N
        B[j, 0, :, 0], B[j, 1, :, 0], B[j, 0, :, 1], B[j, 1, :, 1] = np.cos(th), np.sin(th), -np.sin(th), np.cos(th)
        Inv[j, 0, :, 0], Inv[j, 1, :, 0], Inv[j, 0, :, 1], Inv[j, 1, :, 1] = np.cos(th).T, -np.sin(th).T, np.sin(th).T, np.cos(th).T
    for s in range(R - 1):
        part, k = (1, HALF + R * s) if s < HALF else (0, R * (s - HALF + 1))
        th = 2 * np.pi * n2 * k / N
        B[0, part, :, 0, s], B[0, part, :, 1, s] = np.cos(th), -np.sin(th)
        Inv[0, 0, s, part], Inv[0, 1, s, part] = 2 * np.cos(th), -2 * np.sin(th)
    B[0, 0, :, 0, R - 1], B[0, 0, :, 1, R - 1] = 1, (-1.0) ** n2
    Inv[0, 0, R - 1, 0], Inv[0, 1, R - 1, 0] = 1, (-1.0) ** n2
    Kr, Ki = B.copy(), B.copy()
    Kr[:, :, :, 1], Ki[:, :, :, 0] = B[:, :, :, 0], B[:, :, :, 1]
    Kr[0, :, :, 1, R - 1], Ki[0, :, :, :, R - 1] = B[0, :, :, 1, R - 1], 0
    InvV = np.zeros_like(Inv)
    InvV[:, 0], InvV[:, 1] = Inv[:, 1], -Inv[:, 0]
    InvV[0, :, R - 1] = 0
    mats = np.stack([m.reshape(HALF, P, P) for m in (B, Kr, Ki, Inv, InvV)], 2)
    f = np.float32
    pos, t = n(SEQ, dtype=f), np.linspace(0, 1, SEQ, dtype=f)
    bands = np.linspace(1e-4, 15, 16, dtype=f)
    ang = (f(2 * math.pi / SEQ) * pos)[:, None] * bands
    feats = np.concatenate([t[:, None], np.cos(ang), np.sin(ang)], -1).T
    deltas = np.abs(np.linspace(math.log(1e-2) / 1.5, math.log(1e-2) / 0.3, CH, dtype=f))
    back = np.concatenate([np.zeros(1, f), t[1:][::-1]])
    decay = np.exp(-np.concatenate([t, back])[:, None] * deltas).reshape(P, R // 2, CH)
    out = dict(fa_filter=fa_filter.reshape(P, P), fa_signal=fa_signal.reshape(P, 2, P), inv_a=inv_a.reshape(P, 2, P),
               mats=mats, feats=feats, decay=decay, ident=np.eye(P))
    return {k: np.ascontiguousarray(v, dtype=f) for k, v in out.items()}


def output_projection(nc, dram, X2, LG, gAB, ident):
    NL = N_GROUPS + N_EXP
    with ExitStack() as ctx:
        sb = lambda name, shape, dt=F32: ctx.enter_context(nc.sbuf_tensor(name, shape, dt))
        sem = phase_semaphores(nc, ctx)
        wo = sb("wo", [P, KC, D])
        rw = sb("rw", [P, KC, P])
        rb = sb("rb", [P, NL])
        gain = sb("gain_ffn", [P, D])
        ones = sb("ones5", [P, P])
        yt = sb("yt", [P, 2, KC, P])
        xt = sb("xt", [P, 2, D])
        sq = sb("sq", [P, 2, 512])
        h = sb("h", [P, 2, D])
        hT = sb("hT5", [P, KC, P])
        junk = sb("junk5", [P, D])
        st = sb("st5", [P, 2, 8])
        bank = lambda name: ctx.enter_context(nc.psum_tensor(name, [P, 512], F32))
        pA, pB, pt = [bank("pA0"), bank("pA1")], [bank("pB0"), bank("pB1")], [bank("ph0"), bank("ph1")]
        pl, psq = bank("pl"), bank("psq")
        w_in_, rw_zero, w_ready = sem("wo_in"), sem("rw_zero"), sem("wo_ready")
        y_in, x_in = [sem(f"y_in{s}") for s in range(2)], [sem(f"x5_in{s}") for s in range(2)]
        sq_ready, sum1, sum2, ssq_mm, rA_ms, rA_ready = sem("sq_ready"), sem("sum1"), sem("sum2"), sem("ssq_mm"), sem("rA_ms"), sem("rA_ready")
        projA, projB, xa_ready, x2_ready = sem("projA"), sem("projB"), sem("xa_ready"), sem("x2_ready")
        s2_ready, ms2, rs2, h_ready, tr, hT_ready, lg_mm, lg_ready = (sem(n) for n in ("s2_ready", "ms2", "rs2", "h_ready", "tr5", "hT_ready", "lg_mm", "lg_ready"))
        h_out = [sem(f"h_out{s}") for s in range(2)]
        rA_first, ms2_first = sem("rA_first"), sem("ms2_first")
        N_W = 6

        def pipelined(eng, head, tail):
            head(0, 0)
            with eng.Fori(0, NT // 2 - 1) as it:
                head(it * 2 + 1, 1)
                tail(it * 2, 0)
                head(it * 2 + 2, 0)
                tail(it * 2 + 1, 1)
            head(NT - 1, 1)
            tail(NT - 2, 0)
            tail(NT - 1, 1)

        x_t = dram["x"].rearrange("o (p l) d -> l p (o d)", l=NT)
        block = ctx.enter_context(nc.Block())

        @block.sync
        def _(sp):
            load = lambda dst, src: sp.dma_start(dst, src).then_inc(w_in_, 16)
            load(wo[:, :, :], dram["w_out"].rearrange("o (k p) n -> p (o k) n", p=P))
            sp.wait_ge(rw_zero, 1)
            load(rw[:, :, 0:N_GROUPS], dram["router_group_w"].rearrange("o (k p) n -> p (o k) n", p=P))
            load(rw[:, :, N_GROUPS:NL], dram["router_expert_w"].rearrange("o (k p) n -> p (o k) n", p=P))
            load(rb[:, 0:N_GROUPS], dram["router_group_b"].rearrange("o d -> (o d)").partition_broadcast(P))
            load(rb[:, N_GROUPS:NL], dram["router_expert_b"].rearrange("o d -> (o d)").partition_broadcast(P))
            load(gain[:, :], dram["norm_ffn_g"].rearrange("o d -> (o d)").partition_broadcast(P))
            with sp.Fori(0, NT // 2) as it:
                for s in range(2):
                    sp.wait_ge(x2_ready, it * 4)
                    sp.dma_start(yt[:, s, :, :], dram["YT"][ds(it * 2 + s, 1)].rearrange("a p k n -> (a p) k n")).then_inc(y_in[s], 16)
                    sp.dma_start(xt[:, s, :], x_t[ds(it * 2 + s, 1)].rearrange("a p d -> (a p) d")).then_inc(x_in[s], 16)

        @block.gpsimd
        def _(pool):
            pool.memset(rw[:, :, :], 0.0).then_inc(rw_zero, 1)
            pool.memset(ones[:, :], 1.0).then_inc(rw_zero, 1)
            with pool.Fori(0, NT // 2) as it:
                for s in range(2):
                    t = it * 2 + s
                    pool.wait_ge(sq_ready, t + 1)
                    pool.tensor_tensor(sq[:, s, 0:256], sq[:, s, 0:256], sq[:, s, 256:512], ALU.add).then_inc(sum1, 1)
                    pool.wait_ge(sum1, t + 1)
                    pool.tensor_tensor(sq[:, s, 0:128], sq[:, s, 0:128], sq[:, s, 128:256], ALU.add).then_inc(sum2, 1)

        @block.tensor
        def _(pe):
            pe.wait_ge(w_ready, KC)
            pe.wait_ge(rw_zero, 2)

            def head(t, s):
                pe.wait_ge(sum2, t + 1)
                pe.wait_ge(rA_ms, t)
                pe.matmul(psq[:, 0:P], sq[:, s, 0:P], ones[:, :], start=True, stop=True).then_inc(ssq_mm, 1)
                for banks, k0, done, free in ((pA, 0, projA, xa_ready), (pB, 4, projB, x2_ready)):
                    pe.wait_ge(free, t * 2)
                    for c in range(2):
                        for k in range(k0, k0 + 4):
                            last = pe.matmul(banks[c][:, :], yt[:, s, k, :], wo[:, k, c * 512:(c + 1) * 512], start=(k == k0), stop=(k == k0 + 3))
                        last.then_inc(done, 1)

            def tail(t, s):
                pe.wait_ge(h_ready, t + 1)
                pe.wait_ge(hT_ready, t * 2)
                for k in range(KC):
                    last = pe.transpose(pt[k // 4][:, (k % 4) * P:(k % 4 + 1) * P], h[:, s, k * P:(k + 1) * P], ident[:, :])
                    if k % 4 == 3:
                        last.then_inc(tr, 1)
                pe.wait_ge(hT_ready, t * 2 + 2)
                pe.wait_ge(lg_ready, t)
                for k in range(KC):
                    last = pe.matmul(pl[:, 0:P], hT[:, k, :], rw[:, k, :], start=(k == 0), stop=(k == KC - 1))
                last.then_inc(lg_mm, 1)

            pipelined(pe, head, tail)

        @block.scalar
        def _(act):
            def head(t, s):
                act.wait_ge(y_in[s], (t - s) * 8 + 16)
                act.wait_ge(ssq_mm, (t - s))
                act.activation(sq[:, s, :], yt[:, s, 0:4, :].rearrange("p k n -> p (k n)"), ACT.Square).then_inc(sq_ready, 1)
                act.wait_ge(rA_ms, t + 1)
                act.activation(st[:, s, 2:3], st[:, s, 1:2], ACT.Sqrt).then_inc(rA_ready, 1)

            def mid(t, s):
                act.wait_ge(x2_ready, t * 2 + 2)
                act.wait_ge(s2_ready, t)
                act.activation(junk[:, :], X2[:, ds(t, 1), :].rearrange("p a d -> p (a d)"), ACT.Square, accum_out=st[:, s, 4:5]).then_inc(s2_ready, 1)
                act.wait_ge(ms2, t + 1)
                act.activation(st[:, s, 6:7], st[:, s, 5:6], ACT.Sqrt).then_inc(rs2, 1)

            def tail(t, s):
                for b in range(2):
                    act.wait_ge(tr, t * 2 + b + 1)
                    act.wait_ge(lg_mm, t)
                    act.activation(hT[:, 4 * b:4 * b + 4, :], pt[b].rearrange("p (k n) -> p k n", k=4), ACT.Copy).then_inc(hT_ready, 1)
                act.wait_ge(h_ready, t + 1)
                act.dma_start(dram["H2"][ds(t * P, P), :], h[:, s, :]).then_inc(h_out[s], 16)

            head(0, 0)
            mid(0, 0)
            head(1, 1)
            tail(0, 0)
            mid(1, 1)
            with act.Fori(0, NT // 2 - 1) as it:
                head(it * 2 + 2, 0)
                tail(it * 2 + 1, 1)
                mid(it * 2 + 2, 0)
                head(it * 2 + 3, 1)
                tail(it * 2 + 2, 0)
                mid(it * 2 + 3, 1)
            tail(NT - 1, 1)
            for s in range(2):
                act.wait_ge(h_out[s], 16 * (NT // 2))

        @block.vector
        def _(dve):
            dve.wait_ge(w_in_, 16 * N_W)
            for k in range(KC):
                dve.tensor_scalar(wo[:, k, :], wo[:, k, :], gAB[:, k // 4, k % 4:k % 4 + 1], None, ALU.mult).then_inc(w_ready, 1)

            def root(t, s, col, src, width, first, done):
                dve.tensor_scalar(st[:, s, col:col + 1], src, 1.0 / width, EPS, ALU.mult, ALU.add).then_inc(first, 1)
                dve.wait_ge(first, t + 1)
                dve.reciprocal(st[:, s, col + 1:col + 2], st[:, s, col:col + 1]).then_inc(done, 1)

            def head(t, s):
                dve.wait_ge(ssq_mm, t + 1)
                root(t, s, 0, psq[:, 0:1], CH, rA_first, rA_ms)

            def body(t, s):
                dve.wait_ge(rA_ready, t + 1)
                dve.wait_ge(x_in[s], (t - s) * 8 + 16)
                for c in range(2):
                    dve.wait_ge(projA, t * 2 + c + 1)
                    dve.scalar_tensor_tensor(out=xt[:, s, c * 512:(c + 1) * 512], in0=pA[c][:, :], scalar=st[:, s, 2:3],
                                             in1=xt[:, s, c * 512:(c + 1) * 512], op0=ALU.mult, op1=ALU.add).then_inc(xa_ready, 1)
                for c in range(2):
                    dve.wait_ge(projB, t * 2 + c + 1)
                    dve.wait_ge(xa_ready, t * 2 + 2)
                    dve.tensor_tensor(X2[:, ds(t, 1), c * 512:(c + 1) * 512].rearrange("p a d -> p (a d)"), pB[c][:, :],
                                      xt[:, s, c * 512:(c + 1) * 512], ALU.add).then_inc(x2_ready, 1)
                dve.wait_ge(s2_ready, t + 1)
                root(t, s, 4, st[:, s, 4:5], D, ms2_first, ms2)
                dve.wait_ge(rs2, t + 1)
                dve.wait_ge(h_out[s], (t - s) * 8)
                dve.wait_ge(tr, (t - s) * 2)
                dve.scalar_tensor_tensor(out=h[:, s, :], in0=X2[:, ds(t, 1), :].rearrange("p a d -> p (a d)"), scalar=st[:, s, 6:7],
                                         in1=gain[:, :], op0=ALU.mult, op1=ALU.mult).then_inc(h_ready, 1)

            def tail(t, s):
                dve.wait_ge(lg_mm, t + 1)
                dve.tensor_tensor(LG[:, ds(t, 1), :].rearrange("p a n -> p (a n)"), pl[:, 0:NL], rb[:, :], ALU.add).then_inc(lg_ready, 1)

            head(0, 0)
            body(0, 0)
            head(1, 1)
            tail(0, 0)
            body(1, 1)
            with dve.Fori(0, NT // 2 - 1) as it:
                head(it * 2 + 2, 0)
                tail(it * 2 + 1, 1)
                body(it * 2 + 2, 0)
                head(it * 2 + 3, 1)
                tail(it * 2 + 2, 0)
                body(it * 2 + 3, 1)
            tail(NT - 1, 1)
            dve.wait_ge(lg_ready, NT)


def route(nc, dram, LG, gates, slots, idx, nblk, ident):
    NL = N_GROUPS + N_EXP
    FAR = 99.0
    with ExitStack() as ctx:
        sb = lambda name, shape, dt=F32: ctx.enter_context(nc.sbuf_tensor(name, shape, dt))
        sem = phase_semaphores(nc, ctx)
        tri, ones = sb("tri", [P, P]), sb("ones6", [P, P])
        pos8 = sb("pos8", [P, PER_GROUP])
        thr = sb("thr", [P, NT - 1])
        tok = sb("tok", [P, NT], I32)
        zero = sb("zero6", [P, N_BLOCKS + 1], I32)
        m4, c4, o4 = sb("m4", [P, NT]), sb("c4", [P, NT, 4]), sb("o4", [P, NT, 4])
        e4, gp = sb("e4", [P, NT, 4]), sb("gp", [P, NT])
        t32, sel = sb("t32", [P, NT, N_GROUPS, PER_GROUP]), sb("sel", [P, NT, PER_GROUP])
        m1, m2, c8 = sb("m1", [P, NT]), sb("m2", [P, NT]), sb("c8", [P, NT, PER_GROUP])
        o1, o2 = sb("o1", [P, NT, PER_GROUP]), sb("o2", [P, NT, PER_GROUP])
        M = [sb(f"M{i}", [P, NT, N_GROUPS, PER_GROUP]) for i in range(2)]
        Ms = sb("Ms", [P, NT, N_EXP])
        base = sb("base", [P, NT + 1, N_EXP])
        over = sb("over", [P, N_EXP, NT - 1])
        nb, cum = sb("nb", [P, N_EXP]), sb("cum", [P, N_EXP])
        pos = sb("pos", [P, NT, N_EXP])
        sl = sb("sl", [P, 2, NT])
        ex, one1 = sb("ex", [P, NT]), sb("one1", [P, NT])
        rows_i, rows_f = sb("rows_i", [N_BLOCKS + 1, P], I32), sb("rows_f", [P, P])
        pp, pt = ctx.enter_context(nc.psum_tensor("pp", [P, 512], F32)), ctx.enter_context(nc.psum_tensor("ptot", [P, 512], F32))
        pr = ctx.enter_context(nc.psum_tensor("prows", [P, 512], F32))
        c_in, steps, e_ready, exp_done, M_ready, counted = (sem(n) for n in ("c_in", "r_steps", "e_ready", "exp_done", "M_ready", "counted"))
        filled, slots_ready, zeroed, scattered, rows_in, rows_ready, rows_t = (sem(n) for n in ("filled", "slots_ready", "zeroed6", "scattered", "rows_in", "rows_ready", "rows_t"))
        block = ctx.enter_context(nc.Block())

        @block.sync
        def _(sp):
            for dst, name in ((tri, "tri"), (ones, "ones"), (pos8, "pos8"), (thr, "thr"), (tok, "tok")):
                sp.dma_start(dst[:, :], dram[name]).then_inc(c_in, 16)
            sp.wait_ge(zeroed, 1)
            sp.dma_start(dram["slot_tok"].rearrange("(p b) o -> p (b o)", p=P), zero[:, :]).then_inc(filled, 16)
            sp.wait_ge(scattered, 16 * 2 * NT)
            sp.dma_start(rows_i[:, :], dram["slot_tok"].rearrange("(b p) o -> b (p o)", p=P)).then_inc(rows_in, 16)

        @block.gpsimd
        def _(pool):
            pool.memset(zero[:, :], 0).then_inc(zeroed, 1)
            pool.wait_ge(filled, 16)
            pool.wait_ge(slots_ready, 1)
            pool.wait_ge(c_in, 16 * 5)
            for c in range(2):
                for t in range(NT):
                    pool.indirect_dma_start(out=dram["slot_tok"], out_offset=bass.IndirectOffsetOnAxis(ap=slots[:, c, t:t + 1], axis=0),
                                            in_=tok[:, t:t + 1], in_offset=None).then_inc(scattered, 16)
            pool.wait_ge(scattered, 16 * 2 * NT)

        @block.tensor
        def _(pe):
            pe.wait_ge(c_in, 16 * 5)
            pe.wait_ge(M_ready, 1)
            rhs = Ms.rearrange("p t e -> p (t e)")
            pe.matmul(pp[:, :], tri[:, :], rhs, start=True, stop=True)
            pe.matmul(pt[:, :], ones[:, :], rhs, start=True, stop=True).then_inc(counted, 1)
            pe.wait_ge(rows_ready, 2)
            pe.transpose(pr[:, 0:P], rows_f[:, :], ident[:, :]).then_inc(rows_t, 1)

        @block.scalar
        def _(act):
            act.wait_ge(e_ready, 1)
            act.activation(e4[:, :, :], e4[:, :, :], ACT.Exp).then_inc(exp_done, 1)
            act.wait_ge(e_ready, 2)
            act.activation(ex[:, :], ex[:, :], ACT.Exp).then_inc(exp_done, 1)

        @block.vector
        def _(dve):
            step = Steps(dve, steps)
            tt = lambda out, a, b, op: step(dve.tensor_tensor(out, a, b, op))
            over_last = lambda a, n: a.unsqueeze(len(a.shape)).broadcast_to([*a.shape, n])

            def first_max(x, m, c, onehot, n):
                place = pos8[:, 0:n].unsqueeze(1).broadcast_to([P, NT, n])
                step(dve.tensor_reduce(m[:, :], x, AX.X, ALU.max))
                tt(c, x, over_last(m[:, :], n), ALU.is_equal)
                tt(c, c, place, ALU.mult)
                step(dve.tensor_reduce(one1[:, :], c, AX.X, ALU.min))
                tt(onehot, place, over_last(one1[:, :], n), ALU.is_equal)

            dve.wait_ge(c_in, 16 * 5)
            lg, le = LG[:, :, 0:N_GROUPS], LG[:, :, N_GROUPS:NL].rearrange("p t (g e) -> p t g e", g=N_GROUPS)
            first_max(lg, m4, c4[:, :, :], o4[:, :, :], N_GROUPS)
            dve.tensor_tensor(e4[:, :, :], lg, over_last(m4[:, :], 4), ALU.subtract).then_inc(e_ready, 1)
            tt(t32[:, :, :, :], le, over_last(o4[:, :, :], PER_GROUP), ALU.mult)
            step(dve.tensor_reduce(sel[:, :, :], t32.rearrange("p t g e -> p t e g"), AX.X, ALU.add))
            first_max(sel[:, :, :], m1, c8[:, :, :], o1[:, :, :], PER_GROUP)
            step(dve.scalar_tensor_tensor(out=sel[:, :, :], in0=o1[:, :, :], scalar=-1e30, in1=sel[:, :, :], op0=ALU.mult, op1=ALU.add))
            first_max(sel[:, :, :], m2, c8[:, :, :], o2[:, :, :], PER_GROUP)
            dve.tensor_tensor(ex[:, :], m2[:, :], m1[:, :], ALU.subtract).then_inc(e_ready, 1)
            for i, o in enumerate((o1, o2)):
                tt(M[i][:, :, :, :], over_last(o4[:, :, :], PER_GROUP), o[:, :, :].unsqueeze(2).broadcast_to([P, NT, N_GROUPS, PER_GROUP]), ALU.mult)
            flat = [m.rearrange("p t g e -> p t (g e)") for m in M]
            dve.tensor_tensor(Ms[:, :, :], flat[0], flat[1], ALU.add).then_inc(M_ready, 1)
            dve.wait_ge(exp_done, 2)
            step(dve.tensor_reduce(gp[:, :], e4[:, :, :], AX.X, ALU.add))
            step(dve.tensor_scalar(one1[:, :], ex[:, :], 1.0, None, ALU.add))
            tt(gp[:, :], gp[:, :], one1[:, :], ALU.mult)
            step(dve.reciprocal(gates[:, 0, :], gp[:, :]))
            tt(gates[:, 1, :], gates[:, 0, :], ex[:, :], ALU.mult)
            dve.wait_ge(counted, 1)
            step(dve.memset(base[:, 0, :], 0.0))
            for t in range(NT):
                tt(base[:, t + 1, :], base[:, t, :], pt[:, t * N_EXP:(t + 1) * N_EXP], ALU.add)
            tt(over[:, :, :], over_last(base[:, NT, :], NT - 1), thr[:, :].unsqueeze(1).broadcast_to([P, N_EXP, NT - 1]), ALU.is_gt)
            step(dve.tensor_reduce(nb[:, :], over[:, :, :], AX.X, ALU.add))
            step(dve.tensor_scalar(nb[:, :], nb[:, :], 1.0, None, ALU.add))
            step(dve.memset(over[:, :, 0], 1.0))
            step(dve.tensor_tensor_scan(cum[:, :], over[:, :, 0], nb[:, :], 0.0, ALU.mult, ALU.add))
            step(dve.tensor_copy(nblk[:, 0, :], nb[:, :]))
            step(dve.tensor_copy(nblk[:, 1, :], cum[:, :]))
            tt(cum[:, :], cum[:, :], nb[:, :], ALU.subtract)
            step(dve.tensor_scalar(cum[:, :], cum[:, :], float(P), None, ALU.mult))
            tt(pos[:, :, :], pp.rearrange("p (t e) -> p t e", t=NT), base[:, 0:NT, :], ALU.add)
            tt(pos[:, :, :], pos[:, :, :], cum[:, :].unsqueeze(1).broadcast_to([P, NT, N_EXP]), ALU.add)
            for i in range(2):
                tt(flat[i], flat[i], pos[:, :, :], ALU.mult)
                step(dve.tensor_reduce(sl[:, i, :], flat[i], AX.X, ALU.add))
            dve.tensor_copy(slots[:, :, :], sl[:, :, :]).then_inc(slots_ready, 1)
            step(dve.memset(rows_f[:, :], 0.0))
            dve.wait_ge(rows_in, 16)
            dve.tensor_copy(rows_f[0:N_BLOCKS + 1, :], rows_i[:, :]).then_inc(rows_ready, 2)
            dve.wait_ge(rows_t, 1)
            step(dve.tensor_copy(idx[:, :], pr[:, 0:N_BLOCKS + 1]))


def experts(nc, dram, nblk, idx, ident):
    with ExitStack() as ctx:
        sb = lambda name, shape, dt=F32: ctx.enter_context(nc.sbuf_tensor(name, shape, dt))
        sem = phase_semaphores(nc, ctx)
        FT = D_EXP // P
        w1, w3, w2 = sb("ew1", [P, 2, KC, D_EXP]), sb("ew3", [P, 2, KC, D_EXP]), sb("ew2", [P, 2, FT, D])
        cur = sb("curidx", [P, 1], I32)
        xg, xT = sb("xg", [P, D]), sb("xT", [P, KC, P])
        s1, a, aT, yb = sb("s1", [P, D_EXP]), sb("a", [P, D_EXP]), sb("aT", [P, FT, P]), sb("yb", [P, D])
        bank = lambda name: ctx.enter_context(nc.psum_tensor(name, [P, 512], F32))
        p1, p3, pta = bank("p1"), bank("p3"), bank("pta")
        px, py = [bank("px0"), bank("px1")], [bank("pyy0"), bank("pyy1")]
        w_in = [sem(f"ew_in{r}") for r in range(2)]
        pool_passed, act_passed = sem("pool_passed"), sem("act_passed")
        idx_ready, xg_in, trx, xT_ready, h1_done, h3_done, s_ready, a_ready, tra, aT_ready, y_done, y_evac, y_out = (
            sem(n) for n in ("idx_ready", "xg_in", "trx", "xT_ready", "h1_done", "h3_done", "s_ready", "a_ready", "tra", "aT_ready", "y_done", "y_evac", "y_out"))

        def per_block(eng, name, body, at_expert=lambda e2, r: None):
            B = eng.alloc_register(f"block_{name}")
            eng.reg_mov(B, 0)
            with eng.Fori(0, N_EXP // 2) as e2:
                for r in range(2):
                    at_expert(e2, r)
                    n = eng.value_load(nblk[0:1, 0, ds(e2 * 2 + r, 1)], min_val=1, max_val=NT)
                    with eng.Fori(0, n):
                        body(eng.snap(B), r)
                        eng.reg_add(B, B, 1)
            return B

        block = ctx.enter_context(nc.Block())

        @block.sync
        def _(sp):
            def load(e, r):
                for dst, name in ((w1, "exp_w1"), (w3, "exp_w3"), (w2, "exp_w2")):
                    src = dram[name].rearrange("o e (k p) f -> p (o e) k f", p=P)[:, ds(e, 1)]
                    sp.dma_start(dst[:, r, :, :], src.rearrange("p a k f -> p (a k) f")).then_inc(w_in[r], 16)

            for r in range(2):
                load(r, r)
            with sp.Fori(0, N_EXP // 2 - 1) as e2:
                for r in range(2):
                    end = sp.value_load(nblk[0:1, 1, ds(e2 * 2 + r, 1)], min_val=1, max_val=N_BLOCKS)
                    sp.wait_ge(y_done, end)
                    load(e2 * 2 + r + 2, r)

        @block.gpsimd
        def _(pool):
            def gather(B):
                pool.tensor_copy(cur[:, :], idx[:, ds(B, 1)]).then_inc(idx_ready, 1)
                pool.wait_ge(idx_ready, B + 1)
                pool.sem_inc(pool_passed, 1)
                pool.indirect_dma_start(out=xg[:, :], out_offset=None, in_=dram["H2"],
                                        in_offset=bass.IndirectOffsetOnAxis(ap=cur[:, :], axis=0)).then_inc(xg_in, 16)

            gather(0)

            def body(B, r):
                pool.wait_ge(trx, B + 1)
                pool.wait_ge(xg_in, B * 16 + 16)
                gather(B + 1)

            B = per_block(pool, "pool", body)
            pool.wait_ge(xg_in, pool.snap(B) * 16 + 16)
            pool.sem_inc(pool_passed, 1)

        @block.tensor
        def _(pe):
            def transpose_x(B):
                pe.wait_ge(xg_in, B * 16 + 16)
                for k in range(KC):
                    last = pe.transpose(px[k // 4][:, (k % 4) * P:(k % 4 + 1) * P], xg[:, k * P:(k + 1) * P], ident[:, :])
                last.then_inc(trx, 1)

            transpose_x(0)

            def body(B, r):
                pe.wait_ge(xT_ready, B + 1)
                for bank_, w, done in ((p1, w1, h1_done), (p3, w3, h3_done)):
                    for k in range(KC):
                        last = pe.matmul(bank_[:, :], xT[:, k, :], w[:, r, k, :], start=(k == 0), stop=(k == KC - 1))
                    last.then_inc(done, 1)
                transpose_x(B + 1)
                pe.wait_ge(a_ready, B + 1)
                for k in range(FT):
                    last = pe.transpose(pta[:, k * P:(k + 1) * P], a[:, k * P:(k + 1) * P], ident[:, :])
                last.then_inc(tra, 1)
                pe.wait_ge(aT_ready, B + 1)
                pe.wait_ge(y_evac, B)
                for c in range(2):
                    for k in range(FT):
                        last = pe.matmul(py[c][:, :], aT[:, k, :], w2[:, r, k, c * 512:(c + 1) * 512], start=(k == 0), stop=(k == FT - 1))
                last.then_inc(y_done, 1)

            per_block(pe, "pe", body, lambda e2, r: pe.wait_ge(w_in[r], e2 * 48 + 48))

        @block.scalar
        def _(act):
            def evacuate_x(B):
                act.wait_ge(trx, B + 1)
                for b in range(2):
                    last = act.activation(xT[:, 4 * b:4 * b + 4, :], px[b].rearrange("p (k n) -> p k n", k=4), ACT.Copy)
                last.then_inc(xT_ready, 1)

            evacuate_x(0)

            def body(B, r):
                act.wait_ge(h1_done, B + 1)
                act.wait_ge(a_ready, B)
                act.activation(s1[:, :], p1[:, :], ACT.Silu).then_inc(s_ready, 1)
                evacuate_x(B + 1)
                act.wait_ge(y_done, B + 1)
                act.wait_ge(y_out, B * 16)
                for c in range(2):
                    last = act.activation(yb[:, c * 512:(c + 1) * 512], py[c][:, :], ACT.Copy)
                last.then_inc(y_evac, 1)
                act.wait_ge(y_evac, B + 1)
                act.dma_start(dram["YB"][ds(B * P, P), :], yb[:, :]).then_inc(y_out, 16)

            B = per_block(act, "act", body)
            act.wait_ge(y_out, act.snap(B) * 16)
            act.sem_inc(act_passed, 1)

        @block.vector
        def _(dve):
            def body(B, r):
                dve.wait_ge(h3_done, B + 1)
                dve.wait_ge(s_ready, B + 1)
                dve.wait_ge(tra, B)
                dve.tensor_tensor(a[:, :], p3[:, :], s1[:, :], ALU.mult).then_inc(a_ready, 1)
                dve.wait_ge(tra, B + 1)
                dve.wait_ge(y_done, B)
                dve.tensor_copy(aT.rearrange("p k n -> p (k n)"), pta[:, :]).then_inc(aT_ready, 1)

            per_block(dve, "dve", body)


def combine(nc, dram, X2, gates, slots):
    with ExitStack() as ctx:
        sb = lambda name, shape, dt=F32: ctx.enter_context(nc.sbuf_tensor(name, shape, dt))
        sem = phase_semaphores(nc, ctx)
        y = sb("ycomb", [P, 4, 2, D])
        out = sb("outt", [P, 2, D])
        gain = sb("gain_fin", [P, D])
        st = sb("st8", [P, 2, 4])
        gain_in, y_in = sem("gain8_in"), [sem(f"yc_in{s}") for s in range(4)]
        s1, s2, sqd, m1, m2, rs, o_ready = (sem(n) for n in ("c_s1", "c_s2", "c_sq", "c_m1", "c_m2", "c_rs", "c_out"))
        o_out = [sem(f"o_out{s}") for s in range(2)]
        out_t = dram["out"].rearrange("o (p l) d -> l p (o d)", l=NT)
        block = ctx.enter_context(nc.Block())

        @block.sync
        def _(sp):
            sp.dma_start(gain[:, :], dram["norm_final_g"].partition_broadcast(P)).then_inc(gain_in, 16)
            with sp.Fori(0, NT // 2) as it:
                for s in range(2):
                    sp.wait_ge(o_ready, it * 2 + s + 1)
                    sp.dma_start(out_t[ds(it * 2 + s, 1)].rearrange("a p d -> (a p) d"), out[:, s, :]).then_inc(o_out[s], 16)
            for s in range(2):
                sp.wait_ge(o_out[s], 16 * (NT // 2))

        @block.gpsimd
        def _(pool):
            for t in range(NT):
                if t >= 4:
                    pool.wait_ge(s2, t - 3)
                for c in range(2):
                    pool.indirect_dma_start(out=y[:, t % 4, c, :], out_offset=None, in_=dram["YB"],
                                            in_offset=bass.IndirectOffsetOnAxis(ap=slots[:, c, t:t + 1], axis=0)).then_inc(y_in[t % 4], 16)

        @block.scalar
        def _(act):
            with act.Fori(0, NT // 2) as it:
                for s in range(2):
                    t = it * 2 + s
                    act.wait_ge(s2, t + 1)
                    act.wait_ge(o_out[s], it * 16)
                    act.activation(out[:, s, :], X2[:, ds(t, 1), :].rearrange("p a d -> p (a d)"), ACT.Square, accum_out=st[:, s, 0:1]).then_inc(sqd, 1)
                    act.wait_ge(m2, t + 1)
                    act.activation(st[:, s, 3:4], st[:, s, 2:3], ACT.Sqrt).then_inc(rs, 1)

        @block.vector
        def _(dve):
            dve.wait_ge(gain_in, 16)
            with dve.Fori(0, NT // 4) as it:
                for q in range(4):
                    t, s = it * 4 + q, q % 2
                    x2 = X2[:, ds(t, 1), :].rearrange("p a d -> p (a d)")
                    dve.wait_ge(y_in[q], it * 32 + 32)
                    for c, done in ((0, s1), (1, s2)):
                        dve.scalar_tensor_tensor(out=x2, in0=y[:, q, c, :], scalar=gates[:, c, ds(t, 1)], in1=x2,
                                                 op0=ALU.mult, op1=ALU.add).then_inc(done, 1)
                        dve.wait_ge(done, t + 1)
                    dve.wait_ge(sqd, t + 1)
                    dve.tensor_scalar(st[:, s, 1:2], st[:, s, 0:1], 1.0 / D, EPS, ALU.mult, ALU.add).then_inc(m1, 1)
                    dve.wait_ge(m1, t + 1)
                    dve.reciprocal(st[:, s, 2:3], st[:, s, 1:2]).then_inc(m2, 1)
                    dve.wait_ge(rs, t + 1)
                    dve.scalar_tensor_tensor(out=out[:, s, :], in0=x2, scalar=st[:, s, 3:4], in1=gain[:, :],
                                             op0=ALU.mult, op1=ALU.mult).then_inc(o_ready, 1)


def routing_tables():
    tau, p = np.arange(NT), np.arange(P)
    return dict(tri=np.triu(np.ones((P, P), np.float32), 1), ones=np.ones((P, P), np.float32),
                pos8=np.broadcast_to(np.arange(8, dtype=np.float32) - 99, (P, 8)).copy(),
                thr=np.broadcast_to(P * np.arange(1, NT, dtype=np.float32), (P, NT - 1)).copy(),
                tok=(tau[None] * P + p[:, None]).astype(np.int32))


def build(nc, dram):
    for name, shape, dt in (("L", [3, P, NT, CH], F32), ("YT", [NT, P, KC, P], F32), ("KA", [2, R, R, CH], F32),
                            ("SA", [R, R, CH], F32), ("SI", [R, R, CH], F32), ("H2", [SEQ, D], F32),
                            ("YB", [N_SLOTS, D], F32), ("slot_tok", [(N_BLOCKS + 1) * P, 1], I32)):
        dram[name] = nc.dram_tensor(f"scratch_{name}", shape, dt, kind="Internal").ap()
    with ExitStack() as ctx:
        sb = lambda stack, name, shape, dt=F32: stack.enter_context(nc.sbuf_tensor(name, shape, dt))
        ident = sb(ctx, "ident", [P, P])
        dram["gAB"] = gAB = sb(ctx, "gAB", [P, 2, CT])
        with ExitStack() as phase:
            hT = sb(phase, "hT", [P, KC, SEQ])
            load_and_norm(nc, dram, hT, ident)
            project_and_lru(nc, dram, hT, ident)
        with ExitStack() as phase:
            invn = sb(phase, "invn", [P, 2, CH])
            cur = sb(phase, "cur", [P, NT, CH])
            skip = sb(phase, "skip", [P, CH])
            filters(nc, dram, invn)
            for o in range(2):
                conv_forward(nc, dram, o, cur, skip)
                conv_blocks(nc, dram, o)
                conv_inverse(nc, dram, o, cur, invn, ident)
        X2 = sb(ctx, "X2", [P, NT, D])
        LG = sb(ctx, "LG", [P, NT, N_GROUPS + N_EXP])
        gates, slots = sb(ctx, "gates", [P, 2, NT]), sb(ctx, "slots", [P, 2, NT], I32)
        idx = sb(ctx, "idx", [P, N_BLOCKS + 1], I32)
        nblk = sb(ctx, "nblk", [P, 2, N_EXP], I32)
        output_projection(nc, dram, X2, LG, gAB, ident)
        route(nc, dram, LG, gates, slots, idx, nblk, ident)
        experts(nc, dram, nblk, idx, ident)
        combine(nc, dram, X2, gates, slots)


_INS = ["x", "norm_mix_g", "w_in", "lru_conv_w", "lru_conv_b", "lru_wr_f", "lru_br_f", "lru_wi_f", "lru_bi_f", "lru_lambda_f",
        "lru_wr_b", "lru_br_b", "lru_wi_b", "lru_bi_b", "lru_lambda_b", "hy_conv_w", "hy_conv_b",
        "hy_filt_w1", "hy_filt_b1", "hy_filt_freq1", "hy_filt_w2", "hy_filt_b2", "hy_filt_freq2", "hy_filt_w3", "hy_skip",
        "grp_norm_lru_g", "grp_norm_hy_g", "w_out", "norm_ffn_g", "router_group_w", "router_group_b",
        "router_expert_w", "router_expert_b", "exp_w1", "exp_w3", "exp_w2", "norm_final_g"]


def kernel(**inputs):
    import numpy as _np
    import concourse.bacc as _bacc
    from concourse import mybir as _mybir
    from concourse.bass_utils import run_bass_kernel_spmd as _run

    nc = _bacc.Bacc("TRN2", target_bir_lowering=False, num_devices=1)
    arrays, dram = {}, {}
    tables = {**transform_tables(), **routing_tables()}
    for name, a in [*((n, inputs[n]) for n in _INS), *tables.items()]:
        a = _np.ascontiguousarray(a)
        arrays[f"in_{name}_dram"] = a
        dram[name] = nc.dram_tensor(f"in_{name}_dram", a.shape, _mybir.dt.from_np(a.dtype), kind="ExternalInput").ap()
    dram["out"] = nc.dram_tensor("out_0_dram", (1, SEQ, D), F32, kind="ExternalOutput").ap()
    build(nc, dram)
    r = _run(nc, [arrays], core_ids=[0])
    return r.results[0]["out_0_dram"]
```

```python
import math
from contextlib import ExitStack

import numpy as np

import concourse.bass as bass
from concourse import mybir
from concourse.bass import ds

P = 128
SEQ, D = 2048, 1024
CH = 512
KC = D // P
CT = CH // P
NCHUNK = SEQ // 512
EPS = 1e-6

N = 2 * SEQ
R = 64
HALF = R // 2
NT = 16

N_GROUPS, PER_GROUP = 4, 8
N_EXP = N_GROUPS * PER_GROUP
D_EXP = 512
N_BLOCKS = SEQ * 2 // P + N_EXP
N_SLOTS = N_BLOCKS * P

F32, I32 = mybir.dt.float32, mybir.dt.int32
ALU, ACT = mybir.AluOpType, mybir.ActivationFunctionType
AX = mybir.AxisListType


class Steps:

    def __init__(self, eng, sem, base=0):
        self.eng, self.sem, self.base, self.n = eng, sem, base, 0

    def __call__(self, ins):
        self.n += 1
        ins.then_inc(self.sem, 1)
        self.eng.wait_ge(self.sem, BASE + self.base + self.n)


BASE = 16


class PhaseSemaphores:

    def __init__(self, nc, ctx, suffix=""):
        self.nc, self.ctx, self.suffix, self.from_base, self.from_zero = nc, ctx, suffix, [], []

    def __call__(self, name, start=BASE):
        s = self.nc.alloc_semaphore(name=name + self.suffix)
        (self.from_base if start else self.from_zero).append(s)
        self.ctx.callback(self.nc.release_semaphore, s)
        return s

    def begin(self):
        with self.nc.Block() as block:
            @block.sync
            def _(sp):
                for s in self.from_base + self.from_zero:
                    sp.sem_clear(s)
                for s in self.from_base:
                    sp.sem_inc(s, BASE)
        return self.ctx.enter_context(self.nc.Block())


def load_and_norm(nc, dram, hT, ident):
    GROUPS = 4
    with ExitStack() as ctx:
        sb = lambda name, shape, dt=F32: ctx.enter_context(nc.sbuf_tensor(name, shape, dt))
        sem = PhaseSemaphores(nc, ctx)
        X = sb("X", [P, NT, D])
        junk = sb("junk", [P, D])
        gain = sb("gain", [P, D])
        xn = sb("xn", [P, 2, D])
        ssq = sb("ssq", [P, NT])
        rstd = sb("rstd", [P, NT])
        tp = [[ctx.enter_context(nc.psum_tensor(f"tp{s}{b}", [P, 512], F32)) for b in range(2)] for s in range(2)]
        x_in = [sem(f"x_in{g}") for g in range(GROUPS)]
        gain_in, ident_in = sem("gain_in"), sem("ident_in")
        squares, steps, rstd_ready = sem("squares"), sem("n_steps"), sem("rstd_ready")
        ms_ready, xn_ready, tp_ready, evacuated = sem("ms_ready"), sem("xn_ready"), sem("tp_ready"), sem("evacuated")
        per = NT // GROUPS
        x_t = dram["x"].rearrange("o (i p) d -> p (o i) d", p=P)
        block = sem.begin()

        @block.sync
        def _(sp):
            for g in range(GROUPS):
                sp.dma_start(X[:, g * per:(g + 1) * per, :], x_t[:, g * per:(g + 1) * per, :]).then_inc(x_in[g], 16)
            sp.dma_start(gain[:, :], dram["norm_mix_g"].rearrange("o d -> (o d)").partition_broadcast(P)).then_inc(gain_in, 16)
            sp.dma_start(ident[:, :], dram["ident"]).then_inc(ident_in, 16)

        @block.scalar
        def _(act):
            for g in range(GROUPS):
                act.wait_ge(x_in[g], BASE + 16)
                for i in range(g * per, (g + 1) * per):
                    if i:
                        act.wait_ge(squares, BASE + i)
                    act.activation(junk[:, :], X[:, i, :], ACT.Square, accum_out=ssq[:, i:i + 1]).then_inc(squares, 1)
            act.wait_ge(ms_ready, BASE + 1)
            act.activation(rstd[:, :], rstd[:, :], ACT.Sqrt).then_inc(rstd_ready, 1)
            with act.Fori(0, NT // 2) as it:
                for s in range(2):
                    i = it * 2 + s
                    act.wait_ge(tp_ready, BASE + i + 1)
                    for b in range(2):
                        last = act.activation(hT[:, 4 * b:4 * b + 4, ds(i * P, P)],
                                              tp[s][b].rearrange("p (k t) -> p k t", k=4), ACT.Copy)
                    last.then_inc(evacuated, 1)

        @block.vector
        def _(dve):
            step = Steps(dve, steps)
            dve.wait_ge(squares, BASE + NT)
            step(dve.tensor_scalar(ssq[:, :], ssq[:, :], 1.0 / D, EPS, ALU.mult, ALU.add))
            dve.reciprocal(rstd[:, :], ssq[:, :]).then_inc(ms_ready, 1)
            dve.wait_ge(rstd_ready, BASE + 1)
            dve.wait_ge(gain_in, BASE + 16)
            dve.sem_inc(evacuated, 2)
            with dve.Fori(0, NT // 2) as it:
                for s in range(2):
                    i = it * 2 + s
                    dve.wait_ge(evacuated, BASE + i + 1)
                    dve.scalar_tensor_tensor(out=xn[:, s, :], in0=X[:, ds(i, 1), :].rearrange("p a d -> p (a d)"),
                                             scalar=rstd[:, ds(i, 1)], in1=gain[:, :],
                                             op0=ALU.mult, op1=ALU.mult).then_inc(xn_ready, 1)

        @block.tensor
        def _(pe):
            pe.wait_ge(ident_in, BASE + 16)
            with pe.Fori(0, NT // 2) as it:
                for s in range(2):
                    i = it * 2 + s
                    pe.wait_ge(xn_ready, BASE + i + 1)
                    pe.wait_ge(evacuated, BASE + i + 1)
                    for k in range(KC):
                        last = pe.transpose(tp[s][k // 4][:, (k % 4) * P:(k % 4 + 1) * P],
                                            xn[:, s, k * P:(k + 1) * P], ident[:, :])
                    last.then_inc(tp_ready, 1)


Q_CONV_W, Q_CONV_B, Q_BR, Q_BI, Q_LAM = 0, 4, (5, 7), (6, 8), (9, 10)
Q_HW, Q_HB, Q_GA, N_Q = 11, 20, 23, 25


def project_and_lru(nc, dram, hT, ident):
    with ExitStack() as ctx:
        sb = lambda name, shape, dt=F32: ctx.enter_context(nc.sbuf_tensor(name, shape, dt))
        sem = PhaseSemaphores(nc, ctx)
        W = sb("W", [P, 4, KC, P])
        xraw = sb("xraw", [P, 2 + SEQ + 1])
        xc = sb("xc", [P, SEQ])
        hraw = sb("hraw", [P, 2, 1 + SEQ + 1])
        hc = sb("hc", [P, 2, SEQ])
        tst = sb("tst", [P, NT, P])
        T = [sb("Tf", [P, SEQ]), sb("Tb", [P, SEQ])]
        I = [sb("If", [P, SEQ]), sb("Ib", [P, SEQ])]
        Q = [sb("Qf", [P, SEQ]), sb("Qb", [P, SEQ])]
        G = I[0]
        WG = sb("WG", [P, 4, P])
        prow = sb("prow", [P, P])
        zero = sb("zero", [P, 256])
        PT = sb("PT", [P, N_Q, CT])
        par = sb("par", [P, N_Q])
        sp8 = sb("sp8", [P, 6, 8])
        pj = [ctx.enter_context(nc.psum_tensor(f"pj{n}", [P, 512], F32)) for n in range(4)]
        tp = [ctx.enter_context(nc.psum_tensor(f"tr{n}", [P, 512], F32)) for n in range(4)]
        w_in = [sem(f"w_in{k}") for k in range(5)]
        par_in, zeroed, pt_t, pt_ready, lam_exp = sem("par_in"), sem("zeroed"), sem("pt_t"), sem("pt_ready"), sem("lam_exp")
        wg_in, mm_done, evac, par_ready = sem("wg_in"), sem("mm_done"), sem("evac"), sem("par_ready")
        xc_ready, hc_ready, tr_done, tr_evac, tst_out = sem("xc_ready"), sem("hc_ready"), sem("tr_done"), sem("tr_evac"), sem("tst_out")
        tanh_ready, q1_ready, sqrt_ready, y_ready, y_out = sem("tanh_ready"), sem("q1_ready"), sem("sqrt_ready"), sem("y_ready"), sem("y_out")
        filled = sem("filled_yb")
        sp_passed = sem("sp_passed")
        steps, if_free, lam_ready = sem("p_steps"), sem("p_act"), sem("lam_ready")

        w_v = dram["w_in"].rearrange("o (k p) n -> p (o k) n", p=P)
        USES = 9
        U_X, U_V, U_R, U_I, U_X1, U_X2, U_G = 0, 1, (2, 4), (3, 5), 6, 7, 8
        tiles = [("x", 0, 0, U_X), ("v", 1024, 1, U_V), ("x1", 1536, 2, U_X1), ("x2", 2048, 0, U_X2), ("g", 512, 3, U_G)]
        gates = ["lru_wr_f", "lru_wi_f", "lru_wr_b", "lru_wi_b"]
        L_out = [dram["L"][w] for w in range(3)]
        FILL = (N_SLOTS - SEQ * 2) // CT

        block = sem.begin()

        @block.sync
        def _(sp):
            rows = [("lru_conv_w", Q_CONV_W), ("lru_conv_b", Q_CONV_B), ("lru_br_f", 5), ("lru_bi_f", 6),
                    ("lru_br_b", 7), ("lru_bi_b", 8), ("lru_lambda_f", 9), ("lru_lambda_b", 10),
                    ("hy_conv_w", Q_HW), ("hy_conv_b", Q_HB), ("grp_norm_lru_g", Q_GA), ("grp_norm_hy_g", Q_GA + 1)]
            sp.wait_ge(zeroed, BASE + 1)
            for name, q in rows:
                a = dram[name]
                v = a.rearrange("o j (r p) -> (o j r) p", p=P) if len(a.shape) == 3 else a.rearrange("o (r p) -> (o r) p", p=P)
                sp.dma_start(prow[q * CT:q * CT + v.shape[0], :], v).then_inc(par_in, 16)

            def load_w(k, c):
                _, col, slot, _ = tiles[k]
                sp.dma_start(W[:, slot, :, :], w_v[:, :, ds(c * P + col, P)]).then_inc(w_in[k], 16)

            def load_gates(c):
                for g, name in enumerate(gates):
                    for h in range(2):
                        src = dram[name].rearrange("o h i j -> (o h) i j")[ds(c * 2 + h, 1), :, :]
                        sp.dma_start(WG[R * h:R * h + R, g, R * h:R * h + R], src.rearrange("a i j -> (a i) j")).then_inc(wg_in, 16)

            def mm_of(c, use):
                sp.wait_ge(mm_done, BASE + c * (4 * USES) + 4 * (use + 1))
                sp.sem_inc(sp_passed, 1)

            def store_tiles(c, which):
                sp.wait_ge(tr_evac, BASE + c * 12 + 4 * (which + 1) + 4)
                sp.sem_inc(sp_passed, 1)
                sp.dma_start(L_out[which][:, :, ds(c * P, P)], tst[:, :, :]).then_inc(tst_out, 16)

            for k in (0, 1, 2, 4):
                load_w(k, 0)
            load_gates(0)

            def iteration(c, more):
                mm_of(c, U_X)
                load_w(3, c)
                if more:
                    mm_of(c, U_V)
                    load_w(1, c + 1)
                    mm_of(c, U_I[1])
                    load_gates(c + 1)
                    mm_of(c, U_X1)
                    load_w(2, c + 1)
                store_tiles(c, 0)
                if more:
                    mm_of(c, U_X2)
                    load_w(0, c + 1)
                store_tiles(c, 1)
                if more:
                    mm_of(c, U_G)
                    load_w(4, c + 1)
                store_tiles(c, 2)
                sp.wait_ge(y_ready, BASE + c + 1)
                sp.dma_start(dram["YT"][:, :, ds(c, 1), :].rearrange("t p c n -> p t (c n)"),
                             T[1].rearrange("p (t n) -> p t n", n=P)).then_inc(y_out, 16)

            def fill(c):
                rows = dram["YB"][ds(c * FILL + SEQ * 2, FILL), :]
                sp.dma_start(rows.rearrange("(p b) (a n) -> p (b a) n", p=P, n=256),
                             zero[:, :].unsqueeze(1).broadcast_to([P, FILL // P * 4, 256])).then_inc(filled, 16)

            with sp.Fori(0, CT - 1) as c:
                iteration(c, True)
                fill(c)
            iteration(CT - 1, False)
            fill(CT - 1)
            sp.wait_ge(tst_out, BASE + 16 * 3 * CT)
            sp.wait_ge(y_out, BASE + 16 * CT)
            sp.wait_ge(filled, BASE + 16 * CT)

        @block.gpsimd
        def _(pool):
            pool.memset(prow[:, :], 0.0)
            pool.memset(zero[:, :], 0.0)
            pool.memset(WG[:, :, :], 0.0).then_inc(zeroed, 1)

        @block.tensor
        def _(pe):
            pe.wait_ge(par_in, BASE + 16 * 12)
            pe.transpose(tp[0][:, 0:P], prow[:, :], ident[:, :]).then_inc(pt_t, 1)
            pe.wait_ge(pt_ready, BASE + 1)

            def fill(c, use, lhs, rhs, n_k, need=None):
                for n in range(NCHUNK):
                    pe.wait_ge(evac, BASE + c * (4 * USES) + 4 * use + n + 1)
                    for k in range(n_k):
                        last = pe.matmul(pj[n][:, :], lhs(k), rhs(k, n), start=(k == 0), stop=(k == n_k - 1))
                    last.then_inc(mm_done, 1)

            def project(c, k):
                _, _, slot, use = tiles[k]
                pe.wait_ge(w_in[k], BASE + c * 16 + 16)
                fill(c, use, lambda j: W[:, slot, j, :], lambda j, n: hT[:, j, n * 512:(n + 1) * 512], KC)

            def transposes(c, which, slot):
                pe.wait_ge(hc_ready, BASE + c * 3 + which + 1)
                v = hc[:, slot, :].rearrange("p (q l) -> p l q", l=NT)
                for b in range(4):
                    pe.wait_ge(tr_evac, BASE + c * 12 + 4 * which + b + 1)
                    for q in range(4):
                        last = pe.transpose(tp[b][:, q * P:(q + 1) * P], v[:, 4 * b + q], ident[:, :])
                    last.then_inc(tr_done, 1)

            with pe.Fori(0, CT) as c:
                project(c, 0)
                project(c, 1)
                pe.wait_ge(xc_ready, BASE + c + 1)
                pe.wait_ge(wg_in, BASE + c * (16 * 8) + 16 * 8)
                for g in range(4):
                    fill(c, 2 + g, lambda j, g=g: WG[:, g, :], lambda j, n: xc[:, n * 512:(n + 1) * 512], 1)
                project(c, 2)
                transposes(c, 0, 0)
                project(c, 3)
                transposes(c, 1, 1)
                project(c, 4)
                transposes(c, 2, 0)

        @block.scalar
        def _(act):
            act.wait_ge(pt_ready, BASE + 1)
            act.activation(sp8[:, 0, :], sp8[:, 0, :], ACT.Exp, scale=-1.0).then_inc(lam_exp, 1)
            act.sem_inc(evac, 4)
            act.sem_inc(tr_evac, 4)
            act.wait_ge(lam_ready, BASE + 1)

            def evacuate(c, use, out, func=ACT.Copy, bias=None):
                for n in range(NCHUNK):
                    act.wait_ge(mm_done, BASE + c * (4 * USES) + 4 * use + n + 1)
                    if bias is None:
                        ins = act.activation(out(n), pj[n][:, :], func)
                    else:
                        ins = act.activation(out(n), pj[n][:, :], func, bias=bias)
                    ins.then_inc(evac, 1)

            def evacuate_transposes(c, which):
                act.wait_ge(tst_out, BASE + c * 48 + 16 * which)
                for b in range(4):
                    act.wait_ge(tr_done, BASE + c * 12 + 4 * which + b + 1)
                    act.activation(tst[:, 4 * b:4 * b + 4, :], tp[b].rearrange("p (t n) -> p t n", n=P), ACT.Copy).then_inc(tr_evac, 1)

            with act.Fori(0, CT) as c:
                act.wait_ge(xc_ready, BASE + c)
                evacuate(c, U_X, lambda n: xraw[:, 2 + 512 * n:2 + 512 * (n + 1)])
                act.wait_ge(hc_ready, BASE + c * 3)
                evacuate(c, U_V, lambda n: hraw[:, 0, 1 + 512 * n:1 + 512 * (n + 1)])
                act.wait_ge(par_ready, BASE + c + 1)
                act.wait_ge(y_ready, BASE + c)
                act.wait_ge(y_out, BASE + c * 16)
                for d in range(2):
                    evacuate(c, U_R[d], lambda n, d=d: T[d][:, 512 * n:512 * (n + 1)], ACT.Sigmoid, par[:, Q_BR[d]:Q_BR[d] + 1])
                    evacuate(c, U_I[d], lambda n, d=d: I[d][:, 512 * n:512 * (n + 1)], ACT.Sigmoid, par[:, Q_BI[d]:Q_BI[d] + 1])
                for d in range(2):
                    act.wait_ge(evac, BASE + c * (4 * USES) + 4 * (U_R[d] + 1) + 4)
                    act.activation(T[d][:, :], T[d][:, :], ACT.Tanh, scale=par[:, Q_LAM[d]:Q_LAM[d] + 1]).then_inc(tanh_ready, 1)
                for d in range(2):
                    act.wait_ge(q1_ready, BASE + c * 2 + d + 1)
                    act.activation(T[d][:, :], T[d][:, :], ACT.Sqrt).then_inc(sqrt_ready, 1)
                evacuate(c, U_X1, lambda n: hraw[:, 1, 1 + 512 * n:1 + 512 * (n + 1)])
                evacuate_transposes(c, 0)
                act.wait_ge(hc_ready, BASE + c * 3 + 1)
                evacuate(c, U_X2, lambda n: hraw[:, 0, 1 + 512 * n:1 + 512 * (n + 1)])
                evacuate_transposes(c, 1)
                act.wait_ge(q1_ready, BASE + c * 2 + 2)
                act.wait_ge(if_free, BASE + c + 1)
                evacuate(c, U_G, lambda n: G[:, 512 * n:512 * (n + 1)], ACT.Gelu_apprx_tanh)
                evacuate_transposes(c, 2)

        @block.vector
        def _(dve):
            step = Steps(dve, steps)
            dve.memset(xraw[:, :], 0.0)
            dve.memset(hraw[:, :, :], 0.0)
            dve.wait_ge(pt_t, BASE + 1)
            step(dve.tensor_copy(PT[:, :, :].rearrange("p q c -> p (q c)"), tp[0][:, 0:N_Q * CT]))
            lam = PT[:, Q_LAM[0]:Q_LAM[1] + 1, :].rearrange("p q c -> p (q c)")
            step(dve.tensor_scalar(sp8[:, 1, :], lam, -1.0, 0.0, ALU.mult, ALU.max))
            step(dve.tensor_scalar(sp8[:, 2, :], lam, 0.0, None, ALU.max))
            dve.tensor_tensor(sp8[:, 0, :], sp8[:, 1, :], sp8[:, 2, :], ALU.add).then_inc(pt_ready, 1)
            dve.wait_ge(lam_exp, BASE + 1)
            step(dve.tensor_scalar(sp8[:, 2, :], sp8[:, 0, :], 2.0, None, ALU.add))
            step(dve.reciprocal(sp8[:, 3, :], sp8[:, 2, :]))
            step(dve.tensor_tensor(sp8[:, 2, :], sp8[:, 0, :], sp8[:, 3, :], ALU.mult))
            step(dve.tensor_tensor(sp8[:, 3, :], sp8[:, 2, :], sp8[:, 2, :], ALU.mult))
            step(dve.memset(sp8[:, 4, :], 1.0 / 17))
            for odd in range(15, 0, -2):
                step(dve.tensor_tensor(sp8[:, 4, :], sp8[:, 4, :], sp8[:, 3, :], ALU.mult))
                step(dve.tensor_scalar(sp8[:, 4, :], sp8[:, 4, :], 1.0 / odd, None, ALU.add))
            step(dve.tensor_tensor(sp8[:, 4, :], sp8[:, 4, :], sp8[:, 2, :], ALU.mult))
            step(dve.scalar_tensor_tensor(out=sp8[:, 4, :], in0=sp8[:, 4, :], scalar=2.0, in1=sp8[:, 1, :], op0=ALU.mult, op1=ALU.add))
            step(dve.tensor_scalar(lam, sp8[:, 4, :], 4.0, None, ALU.mult))
            dve.tensor_copy(dram["gAB"][:, :, :], PT[:, Q_GA:Q_GA + 2, :]).then_inc(lam_ready, 1)
            PER_C = 22

            def conv(step, out, raw, taps, q_w, stride, q_b, done):
                step(dve.tensor_scalar(out, raw[:, 0:SEQ], par[:, q_w:q_w + 1], par[:, q_b:q_b + 1], ALU.mult, ALU.add))
                for j in range(1, taps):
                    q = q_w + j * stride
                    ins = dve.scalar_tensor_tensor(out=out, in0=raw[:, j:j + SEQ], scalar=par[:, q:q + 1], in1=out,
                                                   op0=ALU.mult, op1=ALU.add)
                    if j < taps - 1:
                        step(ins)
                ins.then_inc(done, 1)

            with dve.Fori(0, CT) as c:
                step = Steps(dve, steps, c * PER_C + 27)
                dve.wait_ge(hc_ready, BASE + c * 3)
                dve.tensor_copy(par[:, :], PT[:, :, ds(c, 1)].rearrange("p q c -> p (q c)")).then_inc(par_ready, 1)
                dve.wait_ge(par_ready, BASE + c + 1)

                def hyena_conv(which, slot, use):
                    dve.wait_ge(evac, BASE + c * (4 * USES) + 4 * (use + 1) + 4)
                    dve.wait_ge(tr_done, BASE + c * 12 + (4 if which == 2 else 0))
                    conv(step, hc[:, slot, :], hraw[:, slot, :], 3, Q_HW + which, 3, Q_HB + which, hc_ready)

                def lru(d):
                    step(dve.reciprocal(Q[d][:, :], Q[d][:, :]))
                    step(dve.tensor_tensor(I[d][:, :], I[d][:, :], xc[:, :], ALU.mult))
                    step(dve.tensor_tensor(I[d][:, :], I[d][:, :], Q[d][:, :], ALU.mult))
                    dve.wait_ge(sqrt_ready, BASE + c * 2 + d + 1)
                    step(dve.scalar_tensor_tensor(out=I[d][:, :], in0=T[d][:, :], scalar=2.0, in1=I[d][:, :], op0=ALU.mult, op1=ALU.mult))
                    step(dve.tensor_scalar(Q[d][:, :], Q[d][:, :], 2.0, -1.0, ALU.mult, ALU.add))
                    o = slice(None, None, -1) if d else slice(None)
                    step(dve.tensor_tensor_scan(T[d][:, o], Q[d][:, o], I[d][:, o], 0.0, ALU.mult, ALU.add))

                dve.wait_ge(evac, BASE + c * (4 * USES) + 8)
                conv(step, xc[:, :], xraw, 4, Q_CONV_W, 1, Q_CONV_B, xc_ready)
                hyena_conv(0, 0, U_V)
                for d in range(2):
                    dve.wait_ge(tanh_ready, BASE + c * 2 + d + 1)
                    dve.tensor_scalar(Q[d][:, :], T[d][:, :], 1.0, None, ALU.add).then_inc(q1_ready, 1)
                dve.wait_ge(xc_ready, BASE + c + 1)
                dve.wait_ge(q1_ready, BASE + c * 2 + 2)
                lru(0)
                dve.sem_inc(if_free, 1)
                hyena_conv(1, 1, U_X1)
                lru(1)
                step(dve.tensor_tensor(T[0][:, :], T[0][:, :], T[1][:, :], ALU.add))
                hyena_conv(2, 0, U_X2)
                dve.wait_ge(evac, BASE + c * (4 * USES) + 4 * (U_G + 1) + 4)
                dve.tensor_tensor(T[1].rearrange("p (l q) -> p q l", q=P), T[0].rearrange("p (q l) -> p q l", l=NT),
                                  G.rearrange("p (q l) -> p q l", l=NT), ALU.mult).then_inc(y_ready, 1)
                n_steps = step.n
            assert n_steps == PER_C, n_steps

def filters(nc, dram, invn):
    L = R // 2
    MAGIC = 1.5 * 2.0 ** 23
    C1 = 6.28125
    C2 = float(np.float32(np.round((2 * math.pi - C1) * 2 ** 21) / 2 ** 21))
    C3 = 2 * math.pi - C1 - C2
    with ExitStack() as ctx:
        sb = lambda name, shape, dt=F32: ctx.enter_context(nc.sbuf_tensor(name, shape, dt))
        sem = PhaseSemaphores(nc, ctx)
        feats = sb("feats", [33, SEQ])
        w1 = sb("w1", [33, P])
        w2 = sb("w2", [P, P])
        w3 = sb("w3", [P, 2, 512])
        vec = sb("vec", [P, 4])
        fa = sb("fa", [P, P])
        ones = sb("ones", [P, P])
        arg, rnd, z1, zz = sb("arg", [P, SEQ]), sb("rnd", [P, SEQ]), sb("zf1", [P, SEQ]), sb("zz", [P, SEQ])
        zb = sb("zb", [P, 4, P])
        mask = sb("mask", [P, 2, R])
        dec = sb("dec", [P, 4, 512])
        kt = sb("kt", [P, 4, 2, 512])
        acc = sb("acc", [P, 2, 512])
        ka = sb("ka", [P, 2, 2, 512])
        kst = sb("kst", [P, 2, 2, 2, 512])
        pk = [[ctx.enter_context(nc.psum_tensor(f"pk{s}{o}", [P, 512], F32)) for o in range(2)] for s in range(2)]
        pa = [[ctx.enter_context(nc.psum_tensor(f"pa{s}{o}", [P, 512], F32)) for o in range(2)] for s in range(2)]
        flat = [pk[0][0], pk[0][1], pk[1][0], pk[1][1]]
        par_in, w2_zero, mlp_mm, arg_ready, mlp_sin = sem("f_in"), sem("w2_zero"), sem("mlp_mm"), sem("arg_ready"), sem("mlp_sin")
        steps, dec_in, zb_ready, kgen, k_ready = sem("f_steps"), [sem(f"dec_in{s}") for s in range(4)], sem("zb_ready"), sem("kgen"), sem("k_ready")
        fa_done, kst_ready, kst_out, norm_mm, inv_ready = sem("fa_done"), sem("kst_ready"), [sem(f"kst_out{i}") for i in range(2)], sem("norm_mm"), sem("inv_ready")
        summed, mask_ready, abs_ready = sem("summed"), sem("mask_ready"), sem("abs_ready")
        N_PAR = 16
        block = sem.begin()

        @block.sync
        def _(sp):
            load = lambda dst, src: sp.dma_start(dst, src).then_inc(par_in, 16)
            load(feats[:, :], dram["feats"])
            for h in range(2):
                load(w1[:, R * h:R * h + R], dram["hy_filt_w1"].rearrange("o i j -> (o i) j"))
                load(w3[R * h:R * h + R, :, :], dram["hy_filt_w3"].rearrange("o i (d r c) -> (o i) d r c", d=2, r=2)[:, h])
                for q, name in enumerate(("hy_filt_b1", "hy_filt_freq1", "hy_filt_b2", "hy_filt_freq2")):
                    load(vec[R * h:R * h + R, q:q + 1], dram[name].rearrange("o n -> n o"))
            load(fa[:, :], dram["fa_filter"])
            sp.wait_ge(w2_zero, BASE + 1)
            for h in range(2):
                load(w2[0:R, R * h:R * h + R], dram["hy_filt_w2"].rearrange("o i j -> (o i) j"))
            with sp.Fori(0, L // 4) as it:
                for s in range(4):
                    sp.wait_ge(k_ready, BASE + it * 8 + 2 * s - 6)
                    sp.dma_start(dec[:, s, :], dram["decay"][:, ds(it * 4 + s, 1), :].rearrange("p a c -> p (a c)")).then_inc(dec_in[s], 16)

        @block.gpsimd
        def _(pool):
            pool.memset(w2[:, :], 0.0).then_inc(w2_zero, 1)
            pool.memset(ones[:, :], 1.0)
            pool.wait_ge(mlp_sin, BASE + 3)
            pool.wait_ge(mask_ready, BASE + 1)
            pool.memset(acc[:, :, :], 0.0).then_inc(summed, 1)
            view = zz.rearrange("p (q l) -> p l q", l=L)

            def spread(j, s):
                pool.wait_ge(kgen, BASE + j * 2 - 6)
                pool.tensor_tensor(zb[:, s % 4, :].rearrange("p (h q) -> p h q", h=2),
                                   view[:, ds(j, 1), :].broadcast_to([P, 2, R]), mask[:, :, :], ALU.mult).then_inc(zb_ready, 1)

            def add_up(j, s):
                for o in range(2):
                    pool.wait_ge(abs_ready, BASE + j * 2 + o + 1)
                    pool.wait_ge(summed, BASE + j * 2 + 1)
                    pool.tensor_tensor(acc[:, o, :], acc[:, o, :], ka[:, s % 2, o, :], ALU.add).then_inc(summed, 1)

            spread(0, 0)
            spread(1, 1)
            with pool.Fori(0, L // 4 - 1) as it:
                for s in range(4):
                    spread(it * 4 + s + 2, s + 2)
                    add_up(it * 4 + s, s)
            for s in range(4):
                if s < 2:
                    spread(L - 4 + s + 2, s + 2)
                add_up(L - 4 + s, s)

        @block.tensor
        def _(pe):
            pe.wait_ge(par_in, BASE + 16 * N_PAR)
            for n in range(4):
                last = pe.matmul(flat[n][:, :], w1[:, :], feats[:, n * 512:(n + 1) * 512], start=True, stop=True)
            last.then_inc(mlp_mm, 1)
            pe.wait_ge(mlp_sin, BASE + 1)
            for n in range(4):
                last = pe.matmul(flat[n][:, :], w2[:, :], z1[:, n * 512:(n + 1) * 512], start=True, stop=True)
            last.then_inc(mlp_mm, 1)
            pe.wait_ge(arg_ready, BASE + 2)

            def generate(j, s):
                pe.wait_ge(zb_ready, BASE + j + 1)
                pe.wait_ge(k_ready, BASE + j * 2 - 2)
                for o in range(2):
                    pe.matmul(pk[s % 2][o][:, :], zb[:, s % 4, :], w3[:, o, :], start=True, stop=True).then_inc(kgen, 1)

            def transform(j, s):
                for o in range(2):
                    pe.wait_ge(k_ready, BASE + j * 2 + o + 1)
                    pe.wait_ge(kst_ready, BASE + j * 2 + o - 3)
                    pe.matmul(pa[s % 2][o][:, :], fa[:, :], kt[:, s, o, :], start=True, stop=True).then_inc(fa_done, 1)

            generate(0, 0)
            with pe.Fori(0, L // 4 - 1) as it:
                for s in range(4):
                    generate(it * 4 + s + 1, s + 1)
                    transform(it * 4 + s, s)
            for s in range(4):
                if s < 3:
                    generate(L - 4 + s + 1, s + 1)
                transform(L - 4 + s, s)
            pe.wait_ge(summed, BASE + 1 + 8 * (L // 4))
            for o in range(2):
                last = pe.matmul(pk[0][o][:, :], ones[:, :], acc[:, o, :], start=True, stop=True)
            last.then_inc(norm_mm, 1)

        @block.scalar
        def _(act):
            act.wait_ge(arg_ready, BASE + 1)
            act.activation(z1[:, :], arg[:, :], ACT.Sin).then_inc(mlp_sin, 1)
            act.wait_ge(arg_ready, BASE + 2)
            act.activation(zz[0:R, :], arg[0:R, :], ACT.Sin).then_inc(mlp_sin, 1)
            act.activation(zz[R:P, 1:SEQ][:, ::-1], arg[R:P, 1:SEQ], ACT.Sin).then_inc(mlp_sin, 1)
            with act.Fori(0, L // 4) as it:
                for pair in range(2):
                    act.wait_ge(kst_out[pair], BASE + it * (16 * 2))
                    for s in (2 * pair, 2 * pair + 1):
                        for o in range(2):
                            act.wait_ge(fa_done, BASE + it * 8 + 2 * s + o + 1)
                            act.activation(kst[:, pair, o, s % 2, :], pa[s % 2][o][:, :], ACT.Copy).then_inc(kst_ready, 1)
                    act.wait_ge(kst_ready, BASE + it * 8 + 4 * pair + 4)
                    for o in range(2):
                        act.dma_start(dram["KA"][o][:, ds(it * 4 + 2 * pair, 2), :], kst[:, pair, o, :, :]).then_inc(kst_out[pair], 16)
            for pair in range(2):
                act.wait_ge(kst_out[pair], BASE + 16 * 2 * (L // 4))

        @block.vector
        def _(dve):
            step = Steps(dve, steps)

            def reduce_range(b, f):
                for n in range(4):
                    last = dve.tensor_scalar(arg[:, n * 512:(n + 1) * 512], flat[n][:, :], vec[:, b:b + 1], vec[:, f:f + 1], ALU.add, ALU.mult)
                step(last)
                step(dve.tensor_scalar(rnd[:, :], arg[:, :], 1.0 / (2 * math.pi), MAGIC, ALU.mult, ALU.add))
                step(dve.tensor_scalar(rnd[:, :], rnd[:, :], MAGIC, None, ALU.subtract))
                for part in (C1, C2, C3):
                    step(dve.scalar_tensor_tensor(out=arg[:, :], in0=rnd[:, :], scalar=-part, in1=arg[:, :], op0=ALU.mult, op1=ALU.add))
                dve.tensor_scalar(arg[:, :], arg[:, :], 3.1415925, -3.1415925, ALU.min, ALU.max).then_inc(arg_ready, 1)

            dve.memset(zz[R:P, 0:1], 0.0)
            step(dve.memset(mask[:, :, :], 0.0))
            for h in range(2):
                last = dve.memset(mask[R * h:R * h + R, h, :], 1.0)
            last.then_inc(mask_ready, 1)
            dve.wait_ge(par_in, BASE + 16 * N_PAR)
            dve.wait_ge(mlp_mm, BASE + 1)
            reduce_range(0, 1)
            dve.wait_ge(mlp_mm, BASE + 2)
            dve.wait_ge(mlp_sin, BASE + 1)
            reduce_range(2, 3)
            with dve.Fori(0, L // 4) as it:
                for s in range(4):
                    dve.wait_ge(dec_in[s], BASE + it * 16 + 16)
                    for o in range(2):
                        dve.wait_ge(kgen, BASE + it * 8 + 2 * s + o + 1)
                        dve.wait_ge(fa_done, BASE + it * 8 + 2 * s + o - 7)
                        dve.tensor_tensor(kt[:, s, o, :], pk[s % 2][o][:, :], dec[:, s, :], ALU.mult).then_inc(k_ready, 1)
                        dve.wait_ge(k_ready, BASE + it * 8 + 2 * s + o + 1)
                        dve.wait_ge(summed, BASE + it * 8 + 2 * s + o - 2)
                        dve.scalar_tensor_tensor(out=ka[:, s % 2, o, :], in0=kt[:, s, o, :], scalar=-1.0, in1=kt[:, s, o, :],
                                                 op0=ALU.mult, op1=ALU.max).then_inc(abs_ready, 1)
            dve.wait_ge(norm_mm, BASE + 1)
            for o in range(2):
                step(dve.tensor_scalar(acc[:, o, :], pk[0][o][:, :], EPS, None, ALU.add))
            dve.reciprocal(invn[:, :, :], acc[:, :, :]).then_inc(inv_ready, 1)


def conv_forward(nc, dram, o, cur, skip):
    with ExitStack() as ctx:
        sb = lambda name, shape, dt=F32: ctx.enter_context(nc.sbuf_tensor(f"{name}_{o}", shape, dt))
        sem = PhaseSemaphores(nc, ctx, f"_a{o}")
        fa = sb("faz", [P, 2, P])
        st = sb("st", [P, 2, 2, 2, 512])
        pa = [[ctx.enter_context(nc.psum_tensor(f"za_{o}_{s}{h}", [P, 512], F32)) for h in range(2)] for s in range(4)]
        cur_in, fa_in, skip_in, mm, evac = [sem(f"cur_in{g}") for g in range(4)], sem("fa_in"), sem("skip_in"), sem("mm"), sem("evac")
        stored = [sem(f"stored{i}") for i in range(2)]
        block = sem.begin()

        @block.sync
        def _(sp):
            sp.dma_start(fa[:, :, :], dram["fa_signal"]).then_inc(fa_in, 16)
            if o == 0:
                for g in range(4):
                    sp.dma_start(cur[:, 4 * g:4 * g + 4, :], dram["L"][0][:, 4 * g:4 * g + 4, :]).then_inc(cur_in[g], 16)
            sp.dma_start(skip[:, :], dram["hy_skip"].rearrange("a o c -> (a o) c")[o].partition_broadcast(P)).then_inc(skip_in, 16)

        @block.tensor
        def _(pe):
            pe.wait_ge(fa_in, BASE + 16)
            if o == 0:
                for g in range(4):
                    pe.wait_ge(cur_in[g], BASE + 16)
            with pe.Fori(0, NT // 4) as it:
                for s in range(4):
                    for h in range(2):
                        pe.wait_ge(evac, BASE + it * 8 + 2 * s + h - 7)
                        pe.matmul(pa[s][h][:, :], fa[:, h, :], cur[:, ds(it * 4 + s, 1), :].rearrange("p a c -> p (a c)"),
                                  start=True, stop=True).then_inc(mm, 1)

        @block.scalar
        def _(act):
            with act.Fori(0, NT // 4) as it:
                for pair in range(2):
                    act.wait_ge(stored[pair], BASE + it * 16)
                    for s in (2 * pair, 2 * pair + 1):
                        for h in range(2):
                            act.wait_ge(mm, BASE + it * 8 + 2 * s + h + 1)
                            act.activation(st[:, pair, h, s % 2, :], pa[s][h][:, :], ACT.Copy).then_inc(evac, 1)
                    act.wait_ge(evac, BASE + it * 8 + 4 * pair + 4)
                    act.dma_start(dram["SA"][:, :, ds(it * 4 + 2 * pair, 2), :].rearrange("p h l c -> p h (l c)"),
                                  st[:, pair, :, :, :].rearrange("p h l c -> p h (l c)")).then_inc(stored[pair], 16)
            for pair in range(2):
                act.wait_ge(stored[pair], BASE + 16 * (NT // 4))

        @block.gpsimd
        def _(pool):
            pool.wait_ge(skip_in, BASE + 16)
            with pool.Fori(0, NT) as t:
                pool.wait_ge(mm, BASE + t * 2 + 2)
                tile = cur[:, ds(t, 1), :].rearrange("p a c -> p (a c)")
                pool.tensor_tensor(tile, tile, skip[:, :], ALU.mult)


def conv_blocks(nc, dram, o):
    with ExitStack() as ctx:
        sb = lambda name, shape, dt=F32: ctx.enter_context(nc.sbuf_tensor(f"{name}_{o}", shape, dt))
        sem = PhaseSemaphores(nc, ctx, f"_b{o}")
        mats = sb("mats", [P, 4, 5, P])
        zin, kin, qo = sb("zin", [P, 4, 512]), sb("kin", [P, 4, 512]), sb("qo", [P, 4, 512])
        zs, u, v = sb("zs", [P, 2, 512]), sb("u", [P, 2, 512]), sb("v", [P, 2, 512])
        bank = lambda name: [ctx.enter_context(nc.psum_tensor(f"{name}_{o}_{i}", [P, 512], F32)) for i in range(2)]
        pz, pr, pi, pq = bank("pz"), bank("pr"), bank("pi"), bank("pq")
        landed = [sem(f"landed{s}") for s in range(4)]
        fwd, zs_ready, uv_ready, inv, q_evac = sem("fwd"), sem("zs_ready"), sem("uv_ready"), sem("inv"), sem("q_evac")
        stored = [sem(f"stored{s}") for s in range(4)]
        SA, SI = (dram[n].rearrange("(j q) h l c -> j (q h l) c", q=4) for n in ("SA", "SI"))
        KA = dram["KA"][o].rearrange("(j q) l c -> j (q l) c", q=4)
        block = sem.begin()

        @block.sync
        def _(sp):
            with sp.Fori(0, HALF // 4) as it:
                for s in range(4):
                    j = it * 4 + s
                    sp.wait_ge(inv, BASE + it * 4 + s - 3)
                    sp.dma_start(mats[:, s, :, :], dram["mats"][ds(j, 1)].rearrange("a p m n -> (a p) m n")).then_inc(landed[s], 16)
                    for dst, src in ((zin, SA), (kin, KA)):
                        sp.dma_start(dst[:, s, :], src[ds(j, 1)].rearrange("a n c -> (a n) c")).then_inc(landed[s], 16)

        @block.tensor
        def _(pe):
            with pe.Fori(0, HALF // 4) as it:
                def forward(s):
                    pe.wait_ge(landed[s], BASE + it * 48 + 48)
                    pe.wait_ge(zs_ready, BASE + it * 4 + s - 1)
                    pe.wait_ge(uv_ready, BASE + it * 8 + 2 * s - 2)
                    for bank_, m, rhs in ((pz, 0, zin), (pr, 1, kin), (pi, 2, kin)):
                        pe.matmul(bank_[s % 2][:, :], mats[:, s, m, :], rhs[:, s, :], start=True, stop=True).then_inc(fwd, 1)

                def inverse(s):
                    pe.wait_ge(uv_ready, BASE + it * 8 + 2 * s + 2)
                    pe.wait_ge(q_evac, BASE + it * 4 + s - 1)
                    pe.matmul(pq[s % 2][:, :], mats[:, s, 3, :], u[:, s % 2, :], start=True, stop=False)
                    pe.matmul(pq[s % 2][:, :], mats[:, s, 4, :], v[:, s % 2, :], start=False, stop=True).then_inc(inv, 1)

                forward(0)
                for s in range(1, 4):
                    forward(s)
                    inverse(s - 1)
                inverse(3)

        @block.scalar
        def _(act):
            with act.Fori(0, HALF // 4) as it:
                def signal(s):
                    act.wait_ge(fwd, BASE + it * 12 + 3 * s + 1)
                    act.wait_ge(uv_ready, BASE + it * 8 + 2 * s - 2)
                    act.activation(zs[:, s % 2, :], pz[s % 2][:, :], ACT.Copy).then_inc(zs_ready, 1)

                def result(s):
                    act.wait_ge(stored[s], BASE + it * 16)
                    act.wait_ge(inv, BASE + it * 4 + s + 1)
                    act.activation(qo[:, s, :], pq[s % 2][:, :], ACT.Copy).then_inc(q_evac, 1)
                    act.wait_ge(q_evac, BASE + it * 4 + s + 1)
                    act.dma_start(SI[ds(it * 4 + s, 1)].rearrange("a n c -> (a n) c"), qo[:, s, :]).then_inc(stored[s], 16)

                signal(0)
                for s in range(1, 4):
                    signal(s)
                    result(s - 1)
                result(3)
            for s in range(4):
                act.wait_ge(stored[s], BASE + 16 * (HALF // 4))

        @block.vector
        def _(dve):
            with dve.Fori(0, HALF // 4) as it:
                for s in range(4):
                    dve.wait_ge(zs_ready, BASE + it * 4 + s + 1)
                    dve.wait_ge(inv, BASE + it * 4 + s - 1)
                    for n, (dst, src) in enumerate(((u, pr), (v, pi))):
                        dve.wait_ge(fwd, BASE + it * 12 + 3 * s + 2 + n)
                        dve.tensor_tensor(dst[:, s % 2, :], src[s % 2][:, :], zs[:, s % 2, :], ALU.mult).then_inc(uv_ready, 1)


def conv_inverse(nc, dram, o, cur, invn, ident):
    with ExitStack() as ctx:
        sb = lambda name, shape, dt=F32: ctx.enter_context(nc.sbuf_tensor(f"{name}_{o}", shape, dt))
        sem = PhaseSemaphores(nc, ctx, f"_c{o}")
        ia = sb("ia", [P, 2, P])
        si = sb("si", [P, 4, 2, 512])
        gate = sb("gate", [P, 4, 512])
        y = sb("y", [P, 4, 512])
        junk = sb("junkz", [P, 512])
        ssq, rstd = sb("ssqz", [P, NT]), sb("rstdz", [P, NT])
        zn = sb("zn", [P, 2, 512])
        zt = sb("zt", [P, 2, 512])
        pq = [ctx.enter_context(nc.psum_tensor(f"py_{o}_{s}", [P, 512], F32)) for s in range(4)]
        tp = [ctx.enter_context(nc.psum_tensor(f"pt_{o}_{s}", [P, 512], F32)) for s in range(2)]
        ia_in, landed, mm, scaled, added, gated = sem("ia_in"), [sem(f"landed{s}") for s in range(4)], sem("mm"), sem("scaled"), sem("added"), sem("gated")
        squared, ms, rs, zn_ready, tr, zt_ready = sem("squared"), sem("ms"), sem("rs"), sem("zn_ready"), sem("tr"), sem("zt_ready")
        stored = [sem(f"stored{s}") for s in range(2)]
        tile = lambda t: cur[:, ds(t, 1), :].rearrange("p a c -> p (a c)")
        SI = dram["SI"].rearrange("p h l c -> l p h c")
        block = sem.begin()

        @block.sync
        def _(sp):
            sp.dma_start(ia[:, :, :], dram["inv_a"]).then_inc(ia_in, 16)
            with sp.Fori(0, NT // 4) as it:
                for s in range(4):
                    sp.wait_ge(gated, BASE + it * 4 + s - 3)
                    sp.dma_start(si[:, s, :, :], SI[ds(it * 4 + s, 1)].rearrange("a p h c -> (a p) h c")).then_inc(landed[s], 16)
                    sp.dma_start(gate[:, s, :], dram["L"][1 + o][:, ds(it * 4 + s, 1), :].rearrange("p a c -> p (a c)")).then_inc(landed[s], 16)

        @block.tensor
        def _(pe):
            pe.wait_ge(ia_in, BASE + 16)
            with pe.Fori(0, NT // 4) as it:
                for s in range(4):
                    pe.wait_ge(landed[s], BASE + it * 32 + 32)
                    pe.wait_ge(scaled, BASE + it * 4 + s - 3)
                    pe.matmul(pq[s][:, :], ia[:, 0, :], si[:, s, 0, :], start=True, stop=False)
                    pe.matmul(pq[s][:, :], ia[:, 1, :], si[:, s, 1, :], start=False, stop=True).then_inc(mm, 1)
            if o == 1:
                with pe.Fori(0, NT // 2) as it:
                    for s in range(2):
                        t = it * 2 + s
                        pe.wait_ge(zn_ready, BASE + t + 1)
                        pe.wait_ge(zt_ready, BASE + it * 2)
                        for q in range(4):
                            last = pe.transpose(tp[s][:, q * P:(q + 1) * P], zn[:, s, q * P:(q + 1) * P], ident[:, :])
                        last.then_inc(tr, 1)

        @block.gpsimd
        def _(pool):
            with pool.Fori(0, NT // 4) as it:
                for s in range(4):
                    pool.wait_ge(scaled, BASE + it * 4 + s + 1)
                    pool.tensor_tensor(y[:, s, :], y[:, s, :], tile(it * 4 + s), ALU.add).then_inc(added, 1)

        @block.vector
        def _(dve):
            def scale(t, s):
                dve.wait_ge(mm, BASE + t + 1)
                dve.wait_ge(gated, BASE + t - 3)
                dve.tensor_tensor(y[:, s % 4, :], pq[s % 4][:, :], invn[:, o, :], ALU.mult).then_inc(scaled, 1)

            def apply_gate(t, s, it):
                dve.wait_ge(added, BASE + t + 1)
                dve.wait_ge(landed[s], BASE + it * 32 + 32)
                dve.tensor_tensor(tile(t), y[:, s, :], gate[:, s, :], ALU.mult).then_inc(gated, 1)

            scale(0, 0)
            scale(1, 1)
            with dve.Fori(0, NT // 4 - 1) as it:
                for s in range(4):
                    scale(it * 4 + s + 2, s + 2)
                    apply_gate(it * 4 + s, s, it)
            for s in range(4):
                if s < 2:
                    scale(NT - 2 + s, s + 2)
                apply_gate(NT - 4 + s, s, NT // 4 - 1)
            if o == 1:
                dve.wait_ge(squared, BASE + NT)
                dve.tensor_scalar(ssq[:, :], ssq[:, :], 1.0 / CH, EPS, ALU.mult, ALU.add).then_inc(ms, 1)
                dve.wait_ge(ms, BASE + 1)
                dve.reciprocal(rstd[:, :], ssq[:, :]).then_inc(ms, 1)
                dve.wait_ge(rs, BASE + 1)
                with dve.Fori(0, NT // 2) as it:
                    for s in range(2):
                        t = it * 2 + s
                        dve.wait_ge(tr, BASE + it * 2)
                        dve.tensor_scalar(zn[:, s, :], tile(t), rstd[:, ds(t, 1)], None, ALU.mult).then_inc(zn_ready, 1)

        if o == 1:
            @block.scalar
            def _(act):
                with act.Fori(0, NT) as t:
                    act.wait_ge(gated, BASE + t + 1)
                    act.wait_ge(squared, BASE + t)
                    act.activation(junk[:, :], tile(t), ACT.Square, accum_out=ssq[:, ds(t, 1)]).then_inc(squared, 1)
                act.wait_ge(ms, BASE + 2)
                act.activation(rstd[:, :], rstd[:, :], ACT.Sqrt).then_inc(rs, 1)
                with act.Fori(0, NT // 2) as it:
                    for s in range(2):
                        t = it * 2 + s
                        act.wait_ge(tr, BASE + t + 1)
                        act.wait_ge(stored[s], BASE + it * 16)
                        act.activation(zt[:, s, :], tp[s][:, :], ACT.Copy).then_inc(zt_ready, 1)
                        act.wait_ge(zt_ready, BASE + t + 1)
                        act.dma_start(dram["YT"][ds(t, 1), :, 4:8, :].rearrange("a p c n -> (a p) (c n)"), zt[:, s, :]).then_inc(stored[s], 16)
                for s in range(2):
                    act.wait_ge(stored[s], BASE + 16 * (NT // 2))


def transform_tables():
    n = np.arange
    th1 = 2 * np.pi * np.outer(n(R), n(HALF + 1)) / R
    F = np.zeros((R, R))
    F[:, 0:HALF + 1] = np.cos(th1)
    F[:, HALF + 1:] = -np.sin(th1[:, 1:HALF])
    fa_filter = np.zeros((R, 2, 2, R))
    for g in range(2):
        fa_filter[:, g, g] = F
    fa_signal = np.zeros((HALF, 4, 2, 2, R))
    inv_a = np.zeros((2, R, 2, HALF, 4))
    G = np.zeros((R, HALF))
    n1 = n(HALF)
    G[0], G[HALF] = 1, (-1.0) ** n1
    for j in range(1, HALF):
        G[j], G[HALF + j] = 2 * np.cos(2 * np.pi * n1 * j / R), -2 * np.sin(2 * np.pi * n1 * j / R)
    for h in range(2):
        for g2 in range(2):
            fa_signal[:, 2 * h + g2, h, g2] = F[:HALF]
            inv_a[g2, :, h, :, 2 * h + g2] = G / N
    n2 = n(R)
    B, Inv = np.zeros((HALF, 2, R, 2, R)), np.zeros((HALF, 2, R, 2, R))
    for j in range(1, HALF):
        th = 2 * np.pi * np.outer(n2, j + R * n(R)) / N
        B[j, 0, :, 0], B[j, 1, :, 0], B[j, 0, :, 1], B[j, 1, :, 1] = np.cos(th), np.sin(th), -np.sin(th), np.cos(th)
        Inv[j, 0, :, 0], Inv[j, 1, :, 0], Inv[j, 0, :, 1], Inv[j, 1, :, 1] = np.cos(th).T, -np.sin(th).T, np.sin(th).T, np.cos(th).T
    for s in range(R - 1):
        part, k = (1, HALF + R * s) if s < HALF else (0, R * (s - HALF + 1))
        th = 2 * np.pi * n2 * k / N
        B[0, part, :, 0, s], B[0, part, :, 1, s] = np.cos(th), -np.sin(th)
        Inv[0, 0, s, part], Inv[0, 1, s, part] = 2 * np.cos(th), -2 * np.sin(th)
    B[0, 0, :, 0, R - 1], B[0, 0, :, 1, R - 1] = 1, (-1.0) ** n2
    Inv[0, 0, R - 1, 0], Inv[0, 1, R - 1, 0] = 1, (-1.0) ** n2
    Kr, Ki = B.copy(), B.copy()
    Kr[:, :, :, 1], Ki[:, :, :, 0] = B[:, :, :, 0], B[:, :, :, 1]
    Kr[0, :, :, 1, R - 1], Ki[0, :, :, :, R - 1] = B[0, :, :, 1, R - 1], 0
    InvV = np.zeros_like(Inv)
    InvV[:, 0], InvV[:, 1] = Inv[:, 1], -Inv[:, 0]
    InvV[0, :, R - 1] = 0
    f = np.float32
    pos, t = n(SEQ, dtype=f), np.linspace(0, 1, SEQ, dtype=f)
    bands = np.linspace(1e-4, 15, 16, dtype=f)
    ang = (f(2 * math.pi / SEQ) * pos)[:, None] * bands
    feats = np.concatenate([t[:, None], np.cos(ang), np.sin(ang)], -1).T
    deltas = np.abs(np.linspace(math.log(1e-2) / 1.5, math.log(1e-2) / 0.3, CH, dtype=f))
    back = np.concatenate([np.zeros(1, f), t[1:][::-1]])
    decay = np.exp(-np.concatenate([t, back])[:, None] * deltas).reshape(P, R // 2, CH)
    kk = n(R).reshape(2, HALF).T.reshape(-1)
    fa_filter, fa_signal = fa_filter[..., kk].swapaxes(-1, -2), fa_signal[..., kk].swapaxes(-1, -2)
    inv_a = inv_a[:, kk].swapaxes(0, 1)
    ghl = n(R).reshape(2, 2, 16).swapaxes(0, 1).reshape(-1)
    B, Inv, InvV = B[:, :, ghl], Inv[..., ghl], InvV[..., ghl]
    mats = np.stack([m.reshape(HALF, P, P) for m in (B, Kr, Ki, Inv, InvV)], 2)
    out = dict(fa_filter=fa_filter.reshape(P, P), fa_signal=fa_signal.reshape(P, 2, P), inv_a=inv_a.reshape(P, 2, P),
               mats=mats, feats=feats, decay=decay, ident=np.eye(P))
    return {k: np.ascontiguousarray(v, dtype=f) for k, v in out.items()}


def output_projection(nc, dram, X2, LG, gAB, ident):
    NL = N_GROUPS + N_EXP
    with ExitStack() as ctx:
        sb = lambda name, shape, dt=F32: ctx.enter_context(nc.sbuf_tensor(name, shape, dt))
        sem = PhaseSemaphores(nc, ctx)
        wo = sb("wo", [P, KC, D])
        rw = sb("rw", [P, KC, P])
        rb = sb("rb", [P, NL])
        gain = sb("gain_ffn", [P, D])
        ones = sb("ones5", [P, P])
        yt = sb("yt", [P, 4, KC, P])
        xt = sb("xt", [P, 4, D])
        sq = sb("sq", [P, 2, 512])
        h = sb("h", [P, 2, D])
        hT = sb("hT5", [P, KC, P])
        junk = sb("junk5", [P, D])
        st = sb("st5", [P, 2, 8])
        bank = lambda name: ctx.enter_context(nc.psum_tensor(name, [P, 512], F32))
        pA, pB, pt = [bank("pA0"), bank("pA1")], [bank("pB0"), bank("pB1")], [bank("ph0"), bank("ph1")]
        pl, psq = bank("pl"), bank("psq")
        w_in_, rw_zero, w_ready = sem("wo_in"), sem("rw_zero"), sem("wo_ready")
        y_in, x_in = [sem(f"y_in{s}") for s in range(4)], [sem(f"x5_in{s}") for s in range(4)]
        sq_ready, sum1, sum2, ssq_mm, rA_ms, rA_ready = sem("sq_ready"), sem("sum1"), sem("sum2"), sem("ssq_mm"), sem("rA_ms"), sem("rA_ready")
        projA, projB, xa_ready, x2_ready = sem("projA"), sem("projB"), sem("xa_ready"), sem("x2_ready")
        s2_ready, ms2, rs2, h_ready, tr, hT_ready, lg_mm, lg_ready = (sem(n) for n in ("s2_ready", "ms2", "rs2", "h_ready", "tr5", "hT_ready", "lg_mm", "lg_ready"))
        h_out = [sem(f"h_out{s}") for s in range(2)]
        rA_first, ms2_first = sem("rA_first"), sem("ms2_first")
        N_W = 6

        def in_rounds(eng, step):
            for q in range(4):
                step(q, q, behind=q > 0)
            with eng.Fori(1, NT // 4 - 1) as it:
                for q in range(4):
                    step(it * 4 + q, q)
            for q in range(4):
                step(NT - 4 + q, q, ahead=q < 3)

        x_t = dram["x"].rearrange("o (p l) d -> l p (o d)", l=NT)
        block = sem.begin()

        @block.sync
        def _(sp):
            load = lambda dst, src: sp.dma_start(dst, src).then_inc(w_in_, 16)
            load(wo[:, :, :], dram["w_out"].rearrange("o (k p) n -> p (o k) n", p=P))
            sp.wait_ge(rw_zero, BASE + 1)
            load(rw[:, :, 0:N_GROUPS], dram["router_group_w"].rearrange("o (k p) n -> p (o k) n", p=P))
            load(rw[:, :, N_GROUPS:NL], dram["router_expert_w"].rearrange("o (k p) n -> p (o k) n", p=P))
            load(rb[:, 0:N_GROUPS], dram["router_group_b"].rearrange("o d -> (o d)").partition_broadcast(P))
            load(rb[:, N_GROUPS:NL], dram["router_expert_b"].rearrange("o d -> (o d)").partition_broadcast(P))
            load(gain[:, :], dram["norm_ffn_g"].rearrange("o d -> (o d)").partition_broadcast(P))
            with sp.Fori(0, NT // 4) as it:
                for s in range(4):
                    sp.wait_ge(x2_ready, BASE + it * 8 + 2 * s - 6)
                    sp.dma_start(yt[:, s, :, :], dram["YT"][ds(it * 4 + s, 1)].rearrange("a p k n -> (a p) k n")).then_inc(y_in[s], 16)
                    sp.dma_start(xt[:, s, :], x_t[ds(it * 4 + s, 1)].rearrange("a p d -> (a p) d")).then_inc(x_in[s], 16)

        @block.gpsimd
        def _(pool):
            pool.memset(rw[:, :, :], 0.0).then_inc(rw_zero, 1)
            pool.memset(ones[:, :], 1.0).then_inc(rw_zero, 1)
            with pool.Fori(0, NT // 2) as it:
                for s in range(2):
                    t = it * 2 + s
                    pool.wait_ge(sq_ready, BASE + t + 1)
                    pool.tensor_tensor(sq[:, s, 0:256], sq[:, s, 0:256], sq[:, s, 256:512], ALU.add).then_inc(sum1, 1)
                    pool.wait_ge(sum1, BASE + t + 1)
                    pool.tensor_tensor(sq[:, s, 0:128], sq[:, s, 0:128], sq[:, s, 128:256], ALU.add).then_inc(sum2, 1)

        @block.tensor
        def _(pe):
            pe.wait_ge(w_ready, BASE + KC)
            pe.wait_ge(rw_zero, BASE + 2)

            def half(t, q, banks, k0, done, free):
                pe.wait_ge(free, BASE + t * 2)
                for c in range(2):
                    for k in range(k0, k0 + 4):
                        last = pe.matmul(banks[c][:, :], yt[:, q, k, :], wo[:, k, c * 512:(c + 1) * 512], start=(k == k0), stop=(k == k0 + 3))
                    last.then_inc(done, 1)

            def transposes(t, s):
                pe.wait_ge(h_ready, BASE + t + 1)
                pe.wait_ge(hT_ready, BASE + t * 2)
                for k in range(KC):
                    last = pe.transpose(pt[k // 4][:, (k % 4) * P:(k % 4 + 1) * P], h[:, s, k * P:(k + 1) * P], ident[:, :])
                    if k % 4 == 3:
                        last.then_inc(tr, 1)

            def logits(t):
                pe.wait_ge(hT_ready, BASE + t * 2 + 2)
                pe.wait_ge(lg_ready, BASE + t)
                for k in range(KC):
                    last = pe.matmul(pl[:, 0:P], hT[:, k, :], rw[:, k, :], start=(k == 0), stop=(k == KC - 1))
                last.then_inc(lg_mm, 1)

            def step(t, q, behind=True, ahead=True):
                s = q % 2
                pe.wait_ge(sum2, BASE + t + 1)
                pe.wait_ge(rA_ms, BASE + t)
                pe.matmul(psq[:, 0:P], sq[:, s, 0:P], ones[:, :], start=True, stop=True).then_inc(ssq_mm, 1)
                half(t, q, pA, 0, projA, xa_ready)
                if behind:
                    transposes(t - 1, 1 - s)
                half(t, q, pB, 4, projB, x2_ready)
                if behind:
                    logits(t - 1)

            in_rounds(pe, step)
            transposes(NT - 1, 1)
            logits(NT - 1)

        @block.scalar
        def _(act):
            def squares(t, q):
                s = q % 2
                act.wait_ge(y_in[q], BASE + (t - q) * 4 + 16)
                act.wait_ge(ssq_mm, BASE + t - 1)
                act.activation(sq[:, s, :], yt[:, q, 0:4, :].rearrange("p k n -> p (k n)"), ACT.Square).then_inc(sq_ready, 1)

            def turned(t, s):
                for b in range(2):
                    act.wait_ge(tr, BASE + t * 2 + b + 1)
                    act.wait_ge(lg_mm, BASE + t)
                    act.activation(hT[:, 4 * b:4 * b + 4, :], pt[b].rearrange("p (k n) -> p k n", k=4), ACT.Copy).then_inc(hT_ready, 1)
                act.dma_start(dram["H2"][ds(t * P, P), :], h[:, s, :]).then_inc(h_out[s], 16)

            def step(t, q, behind=True, ahead=True):
                s = q % 2
                act.wait_ge(rA_ms, BASE + t + 1)
                act.activation(st[:, s, 2:3], st[:, s, 1:2], ACT.Sqrt).then_inc(rA_ready, 1)
                if ahead:
                    squares(t + 1, (q + 1) % 4)
                if behind:
                    turned(t - 1, 1 - s)
                act.wait_ge(x2_ready, BASE + t * 2 + 2)
                act.wait_ge(s2_ready, BASE + t)
                act.activation(junk[:, :], X2[:, ds(t, 1), :].rearrange("p a d -> p (a d)"), ACT.Square, accum_out=st[:, s, 4:5]).then_inc(s2_ready, 1)
                act.wait_ge(ms2, BASE + t + 1)
                act.activation(st[:, s, 6:7], st[:, s, 5:6], ACT.Sqrt).then_inc(rs2, 1)

            squares(0, 0)
            in_rounds(act, step)
            turned(NT - 1, 1)
            for s in range(2):
                act.wait_ge(h_out[s], BASE + 16 * (NT // 2))

        @block.vector
        def _(dve):
            dve.wait_ge(w_in_, BASE + 16 * N_W)
            for k in range(KC):
                dve.tensor_scalar(wo[:, k, :], wo[:, k, :], gAB[:, k // 4, k % 4:k % 4 + 1], None, ALU.mult).then_inc(w_ready, 1)

            def root(t, s, col, src, width, first, done):
                dve.tensor_scalar(st[:, s, col:col + 1], src, 1.0 / width, EPS, ALU.mult, ALU.add).then_inc(first, 1)
                dve.wait_ge(first, BASE + t + 1)
                dve.reciprocal(st[:, s, col + 1:col + 2], st[:, s, col:col + 1]).then_inc(done, 1)

            def add_bias(t):
                dve.wait_ge(lg_mm, BASE + t + 1)
                dve.tensor_tensor(LG[:, ds(t, 1), :].rearrange("p a n -> p (a n)"), pl[:, 0:NL], rb[:, :], ALU.add).then_inc(lg_ready, 1)

            def step(t, q, behind=True, ahead=True):
                s = q % 2
                dve.wait_ge(ssq_mm, BASE + t + 1)
                dve.wait_ge(rA_ready, BASE + t - 1)
                root(t, s, 0, psq[:, 0:1], CH, rA_first, rA_ms)
                dve.wait_ge(rA_ready, BASE + t + 1)
                dve.wait_ge(x_in[q], BASE + (t - q) * 4 + 16)
                for c in range(2):
                    dve.wait_ge(projA, BASE + t * 2 + c + 1)
                    dve.scalar_tensor_tensor(out=xt[:, q, c * 512:(c + 1) * 512], in0=pA[c][:, :], scalar=st[:, s, 2:3],
                                             in1=xt[:, q, c * 512:(c + 1) * 512], op0=ALU.mult, op1=ALU.add).then_inc(xa_ready, 1)
                for c in range(2):
                    dve.wait_ge(projB, BASE + t * 2 + c + 1)
                    dve.wait_ge(xa_ready, BASE + t * 2 + 2)
                    dve.tensor_tensor(X2[:, ds(t, 1), c * 512:(c + 1) * 512].rearrange("p a d -> p (a d)"), pB[c][:, :],
                                      xt[:, q, c * 512:(c + 1) * 512], ALU.add).then_inc(x2_ready, 1)
                dve.wait_ge(s2_ready, BASE + t + 1)
                root(t, s, 4, st[:, s, 4:5], D, ms2_first, ms2)
                dve.wait_ge(rs2, BASE + t + 1)
                dve.wait_ge(h_out[s], BASE + (t - s) * 8)
                dve.wait_ge(tr, BASE + t * 2 - 2)
                dve.scalar_tensor_tensor(out=h[:, s, :], in0=X2[:, ds(t, 1), :].rearrange("p a d -> p (a d)"), scalar=st[:, s, 6:7],
                                         in1=gain[:, :], op0=ALU.mult, op1=ALU.mult).then_inc(h_ready, 1)
                if behind:
                    add_bias(t - 1)

            in_rounds(dve, step)
            add_bias(NT - 1)
            dve.wait_ge(lg_ready, BASE + NT)


def route(nc, dram, LG, gates, slots, idx, nblk, ident):
    NL = N_GROUPS + N_EXP
    FAR = 99.0
    with ExitStack() as ctx:
        sb = lambda name, shape, dt=F32: ctx.enter_context(nc.sbuf_tensor(name, shape, dt))
        sem = PhaseSemaphores(nc, ctx)
        tri, ones = sb("tri", [P, P]), sb("ones6", [P, P])
        pos8 = sb("pos8", [P, PER_GROUP])
        thr = sb("thr", [P, NT - 1])
        tok = sb("tok", [P, NT], I32)
        zero = sb("zero6", [P, N_BLOCKS + 1], I32)
        m4, c4, o4 = sb("m4", [P, NT]), sb("c4", [P, NT, 4]), sb("o4", [P, NT, 4])
        e4, gp = sb("e4", [P, NT, 4]), sb("gp", [P, NT])
        t32, sel = sb("t32", [P, NT, N_GROUPS, PER_GROUP]), sb("sel", [P, NT, PER_GROUP])
        m1, m2, c8 = sb("m1", [P, NT]), sb("m2", [P, NT]), sb("c8", [P, NT, PER_GROUP])
        o1, o2 = sb("o1", [P, NT, PER_GROUP]), sb("o2", [P, NT, PER_GROUP])
        M = [sb(f"M{i}", [P, NT, N_GROUPS, PER_GROUP]) for i in range(2)]
        Ms = sb("Ms", [P, NT, N_EXP])
        base = sb("base", [P, NT + 1, N_EXP])
        over = sb("over", [P, N_EXP, NT - 1])
        nb, cum = sb("nb", [P, N_EXP]), sb("cum", [P, N_EXP])
        pos = sb("pos", [P, NT, N_EXP])
        sl = sb("sl", [P, 2, NT])
        ex, one1 = sb("ex", [P, NT]), sb("one1", [P, NT])
        rows_i, rows_f = sb("rows_i", [N_BLOCKS + 1, P], I32), sb("rows_f", [P, P])
        pp, pt = ctx.enter_context(nc.psum_tensor("pp", [P, 512], F32)), ctx.enter_context(nc.psum_tensor("ptot", [P, 512], F32))
        pr = ctx.enter_context(nc.psum_tensor("prows", [P, 512], F32))
        c_in, steps, e_ready, exp_done, M_ready, counted = (sem(n) for n in ("c_in", "r_steps", "e_ready", "exp_done", "M_ready", "counted"))
        filled, slots_ready, zeroed, rows_in, rows_ready, rows_t = (sem(n) for n in ("filled", "slots_ready", "zeroed6", "rows_in", "rows_ready", "rows_t"))
        scattered = sem("scattered", 0)
        block = sem.begin()

        @block.sync
        def _(sp):
            for dst, name in ((tri, "tri"), (ones, "ones"), (pos8, "pos8"), (thr, "thr"), (tok, "tok")):
                sp.dma_start(dst[:, :], dram[name]).then_inc(c_in, 16)
            sp.wait_ge(zeroed, BASE + 1)
            sp.dma_start(dram["slot_tok"].rearrange("(p b) o -> p (b o)", p=P), zero[:, :]).then_inc(filled, 16)
            sp.wait_ge(scattered, 16 * 2 * NT)
            sp.dma_start(rows_i[:, :], dram["slot_tok"].rearrange("(b p) o -> b (p o)", p=P)).then_inc(rows_in, 16)

        @block.gpsimd
        def _(pool):
            pool.memset(zero[:, :], 0).then_inc(zeroed, 1)
            pool.wait_ge(filled, BASE + 16)
            pool.wait_ge(slots_ready, BASE + 1)
            pool.wait_ge(c_in, BASE + 16 * 5)
            for c in range(2):
                for t in range(NT):
                    pool.indirect_dma_start(out=dram["slot_tok"], out_offset=bass.IndirectOffsetOnAxis(ap=slots[:, c, t:t + 1], axis=0),
                                            in_=tok[:, t:t + 1], in_offset=None).then_inc(scattered, 16)
            pool.wait_ge(scattered, 16 * 2 * NT)

        @block.tensor
        def _(pe):
            pe.wait_ge(c_in, BASE + 16 * 5)
            pe.wait_ge(M_ready, BASE + 1)
            rhs = Ms.rearrange("p t e -> p (t e)")
            pe.matmul(pp[:, :], tri[:, :], rhs, start=True, stop=True)
            pe.matmul(pt[:, :], ones[:, :], rhs, start=True, stop=True).then_inc(counted, 1)
            pe.wait_ge(rows_ready, BASE + 2)
            pe.transpose(pr[:, 0:P], rows_f[:, :], ident[:, :]).then_inc(rows_t, 1)

        @block.scalar
        def _(act):
            act.wait_ge(e_ready, BASE + 1)
            act.activation(e4[:, :, :], e4[:, :, :], ACT.Exp).then_inc(exp_done, 1)
            act.wait_ge(e_ready, BASE + 2)
            act.activation(ex[:, :], ex[:, :], ACT.Exp).then_inc(exp_done, 1)

        @block.vector
        def _(dve):
            step = Steps(dve, steps)
            tt = lambda out, a, b, op: step(dve.tensor_tensor(out, a, b, op))
            over_last = lambda a, n: a.unsqueeze(len(a.shape)).broadcast_to([*a.shape, n])

            def first_max(x, m, c, onehot, n):
                place = pos8[:, 0:n].unsqueeze(1).broadcast_to([P, NT, n])
                step(dve.tensor_reduce(m[:, :], x, AX.X, ALU.max))
                tt(c, x, over_last(m[:, :], n), ALU.is_equal)
                tt(c, c, place, ALU.mult)
                step(dve.tensor_reduce(one1[:, :], c, AX.X, ALU.min))
                tt(onehot, place, over_last(one1[:, :], n), ALU.is_equal)

            dve.wait_ge(c_in, BASE + 16 * 5)
            lg, le = LG[:, :, 0:N_GROUPS], LG[:, :, N_GROUPS:NL].rearrange("p t (g e) -> p t g e", g=N_GROUPS)
            first_max(lg, m4, c4[:, :, :], o4[:, :, :], N_GROUPS)
            dve.tensor_tensor(e4[:, :, :], lg, over_last(m4[:, :], 4), ALU.subtract).then_inc(e_ready, 1)
            tt(t32[:, :, :, :], le, over_last(o4[:, :, :], PER_GROUP), ALU.mult)
            step(dve.tensor_reduce(sel[:, :, :], t32.rearrange("p t g e -> p t e g"), AX.X, ALU.add))
            first_max(sel[:, :, :], m1, c8[:, :, :], o1[:, :, :], PER_GROUP)
            step(dve.scalar_tensor_tensor(out=sel[:, :, :], in0=o1[:, :, :], scalar=-1e30, in1=sel[:, :, :], op0=ALU.mult, op1=ALU.add))
            first_max(sel[:, :, :], m2, c8[:, :, :], o2[:, :, :], PER_GROUP)
            dve.tensor_tensor(ex[:, :], m2[:, :], m1[:, :], ALU.subtract).then_inc(e_ready, 1)
            for i, o in enumerate((o1, o2)):
                tt(M[i][:, :, :, :], over_last(o4[:, :, :], PER_GROUP), o[:, :, :].unsqueeze(2).broadcast_to([P, NT, N_GROUPS, PER_GROUP]), ALU.mult)
            flat = [m.rearrange("p t g e -> p t (g e)") for m in M]
            dve.tensor_tensor(Ms[:, :, :], flat[0], flat[1], ALU.add).then_inc(M_ready, 1)
            dve.wait_ge(exp_done, BASE + 2)
            step(dve.tensor_reduce(gp[:, :], e4[:, :, :], AX.X, ALU.add))
            step(dve.tensor_scalar(one1[:, :], ex[:, :], 1.0, None, ALU.add))
            tt(gp[:, :], gp[:, :], one1[:, :], ALU.mult)
            step(dve.reciprocal(gates[:, 0, :], gp[:, :]))
            tt(gates[:, 1, :], gates[:, 0, :], ex[:, :], ALU.mult)
            dve.wait_ge(counted, BASE + 1)
            step(dve.memset(base[:, 0, :], 0.0))
            for t in range(NT):
                tt(base[:, t + 1, :], base[:, t, :], pt[:, t * N_EXP:(t + 1) * N_EXP], ALU.add)
            tt(over[:, :, :], over_last(base[:, NT, :], NT - 1), thr[:, :].unsqueeze(1).broadcast_to([P, N_EXP, NT - 1]), ALU.is_gt)
            step(dve.tensor_reduce(nb[:, :], over[:, :, :], AX.X, ALU.add))
            step(dve.tensor_scalar(nb[:, :], nb[:, :], 1.0, None, ALU.add))
            step(dve.memset(over[:, :, 0], 1.0))
            step(dve.tensor_tensor_scan(cum[:, :], over[:, :, 0], nb[:, :], 0.0, ALU.mult, ALU.add))
            step(dve.tensor_copy(nblk[:, 0, :], nb[:, :]))
            step(dve.tensor_copy(nblk[:, 1, :], cum[:, :]))
            tt(cum[:, :], cum[:, :], nb[:, :], ALU.subtract)
            step(dve.tensor_scalar(cum[:, :], cum[:, :], float(P), None, ALU.mult))
            tt(pos[:, :, :], pp.rearrange("p (t e) -> p t e", t=NT), base[:, 0:NT, :], ALU.add)
            tt(pos[:, :, :], pos[:, :, :], cum[:, :].unsqueeze(1).broadcast_to([P, NT, N_EXP]), ALU.add)
            for i in range(2):
                tt(flat[i], flat[i], pos[:, :, :], ALU.mult)
                step(dve.tensor_reduce(sl[:, i, :], flat[i], AX.X, ALU.add))
            dve.tensor_copy(slots[:, :, :], sl[:, :, :]).then_inc(slots_ready, 1)
            step(dve.memset(rows_f[:, :], 0.0))
            dve.wait_ge(rows_in, BASE + 16)
            dve.tensor_copy(rows_f[0:N_BLOCKS + 1, :], rows_i[:, :]).then_inc(rows_ready, 2)
            dve.wait_ge(rows_t, BASE + 1)
            step(dve.tensor_copy(idx[:, :], pr[:, 0:N_BLOCKS + 1]))


def experts(nc, dram, nblk, idx, ident):
    with ExitStack() as ctx:
        sb = lambda name, shape, dt=F32: ctx.enter_context(nc.sbuf_tensor(name, shape, dt))
        sem = PhaseSemaphores(nc, ctx)
        FT = D_EXP // P
        w1, w3, w2 = sb("ew1", [P, 2, KC, D_EXP]), sb("ew3", [P, 2, KC, D_EXP]), sb("ew2", [P, 2, FT, D])
        cur = sb("curidx", [P, 1], I32)
        xg, xT = sb("xg", [P, D]), sb("xT", [P, KC, P])
        s1, a, aT, yb = sb("s1", [P, D_EXP]), sb("a", [P, D_EXP]), sb("aT", [P, FT, P]), sb("yb", [P, D])
        bank = lambda name: ctx.enter_context(nc.psum_tensor(name, [P, 512], F32))
        p1, p3, pta = bank("p1"), bank("p3"), bank("pta")
        px, py = [bank("px0"), bank("px1")], [bank("pyy0"), bank("pyy1")]
        w_in = [sem(f"ew_in{r}") for r in range(2)]
        pool_passed, act_passed = sem("pool_passed"), sem("act_passed")
        xg_in = sem("xg_in", 0)
        idx_ready, trx, xT_ready, h1_done, h3_done, s_ready, a_ready, tra, aT_ready, y_done, y_evac, y_out = (
            sem(n) for n in ("idx_ready", "trx", "xT_ready", "h1_done", "h3_done", "s_ready", "a_ready", "tra", "aT_ready", "y_done", "y_evac", "y_out"))

        def per_block(eng, name, body, at_expert=lambda e2, r: None):
            B = eng.alloc_register(f"block_{name}")
            eng.reg_mov(B, 0)
            with eng.Fori(0, N_EXP // 2) as e2:
                for r in range(2):
                    at_expert(e2, r)
                    n = eng.value_load(nblk[0:1, 0, ds(e2 * 2 + r, 1)], min_val=1, max_val=NT)
                    with eng.Fori(0, n):
                        body(eng.snap(B), r)
                        eng.reg_add(B, B, 1)
            return B

        block = sem.begin()

        @block.sync
        def _(sp):
            def load(e, r):
                for dst, name in ((w1, "exp_w1"), (w3, "exp_w3"), (w2, "exp_w2")):
                    src = dram[name].rearrange("o e (k p) f -> p (o e) k f", p=P)[:, ds(e, 1)]
                    sp.dma_start(dst[:, r, :, :], src.rearrange("p a k f -> p (a k) f")).then_inc(w_in[r], 16)

            for r in range(2):
                load(r, r)
            with sp.Fori(0, N_EXP // 2 - 1) as e2:
                for r in range(2):
                    end = sp.value_load(nblk[0:1, 1, ds(e2 * 2 + r, 1)], min_val=1, max_val=N_BLOCKS)
                    sp.wait_ge(y_done, BASE + end)
                    load(e2 * 2 + r + 2, r)

        @block.gpsimd
        def _(pool):
            def gather(B):
                pool.tensor_copy(cur[:, :], idx[:, ds(B, 1)]).then_inc(idx_ready, 1)
                pool.wait_ge(idx_ready, BASE + B + 1)
                pool.sem_inc(pool_passed, 1)
                pool.indirect_dma_start(out=xg[:, :], out_offset=None, in_=dram["H2"],
                                        in_offset=bass.IndirectOffsetOnAxis(ap=cur[:, :], axis=0)).then_inc(xg_in, 16)

            gather(0)

            def body(B, r):
                pool.wait_ge(trx, BASE + B + 1)
                pool.wait_ge(xg_in, B * 16 + 16)
                gather(B + 1)

            B = per_block(pool, "pool", body)
            pool.wait_ge(xg_in, pool.snap(B) * 16 + 16)
            pool.sem_inc(pool_passed, 1)

        @block.tensor
        def _(pe):
            def transpose_x(B):
                pe.wait_ge(xg_in, B * 16 + 16)
                for k in range(KC):
                    last = pe.transpose(px[k // 4][:, (k % 4) * P:(k % 4 + 1) * P], xg[:, k * P:(k + 1) * P], ident[:, :])
                last.then_inc(trx, 1)

            transpose_x(0)

            def body(B, r):
                pe.wait_ge(xT_ready, BASE + B + 1)
                for bank_, w, done in ((p1, w1, h1_done), (p3, w3, h3_done)):
                    for k in range(KC):
                        last = pe.matmul(bank_[:, :], xT[:, k, :], w[:, r, k, :], start=(k == 0), stop=(k == KC - 1))
                    last.then_inc(done, 1)
                transpose_x(B + 1)
                pe.wait_ge(a_ready, BASE + B + 1)
                for k in range(FT):
                    last = pe.transpose(pta[:, k * P:(k + 1) * P], a[:, k * P:(k + 1) * P], ident[:, :])
                last.then_inc(tra, 1)
                pe.wait_ge(aT_ready, BASE + B + 1)
                pe.wait_ge(y_evac, BASE + B)
                for c in range(2):
                    for k in range(FT):
                        last = pe.matmul(py[c][:, :], aT[:, k, :], w2[:, r, k, c * 512:(c + 1) * 512], start=(k == 0), stop=(k == FT - 1))
                last.then_inc(y_done, 1)

            per_block(pe, "pe", body, lambda e2, r: pe.wait_ge(w_in[r], BASE + e2 * 48 + 48))

        @block.scalar
        def _(act):
            def evacuate_x(B):
                act.wait_ge(trx, BASE + B + 1)
                for b in range(2):
                    last = act.activation(xT[:, 4 * b:4 * b + 4, :], px[b].rearrange("p (k n) -> p k n", k=4), ACT.Copy)
                last.then_inc(xT_ready, 1)

            evacuate_x(0)

            def body(B, r):
                act.wait_ge(h1_done, BASE + B + 1)
                act.wait_ge(a_ready, BASE + B)
                act.activation(s1[:, :], p1[:, :], ACT.Silu).then_inc(s_ready, 1)
                evacuate_x(B + 1)
                act.wait_ge(y_done, BASE + B + 1)
                act.wait_ge(y_out, BASE + B * 16)
                for c in range(2):
                    last = act.activation(yb[:, c * 512:(c + 1) * 512], py[c][:, :], ACT.Copy)
                last.then_inc(y_evac, 1)
                act.wait_ge(y_evac, BASE + B + 1)
                act.dma_start(dram["YB"][ds(B * P, P), :], yb[:, :]).then_inc(y_out, 16)

            B = per_block(act, "act", body)
            act.wait_ge(y_out, BASE + act.snap(B) * 16)
            act.sem_inc(act_passed, 1)

        @block.vector
        def _(dve):
            def body(B, r):
                dve.wait_ge(h3_done, BASE + B + 1)
                dve.wait_ge(s_ready, BASE + B + 1)
                dve.wait_ge(tra, BASE + B)
                dve.tensor_tensor(a[:, :], p3[:, :], s1[:, :], ALU.mult).then_inc(a_ready, 1)
                dve.wait_ge(tra, BASE + B + 1)
                dve.wait_ge(y_done, BASE + B)
                dve.tensor_copy(aT.rearrange("p k n -> p (k n)"), pta[:, :]).then_inc(aT_ready, 1)

            per_block(dve, "dve", body)


def combine(nc, dram, X2, gates, slots):
    with ExitStack() as ctx:
        sb = lambda name, shape, dt=F32: ctx.enter_context(nc.sbuf_tensor(name, shape, dt))
        sem = PhaseSemaphores(nc, ctx)
        y = sb("ycomb", [P, 4, 2, D])
        out = sb("outt", [P, 2, D])
        gain = sb("gain_fin", [P, D])
        st = sb("st8", [P, 2, 4])
        gain_in, y_in = sem("gain8_in"), [sem(f"yc_in{s}", 0) for s in range(4)]
        s1, s2, sqd, m1, m2, rs, o_ready = (sem(n) for n in ("c_s1", "c_s2", "c_sq", "c_m1", "c_m2", "c_rs", "c_out"))
        o_out = [sem(f"o_out{s}") for s in range(2)]
        out_t = dram["out"].rearrange("o (p l) d -> l p (o d)", l=NT)
        block = sem.begin()

        @block.sync
        def _(sp):
            sp.dma_start(gain[:, :], dram["norm_final_g"].partition_broadcast(P)).then_inc(gain_in, 16)
            with sp.Fori(0, NT // 2) as it:
                for s in range(2):
                    sp.wait_ge(o_ready, BASE + it * 2 + s + 1)
                    sp.dma_start(out_t[ds(it * 2 + s, 1)].rearrange("a p d -> (a p) d"), out[:, s, :]).then_inc(o_out[s], 16)
            for s in range(2):
                sp.wait_ge(o_out[s], BASE + 16 * (NT // 2))

        @block.gpsimd
        def _(pool):
            for t in range(NT):
                if t >= 4:
                    pool.wait_ge(s2, BASE + t - 3)
                for c in range(2):
                    pool.indirect_dma_start(out=y[:, t % 4, c, :], out_offset=None, in_=dram["YB"],
                                            in_offset=bass.IndirectOffsetOnAxis(ap=slots[:, c, t:t + 1], axis=0)).then_inc(y_in[t % 4], 16)

        @block.scalar
        def _(act):
            with act.Fori(0, NT // 2) as it:
                for s in range(2):
                    t = it * 2 + s
                    act.wait_ge(s2, BASE + t + 1)
                    act.wait_ge(o_out[s], BASE + it * 16)
                    act.activation(out[:, s, :], X2[:, ds(t, 1), :].rearrange("p a d -> p (a d)"), ACT.Square, accum_out=st[:, s, 0:1]).then_inc(sqd, 1)
                    act.wait_ge(m2, BASE + t + 1)
                    act.activation(st[:, s, 3:4], st[:, s, 2:3], ACT.Sqrt).then_inc(rs, 1)

        @block.vector
        def _(dve):
            dve.wait_ge(gain_in, BASE + 16)
            with dve.Fori(0, NT // 4) as it:
                for q in range(4):
                    t, s = it * 4 + q, q % 2
                    x2 = X2[:, ds(t, 1), :].rearrange("p a d -> p (a d)")
                    dve.wait_ge(y_in[q], it * 32 + 32)
                    for c, done in ((0, s1), (1, s2)):
                        dve.scalar_tensor_tensor(out=x2, in0=y[:, q, c, :], scalar=gates[:, c, ds(t, 1)], in1=x2,
                                                 op0=ALU.mult, op1=ALU.add).then_inc(done, 1)
                        dve.wait_ge(done, BASE + t + 1)
                    dve.wait_ge(sqd, BASE + t + 1)
                    dve.tensor_scalar(st[:, s, 1:2], st[:, s, 0:1], 1.0 / D, EPS, ALU.mult, ALU.add).then_inc(m1, 1)
                    dve.wait_ge(m1, BASE + t + 1)
                    dve.reciprocal(st[:, s, 2:3], st[:, s, 1:2]).then_inc(m2, 1)
                    dve.wait_ge(rs, BASE + t + 1)
                    dve.scalar_tensor_tensor(out=out[:, s, :], in0=x2, scalar=st[:, s, 3:4], in1=gain[:, :],
                                             op0=ALU.mult, op1=ALU.mult).then_inc(o_ready, 1)


def routing_tables():
    tau, p = np.arange(NT), np.arange(P)
    return dict(tri=np.triu(np.ones((P, P), np.float32), 1), ones=np.ones((P, P), np.float32),
                pos8=np.broadcast_to(np.arange(8, dtype=np.float32) - 99, (P, 8)).copy(),
                thr=np.broadcast_to(P * np.arange(1, NT, dtype=np.float32), (P, NT - 1)).copy(),
                tok=(tau[None] * P + p[:, None]).astype(np.int32))


def build(nc, dram):
    for name, shape, dt in (("L", [3, P, NT, CH], F32), ("YT", [NT, P, KC, P], F32), ("KA", [2, P, R // 2, CH], F32),
                            ("SA", [P, 2, NT, CH], F32), ("SI", [P, 2, NT, CH], F32), ("H2", [SEQ, D], F32),
                            ("YB", [N_SLOTS, D], F32), ("slot_tok", [(N_BLOCKS + 1) * P, 1], I32)):
        dram[name] = nc.dram_tensor(f"scratch_{name}", shape, dt, kind="Internal").ap()
    with ExitStack() as ctx:
        sb = lambda stack, name, shape, dt=F32: stack.enter_context(nc.sbuf_tensor(name, shape, dt))
        ident = sb(ctx, "ident", [P, P])
        dram["gAB"] = gAB = sb(ctx, "gAB", [P, 2, CT])
        with ExitStack() as phase:
            hT = sb(phase, "hT", [P, KC, SEQ])
            load_and_norm(nc, dram, hT, ident)
            project_and_lru(nc, dram, hT, ident)
        with ExitStack() as phase:
            invn = sb(phase, "invn", [P, 2, CH])
            cur = sb(phase, "cur", [P, NT, CH])
            skip = sb(phase, "skip", [P, CH])
            filters(nc, dram, invn)
            for o in range(2):
                conv_forward(nc, dram, o, cur, skip)
                conv_blocks(nc, dram, o)
                conv_inverse(nc, dram, o, cur, invn, ident)
        X2 = sb(ctx, "X2", [P, NT, D])
        LG = sb(ctx, "LG", [P, NT, N_GROUPS + N_EXP])
        gates, slots = sb(ctx, "gates", [P, 2, NT]), sb(ctx, "slots", [P, 2, NT], I32)
        idx = sb(ctx, "idx", [P, N_BLOCKS + 1], I32)
        nblk = sb(ctx, "nblk", [P, 2, N_EXP], I32)
        output_projection(nc, dram, X2, LG, gAB, ident)
        route(nc, dram, LG, gates, slots, idx, nblk, ident)
        experts(nc, dram, nblk, idx, ident)
        combine(nc, dram, X2, gates, slots)


_INS = ["x", "norm_mix_g", "w_in", "lru_conv_w", "lru_conv_b", "lru_wr_f", "lru_br_f", "lru_wi_f", "lru_bi_f", "lru_lambda_f",
        "lru_wr_b", "lru_br_b", "lru_wi_b", "lru_bi_b", "lru_lambda_b", "hy_conv_w", "hy_conv_b",
        "hy_filt_w1", "hy_filt_b1", "hy_filt_freq1", "hy_filt_w2", "hy_filt_b2", "hy_filt_freq2", "hy_filt_w3", "hy_skip",
        "grp_norm_lru_g", "grp_norm_hy_g", "w_out", "norm_ffn_g", "router_group_w", "router_group_b",
        "router_expert_w", "router_expert_b", "exp_w1", "exp_w3", "exp_w2", "norm_final_g"]


def kernel(**inputs):
    import numpy as _np
    import concourse.bacc as _bacc
    from concourse import mybir as _mybir
    from concourse.bass_utils import run_bass_kernel_spmd as _run

    nc = _bacc.Bacc("TRN2", target_bir_lowering=False, num_devices=1)
    arrays, dram = {}, {}
    tables = {**transform_tables(), **routing_tables()}
    for name, a in [*((n, inputs[n]) for n in _INS), *tables.items()]:
        a = _np.ascontiguousarray(a)
        arrays[f"in_{name}_dram"] = a
        dram[name] = nc.dram_tensor(f"in_{name}_dram", a.shape, _mybir.dt.from_np(a.dtype), kind="ExternalInput").ap()
    dram["out"] = nc.dram_tensor("out_0_dram", (1, SEQ, D), F32, kind="ExternalOutput").ap()
    build(nc, dram)
    r = _run(nc, [arrays], core_ids=[0])
    return r.results[0]["out_0_dram"]
```

```python
import math
from contextlib import ExitStack

import numpy as np

import concourse.bass as bass
from concourse import mybir
from concourse.bass import ds

P = 128
SEQ, D = 2048, 1024
CH = 512
KC = D // P
CT = CH // P
NCHUNK = SEQ // 512
EPS = 1e-6

N = 2 * SEQ
R = 64
HALF = R // 2
NT = 16

N_GROUPS, PER_GROUP = 4, 8
N_EXP = N_GROUPS * PER_GROUP
D_EXP = 512
N_BLOCKS = SEQ * 2 // P + N_EXP
LEAD = 2
N_SLOTS = (LEAD + N_BLOCKS) * P
IDX_COLS = LEAD + N_BLOCKS + 2

F32, I32 = mybir.dt.float32, mybir.dt.int32
F32R = mybir.dt.float32r
ALU, ACT = mybir.AluOpType, mybir.ActivationFunctionType
AX = mybir.AxisListType


class Steps:

    def __init__(self, eng, sem, base=0):
        self.eng, self.sem, self.base, self.n = eng, sem, base, 0

    def __call__(self, ins):
        self.n += 1
        ins.then_inc(self.sem, 1)
        self.eng.wait_ge(self.sem, BASE + self.base + self.n)


BASE = 16


class PhaseSemaphores:

    def __init__(self, nc, ctx, suffix=""):
        self.nc, self.ctx, self.suffix, self.from_base, self.from_zero = nc, ctx, suffix, [], []

    def __call__(self, name, start=BASE):
        s = self.nc.alloc_semaphore(name=name + self.suffix)
        (self.from_base if start else self.from_zero).append(s)
        self.ctx.callback(self.nc.release_semaphore, s)
        return s

    def begin(self):
        with self.nc.Block() as block:
            @block.sync
            def _(sp):
                for s in self.from_base + self.from_zero:
                    sp.sem_clear(s)
                for s in self.from_base:
                    sp.sem_inc(s, BASE)
        return self.ctx.enter_context(self.nc.Block())


def load_and_norm(nc, dram, hT, ident):
    GROUPS = 4
    MAGIC = 1.5 * 2.0 ** 23
    C1 = 6.28125
    C2 = float(np.float32(np.round((2 * math.pi - C1) * 2 ** 21) / 2 ** 21))
    C3 = 2 * math.pi - C1 - C2
    with ExitStack() as ctx:
        sb = lambda name, shape, dt=F32: ctx.enter_context(nc.sbuf_tensor(name, shape, dt))
        sem = PhaseSemaphores(nc, ctx)
        X = sb("X", [P, NT, D])
        junk = sb("junk", [P, D])
        gain = sb("gain", [P, D])
        xn = sb("xn", [P, 2, D])
        ssq = sb("ssq", [P, NT])
        rstd = sb("rstd", [P, NT])
        tp = [[ctx.enter_context(nc.psum_tensor(f"tp{s}{b}", [P, 512], F32)) for b in range(2)] for s in range(2)]
        feats, w1, w2 = sb("feats", [33, SEQ]), sb("w1", [33, P]), sb("w2", [P, P])
        vec = sb("vec", [P, 4])
        arg, rnd, z1, zz = sb("arg", [P, SEQ]), sb("rnd", [P, SEQ]), sb("zf1", [P, SEQ]), sb("zz1", [P, SEQ])
        flat = [ctx.enter_context(nc.psum_tensor(f"flat{n}", [P, 512], F32)) for n in range(4)]
        par_in, w2_zero, mlp_mm, arg_ready, mlp_sin, zz_out = (sem(n) for n in ("mlp_in", "w2_zero", "mlp_mm", "arg_ready", "mlp_sin", "zz_out"))
        N_PAR = 13
        x_in = [sem(f"x_in{g}") for g in range(GROUPS)]
        gain_in, ident_in = sem("gain_in"), sem("ident_in")
        squares, steps, rstd_ready = sem("squares"), sem("n_steps"), sem("rstd_ready")
        ms_ready, xn_ready, tp_ready, evacuated = sem("ms_ready"), sem("xn_ready"), sem("tp_ready"), sem("evacuated")
        per = NT // GROUPS
        x_t = dram["x"].rearrange("o (i p) d -> p (o i) d", p=P)
        block = sem.begin()

        @block.sync
        def _(sp):
            load = lambda dst, src: sp.dma_start(dst, src).then_inc(par_in, 16)
            load(feats[:, :], dram["feats"])
            for h in range(2):
                load(w1[:, R * h:R * h + R], dram["hy_filt_w1"].rearrange("o i j -> (o i) j"))
                for q, name in enumerate(("hy_filt_b1", "hy_filt_freq1", "hy_filt_b2", "hy_filt_freq2")):
                    load(vec[R * h:R * h + R, q:q + 1], dram[name].rearrange("o n -> n o"))
            sp.wait_ge(w2_zero, BASE + 1)
            for h in range(2):
                load(w2[0:R, R * h:R * h + R], dram["hy_filt_w2"].rearrange("o i j -> (o i) j"))
            for g in range(GROUPS):
                sp.dma_start(X[:, g * per:(g + 1) * per, :], x_t[:, g * per:(g + 1) * per, :]).then_inc(x_in[g], 16)
            sp.dma_start(gain[:, :], dram["norm_mix_g"].rearrange("o d -> (o d)").partition_broadcast(P)).then_inc(gain_in, 16)
            sp.dma_start(ident[:, :], dram["ident"]).then_inc(ident_in, 16)
            sp.wait_ge(mlp_sin, BASE + 3)
            sp.dma_start(dram["ZZ"], zz[:, :]).then_inc(zz_out, 16)
            sp.wait_ge(zz_out, BASE + 16)

        @block.gpsimd
        def _(pool):
            pool.memset(w2[:, :], 0.0).then_inc(w2_zero, 1)

        @block.scalar
        def _(act):
            for g in range(GROUPS):
                act.wait_ge(x_in[g], BASE + 16)
                for i in range(g * per, (g + 1) * per):
                    if i:
                        act.wait_ge(squares, BASE + i)
                    act.activation(junk[:, :], X[:, i, :], ACT.Square, accum_out=ssq[:, i:i + 1]).then_inc(squares, 1)
                if g == 0:
                    act.wait_ge(arg_ready, BASE + 1)
                    act.activation(z1[:, :], arg[:, :], ACT.Sin).then_inc(mlp_sin, 1)
            act.wait_ge(arg_ready, BASE + 2)
            act.activation(zz[0:R, :], arg[0:R, :], ACT.Sin).then_inc(mlp_sin, 1)
            act.activation(zz[R:P, 1:SEQ][:, ::-1], arg[R:P, 1:SEQ], ACT.Sin).then_inc(mlp_sin, 1)
            act.wait_ge(ms_ready, BASE + 1)
            act.activation(rstd[:, :], rstd[:, :], ACT.Sqrt).then_inc(rstd_ready, 1)
            with act.Fori(0, NT // 2) as it:
                for s in range(2):
                    i = it * 2 + s
                    act.wait_ge(tp_ready, BASE + i + 1)
                    for b in range(2):
                        last = act.activation(hT[:, 4 * b:4 * b + 4, ds(i * P, P)],
                                              tp[s][b].rearrange("p (k t) -> p k t", k=4), ACT.Copy)
                    last.then_inc(evacuated, 1)

        @block.vector
        def _(dve):
            step = Steps(dve, steps)

            def reduce_range(b, f):
                for n in range(4):
                    last = dve.tensor_scalar(arg[:, n * 512:(n + 1) * 512], flat[n][:, :], vec[:, b:b + 1], vec[:, f:f + 1], ALU.add, ALU.mult)
                step(last)
                step(dve.tensor_scalar(rnd[:, :], arg[:, :], 1.0 / (2 * math.pi), MAGIC, ALU.mult, ALU.add))
                step(dve.tensor_scalar(rnd[:, :], rnd[:, :], MAGIC, None, ALU.subtract))
                for part in (C1, C2, C3):
                    step(dve.scalar_tensor_tensor(out=arg[:, :], in0=rnd[:, :], scalar=-part, in1=arg[:, :], op0=ALU.mult, op1=ALU.add))
                dve.tensor_scalar(arg[:, :], arg[:, :], 3.1415925, -3.1415925, ALU.min, ALU.max).then_inc(arg_ready, 1)

            dve.memset(zz[R:P, 0:1], 0.0)
            dve.wait_ge(par_in, BASE + 16 * N_PAR)
            dve.wait_ge(mlp_mm, BASE + 1)
            reduce_range(0, 1)
            dve.wait_ge(mlp_mm, BASE + 2)
            dve.wait_ge(mlp_sin, BASE + 1)
            reduce_range(2, 3)
            dve.wait_ge(squares, BASE + NT)
            step(dve.tensor_scalar(ssq[:, :], ssq[:, :], 1.0 / D, EPS, ALU.mult, ALU.add))
            dve.reciprocal(rstd[:, :], ssq[:, :]).then_inc(ms_ready, 1)
            dve.wait_ge(rstd_ready, BASE + 1)
            dve.wait_ge(gain_in, BASE + 16)
            dve.sem_inc(evacuated, 2)
            with dve.Fori(0, NT // 2) as it:
                for s in range(2):
                    i = it * 2 + s
                    dve.wait_ge(evacuated, BASE + i + 1)
                    dve.scalar_tensor_tensor(out=xn[:, s, :], in0=X[:, ds(i, 1), :].rearrange("p a d -> p (a d)"),
                                             scalar=rstd[:, ds(i, 1)], in1=gain[:, :],
                                             op0=ALU.mult, op1=ALU.mult).then_inc(xn_ready, 1)

        @block.tensor
        def _(pe):
            pe.wait_ge(par_in, BASE + 16 * N_PAR)
            for n in range(4):
                last = pe.matmul(flat[n][:, :], w1[:, :], feats[:, n * 512:(n + 1) * 512], start=True, stop=True)
            last.then_inc(mlp_mm, 1)
            pe.wait_ge(mlp_sin, BASE + 1)
            for n in range(4):
                last = pe.matmul(flat[n][:, :], w2[:, :], z1[:, n * 512:(n + 1) * 512], start=True, stop=True)
            last.then_inc(mlp_mm, 1)
            pe.wait_ge(ident_in, BASE + 16)
            with pe.Fori(0, NT // 2) as it:
                for s in range(2):
                    i = it * 2 + s
                    pe.wait_ge(xn_ready, BASE + i + 1)
                    pe.wait_ge(evacuated, BASE + i + 1)
                    for k in range(KC):
                        last = pe.transpose(tp[s][k // 4][:, (k % 4) * P:(k % 4 + 1) * P],
                                            xn[:, s, k * P:(k + 1) * P], ident[:, :])
                    last.then_inc(tp_ready, 1)


Q_CONV_W, Q_CONV_B, Q_BR, Q_BI, Q_LAM = 0, 4, (5, 7), (6, 8), (9, 10)
Q_HW, Q_HB, Q_GA, N_Q = 11, 20, 23, 25


def project_and_lru(nc, dram, hT, ident):
    with ExitStack() as ctx:
        sb = lambda name, shape, dt=F32: ctx.enter_context(nc.sbuf_tensor(name, shape, dt))
        sem = PhaseSemaphores(nc, ctx)
        W = sb("W", [P, 4, KC, P])
        xraw = sb("xraw", [P, 2 + SEQ + 1])
        xc = sb("xc", [P, SEQ])
        hraw = sb("hraw", [P, 2, 1 + SEQ + 1])
        hc = sb("hc", [P, 2, SEQ])
        tst = sb("tst", [P, NT, P])
        T = [sb("Tf", [P, SEQ]), sb("Tb", [P, SEQ])]
        I = [sb("If", [P, SEQ]), sb("Ib", [P, SEQ])]
        Q = [sb("Qf", [P, SEQ]), sb("Qb", [P, SEQ])]
        G = I[0]
        WG = sb("WG", [P, 4, P])
        prow = sb("prow", [P, P])
        zero = sb("zero", [P, 256])
        PT = sb("PT", [P, N_Q, CT])
        par = sb("par", [P, N_Q])
        sp8 = sb("sp8", [P, 6, 8])
        pj = [ctx.enter_context(nc.psum_tensor(f"pj{n}", [P, 512], F32)) for n in range(4)]
        tp = [ctx.enter_context(nc.psum_tensor(f"tr{n}", [P, 512], F32)) for n in range(4)]
        w_in = [sem(f"w_in{k}") for k in range(5)]
        par_in, zeroed, pt_t, pt_ready, lam_exp = sem("par_in"), sem("zeroed"), sem("pt_t"), sem("pt_ready"), sem("lam_exp")
        wg_in, mm_done, evac, par_ready = sem("wg_in"), sem("mm_done"), sem("evac"), sem("par_ready")
        xc_ready, hc_ready, tr_done, tr_evac, tst_out = sem("xc_ready"), sem("hc_ready"), sem("tr_done"), sem("tr_evac"), sem("tst_out")
        tanh_ready, q1_ready, sqrt_ready, y_ready, y_out = sem("tanh_ready"), sem("q1_ready"), sem("sqrt_ready"), sem("y_ready"), sem("y_out")
        filled = sem("filled_yb")
        sp_passed = sem("sp_passed")
        steps, if_free, lam_ready = sem("p_steps"), sem("p_act"), sem("lam_ready")

        w_v = dram["w_in"].rearrange("o (k p) n -> p (o k) n", p=P)
        USES = 9
        U_X, U_V, U_R, U_I, U_X1, U_X2, U_G = 0, 1, (2, 4), (3, 5), 6, 7, 8
        tiles = [("x", 0, 0, U_X), ("v", 1024, 1, U_V), ("x1", 1536, 2, U_X1), ("x2", 2048, 0, U_X2), ("g", 512, 3, U_G)]
        gates = ["lru_wr_f", "lru_wi_f", "lru_wr_b", "lru_wi_b"]
        L_out = [dram["L"][w] for w in range(3)]
        FILLED = SEQ * 2 + LEAD * P
        FILL = (N_SLOTS - FILLED) // CT

        block = sem.begin()

        @block.sync
        def _(sp):
            rows = [("lru_conv_w", Q_CONV_W), ("lru_conv_b", Q_CONV_B), ("lru_br_f", 5), ("lru_bi_f", 6),
                    ("lru_br_b", 7), ("lru_bi_b", 8), ("lru_lambda_f", 9), ("lru_lambda_b", 10),
                    ("hy_conv_w", Q_HW), ("hy_conv_b", Q_HB), ("grp_norm_lru_g", Q_GA), ("grp_norm_hy_g", Q_GA + 1)]
            sp.wait_ge(zeroed, BASE + 1)
            for name, q in rows:
                a = dram[name]
                v = a.rearrange("o j (r p) -> (o j r) p", p=P) if len(a.shape) == 3 else a.rearrange("o (r p) -> (o r) p", p=P)
                sp.dma_start(prow[q * CT:q * CT + v.shape[0], :], v).then_inc(par_in, 16)

            def load_w(k, c):
                _, col, slot, _ = tiles[k]
                sp.dma_start(W[:, slot, :, :], w_v[:, :, ds(c * P + col, P)]).then_inc(w_in[k], 16)

            def load_gates(c):
                for g, name in enumerate(gates):
                    for h in range(2):
                        src = dram[name].rearrange("o h i j -> (o h) i j")[ds(c * 2 + h, 1), :, :]
                        sp.dma_start(WG[R * h:R * h + R, g, R * h:R * h + R], src.rearrange("a i j -> (a i) j")).then_inc(wg_in, 16)

            def mm_of(c, use):
                sp.wait_ge(mm_done, BASE + c * (4 * USES) + 4 * (use + 1))
                sp.sem_inc(sp_passed, 1)

            def store_tiles(c, which):
                sp.wait_ge(tr_evac, BASE + c * 12 + 4 * (which + 1) + 4)
                sp.sem_inc(sp_passed, 1)
                sp.dma_start(L_out[which][:, :, ds(c * P, P)], tst[:, :, :]).then_inc(tst_out, 16)

            for k in (0, 1, 2, 4):
                load_w(k, 0)
            load_gates(0)

            def fill(c):
                rows = dram["YB"][ds(c * FILL + FILLED, FILL), :]
                sp.dma_start(rows.rearrange("(p b) (a n) -> p (b a) n", p=P, n=256),
                             zero[:, :].unsqueeze(1).broadcast_to([P, FILL // P * 4, 256])).then_inc(filled, 16)

            def iteration(c, more):
                mm_of(c, U_X)
                load_w(3, c)
                fill(c)
                if more:
                    mm_of(c, U_V)
                    load_w(1, c + 1)
                    mm_of(c, U_I[1])
                    load_gates(c + 1)
                    mm_of(c, U_X1)
                    load_w(2, c + 1)
                store_tiles(c, 0)
                if more:
                    mm_of(c, U_X2)
                    load_w(0, c + 1)
                store_tiles(c, 1)
                if more:
                    mm_of(c, U_G)
                    load_w(4, c + 1)
                store_tiles(c, 2)
                sp.wait_ge(y_ready, BASE + c + 1)
                sp.dma_start(dram["YT"][:, :, ds(c, 1), :].rearrange("t p c n -> p t (c n)"),
                             T[1].rearrange("p (t n) -> p t n", n=P)).then_inc(y_out, 16)

            with sp.Fori(0, CT - 1) as c:
                iteration(c, True)
            iteration(CT - 1, False)
            sp.wait_ge(tst_out, BASE + 16 * 3 * CT)
            sp.wait_ge(y_out, BASE + 16 * CT)
            sp.wait_ge(filled, BASE + 16 * CT)

        @block.gpsimd
        def _(pool):
            pool.memset(prow[:, :], 0.0)
            pool.memset(zero[:, :], 0.0)
            pool.memset(WG[:, :, :], 0.0).then_inc(zeroed, 1)

        @block.tensor
        def _(pe):
            pe.wait_ge(par_in, BASE + 16 * 12)
            pe.transpose(tp[0][:, 0:P], prow[:, :], ident[:, :]).then_inc(pt_t, 1)
            pe.wait_ge(pt_ready, BASE + 1)

            def fill(c, use, lhs, rhs, n_k, need=None):
                for n in range(NCHUNK):
                    pe.wait_ge(evac, BASE + c * (4 * USES) + 4 * use + n + 1)
                    for k in range(n_k):
                        last = pe.matmul(pj[n][:, :], lhs(k), rhs(k, n), start=(k == 0), stop=(k == n_k - 1))
                    last.then_inc(mm_done, 1)

            def project(c, k):
                _, _, slot, use = tiles[k]
                pe.wait_ge(w_in[k], BASE + c * 16 + 16)
                fill(c, use, lambda j: W[:, slot, j, :], lambda j, n: hT[:, j, n * 512:(n + 1) * 512], KC)

            def transposes(c, which, slot):
                pe.wait_ge(hc_ready, BASE + c * 3 + which + 1)
                v = hc[:, slot, :].rearrange("p (q l) -> p l q", l=NT)
                for b in range(4):
                    pe.wait_ge(tr_evac, BASE + c * 12 + 4 * which + b + 1)
                    for q in range(4):
                        last = pe.transpose(tp[b][:, q * P:(q + 1) * P], v[:, 4 * b + q], ident[:, :])
                    last.then_inc(tr_done, 1)

            with pe.Fori(0, CT) as c:
                project(c, 0)
                project(c, 1)
                pe.wait_ge(xc_ready, BASE + c + 1)
                pe.wait_ge(wg_in, BASE + c * (16 * 8) + 16 * 8)
                for g in range(4):
                    fill(c, 2 + g, lambda j, g=g: WG[:, g, :], lambda j, n: xc[:, n * 512:(n + 1) * 512], 1)
                project(c, 2)
                transposes(c, 0, 0)
                project(c, 3)
                transposes(c, 1, 1)
                project(c, 4)
                transposes(c, 2, 0)

        @block.scalar
        def _(act):
            act.wait_ge(pt_ready, BASE + 1)
            act.activation(sp8[:, 0, :], sp8[:, 0, :], ACT.Exp, scale=-1.0).then_inc(lam_exp, 1)
            act.sem_inc(evac, 4)
            act.sem_inc(tr_evac, 4)
            act.wait_ge(lam_ready, BASE + 1)

            def evacuate(c, use, out, func=ACT.Copy, bias=None):
                for n in range(NCHUNK):
                    act.wait_ge(mm_done, BASE + c * (4 * USES) + 4 * use + n + 1)
                    if bias is None:
                        ins = act.activation(out(n), pj[n][:, :], func)
                    else:
                        ins = act.activation(out(n), pj[n][:, :], func, bias=bias)
                    ins.then_inc(evac, 1)

            def evacuate_transposes(c, which):
                act.wait_ge(tst_out, BASE + c * 48 + 16 * which)
                for b in range(4):
                    act.wait_ge(tr_done, BASE + c * 12 + 4 * which + b + 1)
                    act.activation(tst[:, 4 * b:4 * b + 4, :], tp[b].rearrange("p (t n) -> p t n", n=P), ACT.Copy).then_inc(tr_evac, 1)

            with act.Fori(0, CT) as c:
                act.wait_ge(xc_ready, BASE + c)
                evacuate(c, U_X, lambda n: xraw[:, 2 + 512 * n:2 + 512 * (n + 1)])
                act.wait_ge(hc_ready, BASE + c * 3)
                evacuate(c, U_V, lambda n: hraw[:, 0, 1 + 512 * n:1 + 512 * (n + 1)])
                act.wait_ge(par_ready, BASE + c + 1)
                act.wait_ge(y_ready, BASE + c)
                act.wait_ge(y_out, BASE + c * 16)
                for d in range(2):
                    evacuate(c, U_R[d], lambda n, d=d: T[d][:, 512 * n:512 * (n + 1)], ACT.Sigmoid, par[:, Q_BR[d]:Q_BR[d] + 1])
                    evacuate(c, U_I[d], lambda n, d=d: I[d][:, 512 * n:512 * (n + 1)], ACT.Sigmoid, par[:, Q_BI[d]:Q_BI[d] + 1])
                for d in range(2):
                    act.wait_ge(evac, BASE + c * (4 * USES) + 4 * (U_R[d] + 1) + 4)
                    act.activation(T[d][:, :], T[d][:, :], ACT.Tanh, scale=par[:, Q_LAM[d]:Q_LAM[d] + 1]).then_inc(tanh_ready, 1)
                for d in range(2):
                    act.wait_ge(q1_ready, BASE + c * 2 + d + 1)
                    act.activation(T[d][:, :], T[d][:, :], ACT.Sqrt).then_inc(sqrt_ready, 1)
                evacuate(c, U_X1, lambda n: hraw[:, 1, 1 + 512 * n:1 + 512 * (n + 1)])
                evacuate_transposes(c, 0)
                act.wait_ge(hc_ready, BASE + c * 3 + 1)
                evacuate(c, U_X2, lambda n: hraw[:, 0, 1 + 512 * n:1 + 512 * (n + 1)])
                evacuate_transposes(c, 1)
                act.wait_ge(q1_ready, BASE + c * 2 + 2)
                act.wait_ge(if_free, BASE + c + 1)
                evacuate(c, U_G, lambda n: G[:, 512 * n:512 * (n + 1)], ACT.Gelu_apprx_tanh)
                evacuate_transposes(c, 2)

        @block.vector
        def _(dve):
            step = Steps(dve, steps)
            dve.memset(xraw[:, :], 0.0)
            dve.memset(hraw[:, :, :], 0.0)
            dve.wait_ge(pt_t, BASE + 1)
            step(dve.tensor_copy(PT[:, :, :].rearrange("p q c -> p (q c)"), tp[0][:, 0:N_Q * CT]))
            lam = PT[:, Q_LAM[0]:Q_LAM[1] + 1, :].rearrange("p q c -> p (q c)")
            step(dve.tensor_scalar(sp8[:, 1, :], lam, -1.0, 0.0, ALU.mult, ALU.max))
            step(dve.tensor_scalar(sp8[:, 2, :], lam, 0.0, None, ALU.max))
            dve.tensor_tensor(sp8[:, 0, :], sp8[:, 1, :], sp8[:, 2, :], ALU.add).then_inc(pt_ready, 1)
            dve.wait_ge(lam_exp, BASE + 1)
            step(dve.tensor_scalar(sp8[:, 2, :], sp8[:, 0, :], 2.0, None, ALU.add))
            step(dve.reciprocal(sp8[:, 3, :], sp8[:, 2, :]))
            step(dve.tensor_tensor(sp8[:, 2, :], sp8[:, 0, :], sp8[:, 3, :], ALU.mult))
            step(dve.tensor_tensor(sp8[:, 3, :], sp8[:, 2, :], sp8[:, 2, :], ALU.mult))
            step(dve.memset(sp8[:, 4, :], 1.0 / 17))
            for odd in range(15, 0, -2):
                step(dve.tensor_tensor(sp8[:, 4, :], sp8[:, 4, :], sp8[:, 3, :], ALU.mult))
                step(dve.tensor_scalar(sp8[:, 4, :], sp8[:, 4, :], 1.0 / odd, None, ALU.add))
            step(dve.tensor_tensor(sp8[:, 4, :], sp8[:, 4, :], sp8[:, 2, :], ALU.mult))
            step(dve.scalar_tensor_tensor(out=sp8[:, 4, :], in0=sp8[:, 4, :], scalar=2.0, in1=sp8[:, 1, :], op0=ALU.mult, op1=ALU.add))
            step(dve.tensor_scalar(lam, sp8[:, 4, :], 4.0, None, ALU.mult))
            dve.tensor_copy(dram["gAB"][:, :, :], PT[:, Q_GA:Q_GA + 2, :]).then_inc(lam_ready, 1)
            PER_C = 22

            def conv(step, out, raw, taps, q_w, stride, q_b, done):
                step(dve.tensor_scalar(out, raw[:, 0:SEQ], par[:, q_w:q_w + 1], par[:, q_b:q_b + 1], ALU.mult, ALU.add))
                for j in range(1, taps):
                    q = q_w + j * stride
                    ins = dve.scalar_tensor_tensor(out=out, in0=raw[:, j:j + SEQ], scalar=par[:, q:q + 1], in1=out,
                                                   op0=ALU.mult, op1=ALU.add)
                    if j < taps - 1:
                        step(ins)
                ins.then_inc(done, 1)

            with dve.Fori(0, CT) as c:
                step = Steps(dve, steps, c * PER_C + 27)
                dve.wait_ge(hc_ready, BASE + c * 3)
                dve.tensor_copy(par[:, :], PT[:, :, ds(c, 1)].rearrange("p q c -> p (q c)")).then_inc(par_ready, 1)
                dve.wait_ge(par_ready, BASE + c + 1)

                def hyena_conv(which, slot, use):
                    dve.wait_ge(evac, BASE + c * (4 * USES) + 4 * (use + 1) + 4)
                    dve.wait_ge(tr_done, BASE + c * 12 + (4 if which == 2 else 0))
                    conv(step, hc[:, slot, :], hraw[:, slot, :], 3, Q_HW + which, 3, Q_HB + which, hc_ready)

                def lru(d):
                    step(dve.reciprocal(Q[d][:, :], Q[d][:, :]))
                    step(dve.tensor_tensor(I[d][:, :], I[d][:, :], xc[:, :], ALU.mult))
                    step(dve.tensor_tensor(I[d][:, :], I[d][:, :], Q[d][:, :], ALU.mult))
                    dve.wait_ge(sqrt_ready, BASE + c * 2 + d + 1)
                    step(dve.scalar_tensor_tensor(out=I[d][:, :], in0=T[d][:, :], scalar=2.0, in1=I[d][:, :], op0=ALU.mult, op1=ALU.mult))
                    step(dve.tensor_scalar(Q[d][:, :], Q[d][:, :], 2.0, -1.0, ALU.mult, ALU.add))
                    o = slice(None, None, -1) if d else slice(None)
                    step(dve.tensor_tensor_scan(T[d][:, o], Q[d][:, o], I[d][:, o], 0.0, ALU.mult, ALU.add))

                dve.wait_ge(evac, BASE + c * (4 * USES) + 8)
                conv(step, xc[:, :], xraw, 4, Q_CONV_W, 1, Q_CONV_B, xc_ready)
                hyena_conv(0, 0, U_V)
                for d in range(2):
                    dve.wait_ge(tanh_ready, BASE + c * 2 + d + 1)
                    dve.tensor_scalar(Q[d][:, :], T[d][:, :], 1.0, None, ALU.add).then_inc(q1_ready, 1)
                dve.wait_ge(xc_ready, BASE + c + 1)
                dve.wait_ge(q1_ready, BASE + c * 2 + 2)
                lru(0)
                dve.sem_inc(if_free, 1)
                hyena_conv(1, 1, U_X1)
                lru(1)
                step(dve.tensor_tensor(T[0][:, :], T[0][:, :], T[1][:, :], ALU.add))
                hyena_conv(2, 0, U_X2)
                dve.wait_ge(evac, BASE + c * (4 * USES) + 4 * (U_G + 1) + 4)
                dve.tensor_tensor(T[1].rearrange("p (l q) -> p q l", q=P), T[0].rearrange("p (q l) -> p q l", l=NT),
                                  G.rearrange("p (q l) -> p q l", l=NT), ALU.mult).then_inc(y_ready, 1)
                n_steps = step.n
            assert n_steps == PER_C, n_steps

def filters(nc, dram, invn, cur):
    L = R // 2
    with ExitStack() as ctx:
        sb = lambda name, shape, dt=F32: ctx.enter_context(nc.sbuf_tensor(name, shape, dt))
        sem = PhaseSemaphores(nc, ctx)
        w3 = sb("w3", [P, 2, 512])
        fa = sb("fa", [P, P])
        ones = sb("ones", [P, P])
        zz = sb("zz", [P, SEQ])
        zb = sb("zb", [P, 4, P])
        mask = sb("mask", [P, 2, R])
        dec = sb("dec", [P, 4, 512])
        kt = sb("kt", [P, 4, 2, 512])
        acc = sb("acc", [P, 2, 512])
        ka = sb("ka", [P, 2, 2, 512])
        kst = sb("kst", [P, 2, 2, 2, 512])
        pk = [[ctx.enter_context(nc.psum_tensor(f"pk{s}{o}", [P, 512], F32)) for o in range(2)] for s in range(2)]
        pa = [[ctx.enter_context(nc.psum_tensor(f"pa{s}{o}", [P, 512], F32)) for o in range(2)] for s in range(2)]
        par_in = sem("f_in")
        steps, dec_in, zb_ready, kgen, k_ready = sem("f_steps"), [sem(f"dec_in{s}") for s in range(4)], sem("zb_ready"), sem("kgen"), sem("k_ready")
        fa_done, kst_ready, kst_out, norm_mm, inv_ready = sem("fa_done"), sem("kst_ready"), [sem(f"kst_out{i}") for i in range(2)], sem("norm_mm"), sem("inv_ready")
        summed, mask_ready, abs_ready = sem("summed"), sem("mask_ready"), sem("abs_ready")
        cur_in = sem("cur_in")
        N_PAR = 4
        block = sem.begin()

        @block.sync
        def _(sp):
            load = lambda dst, src: sp.dma_start(dst, src).then_inc(par_in, 16)
            load(zz[:, :], dram["ZZ"])
            for h in range(2):
                load(w3[R * h:R * h + R, :, :], dram["hy_filt_w3"].rearrange("o i (d r c) -> (o i) d r c", d=2, r=2)[:, h])
            load(fa[:, :], dram["fa_filter"])
            with sp.Fori(0, L // 4) as it:
                for s in range(4):
                    sp.wait_ge(k_ready, BASE + it * 8 + 2 * s - 6)
                    sp.dma_start(dec[:, s, :], dram["decay"][:, ds(it * 4 + s, 1), :].rearrange("p a c -> p (a c)")).then_inc(dec_in[s], 16)
                sp.dma_start(cur[:, ds(it * 2, 2), :], dram["L"][0][:, ds(it * 2, 2), :]).then_inc(cur_in, 16)
            sp.wait_ge(cur_in, BASE + 16 * (L // 4))

        @block.gpsimd
        def _(pool):
            pool.memset(ones[:, :], 1.0)
            pool.wait_ge(par_in, BASE + 16 * N_PAR)
            pool.wait_ge(mask_ready, BASE + 1)
            pool.memset(acc[:, :, :], 0.0).then_inc(summed, 1)
            view = zz.rearrange("p (q l) -> p l q", l=L)

            def spread(j, s):
                pool.wait_ge(kgen, BASE + j * 2 - 6)
                pool.tensor_tensor(zb[:, s % 4, :].rearrange("p (h q) -> p h q", h=2),
                                   view[:, ds(j, 1), :].broadcast_to([P, 2, R]), mask[:, :, :], ALU.mult).then_inc(zb_ready, 1)

            def add_up(j, s):
                for o in range(2):
                    pool.wait_ge(abs_ready, BASE + j * 2 + o + 1)
                    pool.wait_ge(summed, BASE + j * 2 + 1)
                    pool.tensor_tensor(acc[:, o, :], acc[:, o, :], ka[:, s % 2, o, :], ALU.add).then_inc(summed, 1)

            spread(0, 0)
            spread(1, 1)
            with pool.Fori(0, L // 4 - 1) as it:
                for s in range(4):
                    spread(it * 4 + s + 2, s + 2)
                    add_up(it * 4 + s, s)
            for s in range(4):
                if s < 2:
                    spread(L - 4 + s + 2, s + 2)
                add_up(L - 4 + s, s)

        @block.tensor
        def _(pe):
            pe.wait_ge(par_in, BASE + 16 * N_PAR)
            def generate(j, s):
                pe.wait_ge(zb_ready, BASE + j + 1)
                pe.wait_ge(k_ready, BASE + j * 2 - 2)
                for o in range(2):
                    pe.matmul(pk[s % 2][o][:, :], zb[:, s % 4, :], w3[:, o, :], start=True, stop=True).then_inc(kgen, 1)

            def transform(j, s):
                for o in range(2):
                    pe.wait_ge(k_ready, BASE + j * 2 + o + 1)
                    pe.wait_ge(kst_ready, BASE + j * 2 + o - 3)
                    pe.matmul(pa[s % 2][o][:, :], fa[:, :], kt[:, s, o, :], start=True, stop=True).then_inc(fa_done, 1)

            generate(0, 0)
            with pe.Fori(0, L // 4 - 1) as it:
                for s in range(4):
                    generate(it * 4 + s + 1, s + 1)
                    transform(it * 4 + s, s)
            for s in range(4):
                if s < 3:
                    generate(L - 4 + s + 1, s + 1)
                transform(L - 4 + s, s)
            pe.wait_ge(summed, BASE + 1 + 8 * (L // 4))
            for o in range(2):
                last = pe.matmul(pk[0][o][:, :], ones[:, :], acc[:, o, :], start=True, stop=True)
            last.then_inc(norm_mm, 1)

        @block.scalar
        def _(act):
            with act.Fori(0, L // 4) as it:
                for pair in range(2):
                    act.wait_ge(kst_out[pair], BASE + it * (16 * 2))
                    for s in (2 * pair, 2 * pair + 1):
                        for o in range(2):
                            act.wait_ge(fa_done, BASE + it * 8 + 2 * s + o + 1)
                            act.activation(kst[:, pair, o, s % 2, :], pa[s % 2][o][:, :], ACT.Copy).then_inc(kst_ready, 1)
                    act.wait_ge(kst_ready, BASE + it * 8 + 4 * pair + 4)
                    for o in range(2):
                        act.dma_start(dram["KA"][o][:, ds(it * 4 + 2 * pair, 2), :], kst[:, pair, o, :, :]).then_inc(kst_out[pair], 16)
            for pair in range(2):
                act.wait_ge(kst_out[pair], BASE + 16 * 2 * (L // 4))

        @block.vector
        def _(dve):
            step = Steps(dve, steps)

            step(dve.memset(mask[:, :, :], 0.0))
            for h in range(2):
                last = dve.memset(mask[R * h:R * h + R, h, :], 1.0)
            last.then_inc(mask_ready, 1)
            with dve.Fori(0, L // 4) as it:
                for s in range(4):
                    dve.wait_ge(dec_in[s], BASE + it * 16 + 16)
                    for o in range(2):
                        dve.wait_ge(kgen, BASE + it * 8 + 2 * s + o + 1)
                        dve.wait_ge(fa_done, BASE + it * 8 + 2 * s + o - 7)
                        dve.tensor_tensor(kt[:, s, o, :], pk[s % 2][o][:, :], dec[:, s, :], ALU.mult).then_inc(k_ready, 1)
                        dve.wait_ge(k_ready, BASE + it * 8 + 2 * s + o + 1)
                        dve.wait_ge(summed, BASE + it * 8 + 2 * s + o - 2)
                        dve.scalar_tensor_tensor(out=ka[:, s % 2, o, :], in0=kt[:, s, o, :], scalar=-1.0, in1=kt[:, s, o, :],
                                                 op0=ALU.mult, op1=ALU.max).then_inc(abs_ready, 1)
            dve.wait_ge(norm_mm, BASE + 1)
            for o in range(2):
                step(dve.tensor_scalar(acc[:, o, :], pk[0][o][:, :], EPS, None, ALU.add))
            dve.reciprocal(invn[:, :, :], acc[:, :, :]).then_inc(inv_ready, 1)


def conv_forward(nc, dram, o, cur, skip, stage):
    with ExitStack() as ctx:
        sb = lambda name, shape, dt=F32: ctx.enter_context(nc.sbuf_tensor(f"{name}_{o}", shape, dt))
        sem = PhaseSemaphores(nc, ctx, f"_a{o}")
        fa = sb("faz", [P, 2, P])
        pa = [[ctx.enter_context(nc.psum_tensor(f"za_{o}_{s}{h}", [P, 512], F32)) for h in range(2)] for s in range(4)]
        fa_in, skip_in, mm, evac, stored = sem("fa_in"), sem("skip_in"), sem("mm"), sem("evac"), sem("stored")
        block = sem.begin()

        @block.sync
        def _(sp):
            sp.dma_start(fa[:, :, :], dram["fa_signal"]).then_inc(fa_in, 16)
            sp.dma_start(skip[:, :], dram["hy_skip"].rearrange("a o c -> (a o) c")[o].partition_broadcast(P)).then_inc(skip_in, 16)

        @block.tensor
        def _(pe):
            pe.wait_ge(fa_in, BASE + 16)
            with pe.Fori(0, NT // 4) as it:
                for s in range(4):
                    for h in range(2):
                        pe.wait_ge(evac, BASE + it * 8 + 2 * s + h - 7)
                        pe.matmul(pa[s][h][:, :], fa[:, h, :], cur[:, ds(it * 4 + s, 1), :].rearrange("p a c -> p (a c)"),
                                  start=True, stop=True).then_inc(mm, 1)

        @block.scalar
        def _(act):
            with act.Fori(0, NT // 4) as it:
                for s in range(4):
                    for h in range(2):
                        act.wait_ge(mm, BASE + it * 8 + 2 * s + h + 1)
                        act.activation(stage[:, h, ds(it * 4 + s, 1), :].rearrange("p a c -> p (a c)"), pa[s][h][:, :], ACT.Copy).then_inc(evac, 1)
                act.wait_ge(evac, BASE + it * 8 + 8)
                four = lambda a: a[:, :, ds(it * 4, 4), :].rearrange("p h l c -> p h (l c)")
                act.dma_start(four(dram["SA"]), four(stage)).then_inc(stored, 16)
            act.wait_ge(stored, BASE + 16 * (NT // 4))

        @block.gpsimd
        def _(pool):
            pool.wait_ge(skip_in, BASE + 16)
            with pool.Fori(0, NT) as t:
                pool.wait_ge(mm, BASE + t * 2 + 2)
                tile = cur[:, ds(t, 1), :].rearrange("p a c -> p (a c)")
                pool.tensor_tensor(tile, tile, skip[:, :], ALU.mult)


def conv_blocks(nc, dram, o, gate):
    with ExitStack() as ctx:
        sb = lambda name, shape, dt=F32: ctx.enter_context(nc.sbuf_tensor(f"{name}_{o}", shape, dt))
        sem = PhaseSemaphores(nc, ctx, f"_b{o}")
        mats = sb("mats", [P, 4, 5, P])
        zin, kin, qo = sb("zin", [P, 4, 512]), sb("kin", [P, 4, 512]), sb("qo", [P, 4, 512])
        zs, u, v = sb("zs", [P, 2, 512]), sb("u", [P, 2, 512]), sb("v", [P, 2, 512])
        bank = lambda name: [ctx.enter_context(nc.psum_tensor(f"{name}_{o}_{i}", [P, 512], F32)) for i in range(2)]
        pz, pr, pi, pq = bank("pz"), bank("pr"), bank("pi"), bank("pq")
        landed = [sem(f"landed{s}") for s in range(4)]
        fwd, zs_ready, uv_ready, inv, q_evac = sem("fwd"), sem("zs_ready"), sem("uv_ready"), sem("inv"), sem("q_evac")
        stored = [sem(f"stored{s}") for s in range(4)]
        gate_in = sem("gate_in")
        SA, SI = (dram[n].rearrange("(j q) h l c -> j (q h l) c", q=4) for n in ("SA", "SI"))
        KA = dram["KA"][o].rearrange("(j q) l c -> j (q l) c", q=4)
        block = sem.begin()

        @block.sync
        def _(sp):
            with sp.Fori(0, HALF // 4) as it:
                for s in range(4):
                    j = it * 4 + s
                    sp.wait_ge(inv, BASE + it * 4 + s - 3)
                    sp.dma_start(mats[:, s, :, :], dram["mats"][ds(j, 1)].rearrange("a p m n -> (a p) m n")).then_inc(landed[s], 16)
                    for dst, src in ((zin, SA), (kin, KA)):
                        sp.dma_start(dst[:, s, :], src[ds(j, 1)].rearrange("a n c -> (a n) c")).then_inc(landed[s], 16)
                sp.dma_start(gate[:, ds(it * 2, 2), :], dram["L"][1 + o][:, ds(it * 2, 2), :]).then_inc(gate_in, 16)
            sp.wait_ge(gate_in, BASE + 16 * (HALF // 4))

        @block.tensor
        def _(pe):
            with pe.Fori(0, HALF // 4) as it:
                def forward(s):
                    pe.wait_ge(landed[s], BASE + it * 48 + 48)
                    pe.wait_ge(zs_ready, BASE + it * 4 + s - 1)
                    pe.wait_ge(uv_ready, BASE + it * 8 + 2 * s - 2)
                    for bank_, m, rhs in ((pz, 0, zin), (pr, 1, kin), (pi, 2, kin)):
                        pe.matmul(bank_[s % 2][:, :], mats[:, s, m, :], rhs[:, s, :], start=True, stop=True).then_inc(fwd, 1)

                def inverse(s):
                    pe.wait_ge(uv_ready, BASE + it * 8 + 2 * s + 2)
                    pe.wait_ge(q_evac, BASE + it * 4 + s - 1)
                    pe.matmul(pq[s % 2][:, :], mats[:, s, 3, :], u[:, s % 2, :], start=True, stop=False)
                    pe.matmul(pq[s % 2][:, :], mats[:, s, 4, :], v[:, s % 2, :], start=False, stop=True).then_inc(inv, 1)

                forward(0)
                for s in range(1, 4):
                    forward(s)
                    inverse(s - 1)
                inverse(3)

        @block.scalar
        def _(act):
            with act.Fori(0, HALF // 4) as it:
                def signal(s):
                    act.wait_ge(fwd, BASE + it * 12 + 3 * s + 1)
                    act.wait_ge(uv_ready, BASE + it * 8 + 2 * s - 2)
                    act.activation(zs[:, s % 2, :], pz[s % 2][:, :], ACT.Copy).then_inc(zs_ready, 1)

                def result(s):
                    act.wait_ge(stored[s], BASE + it * 16)
                    act.wait_ge(inv, BASE + it * 4 + s + 1)
                    act.activation(qo[:, s, :], pq[s % 2][:, :], ACT.Copy).then_inc(q_evac, 1)
                    act.wait_ge(q_evac, BASE + it * 4 + s + 1)
                    act.dma_start(SI[ds(it * 4 + s, 1)].rearrange("a n c -> (a n) c"), qo[:, s, :]).then_inc(stored[s], 16)

                signal(0)
                for s in range(1, 4):
                    signal(s)
                    result(s - 1)
                result(3)
            for s in range(4):
                act.wait_ge(stored[s], BASE + 16 * (HALF // 4))

        @block.vector
        def _(dve):
            with dve.Fori(0, HALF // 4) as it:
                for s in range(4):
                    dve.wait_ge(zs_ready, BASE + it * 4 + s + 1)
                    dve.wait_ge(inv, BASE + it * 4 + s - 1)
                    for n, (dst, src) in enumerate(((u, pr), (v, pi))):
                        dve.wait_ge(fwd, BASE + it * 12 + 3 * s + 2 + n)
                        dve.tensor_tensor(dst[:, s % 2, :], src[s % 2][:, :], zs[:, s % 2, :], ALU.mult).then_inc(uv_ready, 1)


def conv_inverse(nc, dram, o, cur, stage, gate, invn, rB, ident):
    with ExitStack() as ctx:
        sb = lambda name, shape, dt=F32: ctx.enter_context(nc.sbuf_tensor(f"{name}_{o}", shape, dt))
        sem = PhaseSemaphores(nc, ctx, f"_c{o}")
        ia = sb("ia", [P, 2, P])
        y = sb("y", [P, 4, 512])
        junk = sb("junkz", [P, 512])
        ssq = sb("ssqz", [P, NT])
        zn = sb("zn", [P, 4, 512])
        zt = sb("zt", [P, 2, 512])
        pq = [ctx.enter_context(nc.psum_tensor(f"py_{o}_{s}", [P, 512], F32)) for s in range(4)]
        tp = [ctx.enter_context(nc.psum_tensor(f"pt_{o}_{s}", [P, 512], F32)) for s in range(2)]
        ia_in, landed, mm, scaled, added, gated = sem("ia_in"), [sem(f"landed{s}") for s in range(4)], sem("mm"), sem("scaled"), sem("added"), sem("gated")
        squared, ms, tr, zt_ready = sem("squared"), sem("ms"), sem("tr"), sem("zt_ready")
        stored = [sem(f"stored{s}") for s in range(2)]
        tile = lambda t, a=cur: a[:, ds(t, 1), :].rearrange("p a c -> p (a c)")
        block = sem.begin()

        @block.sync
        def _(sp):
            sp.dma_start(ia[:, :, :], dram["inv_a"]).then_inc(ia_in, 16)
            for g in range(4):
                four = lambda a: a[:, :, 4 * g:4 * g + 4, :].rearrange("p h l c -> p h (l c)")
                sp.dma_start(four(stage), four(dram["SI"])).then_inc(landed[g], 16)

        @block.tensor
        def _(pe):
            pe.wait_ge(ia_in, BASE + 16)

            def product(t):
                pe.wait_ge(landed[t // 4], BASE + 16)
                pe.wait_ge(scaled, BASE + t - 3)
                pe.matmul(pq[t % 4][:, :], ia[:, 0, :], stage[:, 0, t, :], start=True, stop=False)
                pe.matmul(pq[t % 4][:, :], ia[:, 1, :], stage[:, 1, t, :], start=False, stop=True).then_inc(mm, 1)

            def transposes(t, s):
                pe.wait_ge(gated, BASE + t + 1)
                pe.wait_ge(zt_ready, BASE + t - 1)
                for q in range(4):
                    last = pe.transpose(tp[s % 2][:, q * P:(q + 1) * P], zn[:, s, q * P:(q + 1) * P], ident[:, :])
                last.then_inc(tr, 1)

            LAG = 3
            for t in range(NT + LAG):
                if t < NT:
                    product(t)
                if o == 1 and t >= LAG:
                    transposes(t - LAG, (t - LAG) % 4)

        @block.gpsimd
        def _(pool):
            with pool.Fori(0, NT // 4) as it:
                for s in range(4):
                    pool.wait_ge(scaled, BASE + it * 4 + s + 1)
                    pool.tensor_tensor(y[:, s, :], y[:, s, :], tile(it * 4 + s), ALU.add).then_inc(added, 1)

        @block.vector
        def _(dve):
            def scale(t, s):
                dve.wait_ge(mm, BASE + t + 1)
                dve.wait_ge(gated, BASE + t - 3)
                dve.tensor_tensor(y[:, s % 4, :], pq[s % 4][:, :], invn[:, o, :], ALU.mult).then_inc(scaled, 1)

            def apply_gate(t, s):
                dve.wait_ge(added, BASE + t + 1)
                if o == 1:
                    dve.wait_ge(tr, BASE + t - 3)
                    dve.wait_ge(squared, BASE + t - 3)
                dve.tensor_tensor(zn[:, s, :] if o == 1 else tile(t), y[:, s, :], tile(t, gate), ALU.mult).then_inc(gated, 1)

            scale(0, 0)
            scale(1, 1)
            with dve.Fori(0, NT // 4 - 1) as it:
                for s in range(4):
                    scale(it * 4 + s + 2, s + 2)
                    apply_gate(it * 4 + s, s)
            for s in range(4):
                if s < 2:
                    scale(NT - 2 + s, s + 2)
                apply_gate(NT - 4 + s, s)
            if o == 1:
                dve.wait_ge(squared, BASE + NT)
                dve.tensor_scalar(ssq[:, :], ssq[:, :], 1.0 / CH, EPS, ALU.mult, ALU.add).then_inc(ms, 1)
                dve.wait_ge(ms, BASE + 1)
                dve.reciprocal(rB[:, :], ssq[:, :]).then_inc(ms, 1)

        if o == 1:
            @block.scalar
            def _(act):
                with act.Fori(0, NT // 4) as it:
                    for q in range(4):
                        t, s = it * 4 + q, q % 2
                        act.wait_ge(gated, BASE + t + 1)
                        act.wait_ge(squared, BASE + t)
                        act.activation(junk[:, :], zn[:, q, :], ACT.Square, accum_out=ssq[:, ds(t, 1)]).then_inc(squared, 1)
                        act.wait_ge(tr, BASE + t + 1)
                        act.wait_ge(stored[s], BASE + (t - s) * 8)
                        act.activation(zt[:, s, :], tp[s][:, :], ACT.Copy).then_inc(zt_ready, 1)
                        act.wait_ge(zt_ready, BASE + t + 1)
                        act.dma_start(dram["YT"][ds(t, 1), :, 4:8, :].rearrange("a p c n -> (a p) (c n)"), zt[:, s, :]).then_inc(stored[s], 16)
                act.wait_ge(ms, BASE + 2)
                act.activation(rB[:, :], rB[:, :], ACT.Sqrt)
                for s in range(2):
                    act.wait_ge(stored[s], BASE + 16 * (NT // 2))


def transform_tables():
    n = np.arange
    th1 = 2 * np.pi * np.outer(n(R), n(HALF + 1)) / R
    F = np.zeros((R, R))
    F[:, 0:HALF + 1] = np.cos(th1)
    F[:, HALF + 1:] = -np.sin(th1[:, 1:HALF])
    fa_filter = np.zeros((R, 2, 2, R))
    for g in range(2):
        fa_filter[:, g, g] = F
    fa_signal = np.zeros((HALF, 4, 2, 2, R))
    inv_a = np.zeros((2, R, 2, HALF, 4))
    G = np.zeros((R, HALF))
    n1 = n(HALF)
    G[0], G[HALF] = 1, (-1.0) ** n1
    for j in range(1, HALF):
        G[j], G[HALF + j] = 2 * np.cos(2 * np.pi * n1 * j / R), -2 * np.sin(2 * np.pi * n1 * j / R)
    for h in range(2):
        for g2 in range(2):
            fa_signal[:, 2 * h + g2, h, g2] = F[:HALF]
            inv_a[g2, :, h, :, 2 * h + g2] = G / N
    n2 = n(R)
    B, Inv = np.zeros((HALF, 2, R, 2, R)), np.zeros((HALF, 2, R, 2, R))
    for j in range(1, HALF):
        th = 2 * np.pi * np.outer(n2, j + R * n(R)) / N
        B[j, 0, :, 0], B[j, 1, :, 0], B[j, 0, :, 1], B[j, 1, :, 1] = np.cos(th), np.sin(th), -np.sin(th), np.cos(th)
        Inv[j, 0, :, 0], Inv[j, 1, :, 0], Inv[j, 0, :, 1], Inv[j, 1, :, 1] = np.cos(th).T, -np.sin(th).T, np.sin(th).T, np.cos(th).T
    for s in range(R - 1):
        part, k = (1, HALF + R * s) if s < HALF else (0, R * (s - HALF + 1))
        th = 2 * np.pi * n2 * k / N
        B[0, part, :, 0, s], B[0, part, :, 1, s] = np.cos(th), -np.sin(th)
        Inv[0, 0, s, part], Inv[0, 1, s, part] = 2 * np.cos(th), -2 * np.sin(th)
    B[0, 0, :, 0, R - 1], B[0, 0, :, 1, R - 1] = 1, (-1.0) ** n2
    Inv[0, 0, R - 1, 0], Inv[0, 1, R - 1, 0] = 1, (-1.0) ** n2
    Kr, Ki = B.copy(), B.copy()
    Kr[:, :, :, 1], Ki[:, :, :, 0] = B[:, :, :, 0], B[:, :, :, 1]
    Kr[0, :, :, 1, R - 1], Ki[0, :, :, :, R - 1] = B[0, :, :, 1, R - 1], 0
    InvV = np.zeros_like(Inv)
    InvV[:, 0], InvV[:, 1] = Inv[:, 1], -Inv[:, 0]
    InvV[0, :, R - 1] = 0
    f = np.float32
    pos, t = n(SEQ, dtype=f), np.linspace(0, 1, SEQ, dtype=f)
    bands = np.linspace(1e-4, 15, 16, dtype=f)
    ang = (f(2 * math.pi / SEQ) * pos)[:, None] * bands
    feats = np.concatenate([t[:, None], np.cos(ang), np.sin(ang)], -1).T
    deltas = np.abs(np.linspace(math.log(1e-2) / 1.5, math.log(1e-2) / 0.3, CH, dtype=f))
    back = np.concatenate([np.zeros(1, f), t[1:][::-1]])
    decay = np.exp(-np.concatenate([t, back])[:, None] * deltas).reshape(P, R // 2, CH)
    kk = n(R).reshape(2, HALF).T.reshape(-1)
    fa_filter, fa_signal = fa_filter[..., kk].swapaxes(-1, -2), fa_signal[..., kk].swapaxes(-1, -2)
    inv_a = inv_a[:, kk].swapaxes(0, 1)
    ghl = n(R).reshape(2, 2, 16).swapaxes(0, 1).reshape(-1)
    B, Inv, InvV = B[:, :, ghl], Inv[..., ghl], InvV[..., ghl]
    mats = np.stack([m.reshape(HALF, P, P) for m in (B, Kr, Ki, Inv, InvV)], 2)
    out = dict(fa_filter=fa_filter.reshape(P, P), fa_signal=fa_signal.reshape(P, 2, P), inv_a=inv_a.reshape(P, 2, P),
               mats=mats, feats=feats, decay=decay, ident=np.eye(P))
    return {k: np.ascontiguousarray(v, dtype=f) for k, v in out.items()}


def output_projection(nc, dram, LG, gAB, rB, ident):
    NL = N_GROUPS + N_EXP
    with ExitStack() as ctx:
        sb = lambda name, shape, dt=F32: ctx.enter_context(nc.sbuf_tensor(name, shape, dt))
        sem = PhaseSemaphores(nc, ctx)
        wo_hi, wo_lo = sb("wo_hi", [P, KC, D], F32R), sb("wo_lo", [P, KC, D], F32R)
        wo = sb("wo", [P, KC, D])
        X2 = sb("X2", [P, 4, D])
        rw = sb("rw", [P, KC, P])
        rb = sb("rb", [P, NL])
        gain = sb("gain_ffn", [P, D])
        ones = sb("ones5", [P, P])
        yt = sb("yt", [P, 4, KC, P])
        y_hi, y_lo = sb("y_hi", [P, 2, KC, P], F32R), sb("y_lo", [P, 2, KC, P], F32R)
        xt = sb("xt", [P, 2, D])
        sq = sb("sq", [P, 2, 512])
        h = sb("h", [P, 2, D])
        hT = sb("hT5", [P, KC, P])
        junk = sb("junk5", [P, D])
        st = sb("st5", [P, 2, 8])
        bank = lambda name: ctx.enter_context(nc.psum_tensor(name, [P, 512], F32))
        pA, pB, pt = [bank("pA0"), bank("pA1")], [bank("pB0"), bank("pB1")], [bank("ph0"), bank("ph1")]
        pl, psq = bank("pl"), bank("psq")
        w_in_, rw_zero, w_ready = sem("par5_in"), sem("rw_zero"), sem("wo_ready")
        y_in, x_in = [sem(f"y_in{s}") for s in range(4)], [sem(f"x5_in{s}") for s in range(2)]
        sq_ready, sum1, sum2, ssq_mm, rA_ms, rA_ready = sem("sq_ready"), sem("sum1"), sem("sum2"), sem("ssq_mm"), sem("rA_ms"), sem("rA_ready")
        projA, projB, xa_ready, x2_ready = sem("projA"), sem("projB"), sem("xa_ready"), sem("x2_ready")
        s2_ready, ms2, rs2, h_ready, tr, hT_ready, lg_mm, lg_ready = (sem(n) for n in ("s2_ready", "ms2", "rs2", "h_ready", "tr5", "hT_ready", "lg_mm", "lg_ready"))
        h_out = [sem(f"h_out{s}") for s in range(2)]
        x2_out = [sem(f"x2_out{q}") for q in range(4)]
        wo_in = [sem(f"wo_in{c}") for c in range(KC // 2)]
        w_rounded, y_rounded, y_split = sem("w_rounded"), sem("y_rounded"), sem("y_split")
        rA_first, ms2_first = sem("rA_first"), sem("ms2_first")
        N_W = 5

        def in_rounds(eng, step):
            for q in range(4):
                step(q, q, behind=q)
            with eng.Fori(1, NT // 4 - 1) as it:
                for q in range(4):
                    step(it * 4 + q, q)
            for q in range(4):
                step(NT - 4 + q, q, ahead=q < 3)

        x_t = dram["x"].rearrange("o (p l) d -> l p (o d)", l=NT)
        block = sem.begin()

        @block.sync
        def _(sp):
            load = lambda dst, src: sp.dma_start(dst, src).then_inc(w_in_, 16)
            w_out = dram["w_out"].rearrange("o (k p) n -> p (o k) n", p=P)
            for c in range(KC // 2):
                sp.dma_start(wo[:, 2 * c:2 * c + 2, :], w_out[:, 2 * c:2 * c + 2, :]).then_inc(wo_in[c], 16)
            for s in range(4):
                sp.dma_start(yt[:, s, :, :], dram["YT"][s]).then_inc(y_in[s], 16)
                if s < 2:
                    sp.dma_start(xt[:, s, :], x_t[s]).then_inc(x_in[s], 16)
            sp.wait_ge(rw_zero, BASE + 1)
            load(rw[:, :, 0:N_GROUPS], dram["router_group_w"].rearrange("o (k p) n -> p (o k) n", p=P))
            load(rw[:, :, N_GROUPS:NL], dram["router_expert_w"].rearrange("o (k p) n -> p (o k) n", p=P))
            load(rb[:, 0:N_GROUPS], dram["router_group_b"].rearrange("o d -> (o d)").partition_broadcast(P))
            load(rb[:, N_GROUPS:NL], dram["router_expert_b"].rearrange("o d -> (o d)").partition_broadcast(P))
            load(gain[:, :], dram["norm_ffn_g"].rearrange("o d -> (o d)").partition_broadcast(P))
            for s in (2, 3):
                sp.wait_ge(x2_ready, BASE + 2 * s - 2)
                sp.dma_start(xt[:, s % 2, :], x_t[s]).then_inc(x_in[s % 2], 16)
            with sp.Fori(1, NT // 4) as it:
                for s in range(4):
                    sp.wait_ge(x2_ready, BASE + it * 8 + 2 * s - 6)
                    sp.dma_start(yt[:, s, :, :], dram["YT"][ds(it * 4 + s, 1)].rearrange("a p k n -> (a p) k n")).then_inc(y_in[s], 16)
                    sp.wait_ge(x2_ready, BASE + it * 8 + 2 * s - 2)
                    sp.dma_start(xt[:, s % 2, :], x_t[ds(it * 4 + s, 1)].rearrange("a p d -> (a p) d")).then_inc(x_in[s % 2], 16)

        @block.gpsimd
        def _(pool):
            pool.memset(rw[:, :, :], 0.0).then_inc(rw_zero, 1)
            pool.memset(ones[:, :], 1.0).then_inc(rw_zero, 1)
            with pool.Fori(0, NT // 2) as it:
                for s in range(2):
                    t = it * 2 + s
                    pool.wait_ge(sq_ready, BASE + t + 1)
                    pool.tensor_tensor(sq[:, s, 0:256], sq[:, s, 0:256], sq[:, s, 256:512], ALU.add).then_inc(sum1, 1)
                    pool.wait_ge(sum1, BASE + t + 1)
                    pool.tensor_tensor(sq[:, s, 0:128], sq[:, s, 0:128], sq[:, s, 128:256], ALU.add).then_inc(sum2, 1)

        @block.tensor
        def _(pe):
            pe.wait_ge(rw_zero, BASE + 2)

            def half(t, q, banks, k0, done, free):
                pe.wait_ge(free, BASE + t * 2)
                pe.wait_ge(y_split, BASE + t + 1)
                for c in range(2):
                    for k in range(k0, k0 + 4):
                        for i, (y, w) in enumerate(((y_hi, wo_hi), (y_hi, wo_lo), (y_lo, wo_hi))):
                            last = pe.matmul(banks[c][:, :], y[:, q % 2, k, :], w[:, k, c * 512:(c + 1) * 512],
                                             start=(k == k0 and i == 0), stop=(k == k0 + 3 and i == 2))
                    last.then_inc(done, 1)

            def transposes(t, s):
                pe.wait_ge(h_ready, BASE + t + 1)
                pe.wait_ge(hT_ready, BASE + t * 2)
                for k in range(KC):
                    last = pe.transpose(pt[k // 4][:, (k % 4) * P:(k % 4 + 1) * P], h[:, s, k * P:(k + 1) * P], ident[:, :])
                    if k % 4 == 3:
                        last.then_inc(tr, 1)

            def logits(t):
                pe.wait_ge(hT_ready, BASE + t * 2 + 2)
                pe.wait_ge(lg_ready, BASE + t)
                for k in range(KC):
                    last = pe.matmul(pl[:, 0:P], hT[:, k, :], rw[:, k, :], start=(k == 0), stop=(k == KC - 1))
                last.then_inc(lg_mm, 1)

            def step(t, q, behind=2, ahead=True):
                s = q % 2
                pe.wait_ge(sum2, BASE + t + 1)
                pe.wait_ge(rA_ms, BASE + t)
                pe.matmul(psq[:, 0:P], sq[:, s, 0:P], ones[:, :], start=True, stop=True).then_inc(ssq_mm, 1)
                if not behind:
                    pe.wait_ge(w_ready, BASE + KC // 2)
                half(t, q, pA, 0, projA, xa_ready)
                if not behind:
                    pe.wait_ge(w_ready, BASE + KC)
                if behind > 1:
                    logits(t - 2)
                half(t, q, pB, 4, projB, x2_ready)
                if behind:
                    transposes(t - 1, 1 - s)

            in_rounds(pe, step)
            logits(NT - 2)
            transposes(NT - 1, 1)
            logits(NT - 1)

        @block.scalar
        def _(act):
            def squares(t, q):
                s = q % 2
                act.wait_ge(y_in[q], BASE + (t - q) * 4 + 16)
                act.wait_ge(ssq_mm, BASE + t - 1)
                act.activation(sq[:, s, :], yt[:, q, 0:4, :].rearrange("p k n -> p (k n)"), ACT.Square).then_inc(sq_ready, 1)
                act.wait_ge(projB, BASE + (t - s) * 2)
                act.activation(y_hi[:, s, :, :], yt[:, q, :, :], ACT.Copy).then_inc(y_rounded, 1)

            def turned(t, s):
                for b in range(2):
                    act.wait_ge(tr, BASE + t * 2 + b + 1)
                    act.wait_ge(lg_mm, BASE + t)
                    act.activation(hT[:, 4 * b:4 * b + 4, :], pt[b].rearrange("p (k n) -> p k n", k=4), ACT.Copy).then_inc(hT_ready, 1)
                act.dma_start(dram["H2"][ds(t * P, P), :], h[:, s, :]).then_inc(h_out[s], 16)

            def step(t, q, behind=2, ahead=True):
                s = q % 2
                act.wait_ge(rA_ms, BASE + t + 1)
                act.activation(st[:, s, 2:3], st[:, s, 1:2], ACT.Sqrt).then_inc(rA_ready, 1)
                if ahead:
                    squares(t + 1, (q + 1) % 4)
                if behind:
                    turned(t - 1, 1 - s)
                act.wait_ge(x2_ready, BASE + t * 2 + 2)
                act.dma_start(dram["X2"][ds(t, 1)].rearrange("a p d -> (a p) d"), X2[:, q, :]).then_inc(x2_out[q], 16)
                act.wait_ge(s2_ready, BASE + t)
                act.activation(junk[:, :], X2[:, q, :], ACT.Square, accum_out=st[:, s, 4:5]).then_inc(s2_ready, 1)
                act.wait_ge(ms2, BASE + t + 1)
                act.activation(st[:, s, 6:7], st[:, s, 5:6], ACT.Sqrt).then_inc(rs2, 1)

            squares(0, 0)
            in_rounds(act, step)
            turned(NT - 1, 1)
            for s in range(2):
                act.wait_ge(h_out[s], BASE + 16 * (NT // 2))
            for q in range(4):
                act.wait_ge(x2_out[q], BASE + 16 * (NT // 4))

        @block.vector
        def _(dve):
            def root(t, s, col, src, width, first, done):
                dve.tensor_scalar(st[:, s, col:col + 1], src, 1.0 / width, EPS, ALU.mult, ALU.add).then_inc(first, 1)
                dve.wait_ge(first, BASE + t + 1)
                dve.reciprocal(st[:, s, col + 1:col + 2], st[:, s, col:col + 1]).then_inc(done, 1)

            def add_bias(t):
                dve.wait_ge(lg_mm, BASE + t + 1)
                dve.tensor_tensor(LG[:, ds(t, 1), :].rearrange("p a n -> p (a n)"), pl[:, 0:NL], rb[:, :], ALU.add).then_inc(lg_ready, 1)

            def split(t, q):
                s = q % 2
                dve.wait_ge(y_rounded, BASE + t + 1)
                dve.wait_ge(projB, BASE + (t - s) * 2)
                dve.tensor_tensor(y_lo[:, s, :, :], yt[:, q, :, :], y_hi[:, s, :, :].bitcast(F32), ALU.subtract).then_inc(y_split, 1)

            def step(t, q, behind=2, ahead=True):
                s = q % 2
                dve.wait_ge(ssq_mm, BASE + t + 1)
                dve.wait_ge(rA_ready, BASE + t - 1)
                root(t, s, 0, psq[:, 0:1], CH, rA_first, rA_ms)
                dve.wait_ge(rA_ready, BASE + t + 1)
                dve.wait_ge(x_in[s], BASE + (t - s) * 8 + 16)
                for c in range(2):
                    dve.wait_ge(projA, BASE + t * 2 + c + 1)
                    dve.scalar_tensor_tensor(out=xt[:, s, c * 512:(c + 1) * 512], in0=pA[c][:, :], scalar=st[:, s, 2:3],
                                             in1=xt[:, s, c * 512:(c + 1) * 512], op0=ALU.mult, op1=ALU.add).then_inc(xa_ready, 1)
                if ahead:
                    split(t + 1, (q + 1) % 4)
                if behind > 1:
                    add_bias(t - 2)
                for c in range(2):
                    dve.wait_ge(projB, BASE + t * 2 + c + 1)
                    dve.wait_ge(xa_ready, BASE + t * 2 + 2)
                    dve.wait_ge(x2_out[q], BASE + (t - q) * 4)
                    dve.scalar_tensor_tensor(out=X2[:, q, c * 512:(c + 1) * 512], in0=pB[c][:, :], scalar=rB[:, ds(t, 1)],
                                             in1=xt[:, s, c * 512:(c + 1) * 512], op0=ALU.mult, op1=ALU.add).then_inc(x2_ready, 1)
                dve.wait_ge(s2_ready, BASE + t + 1)
                root(t, s, 4, st[:, s, 4:5], D, ms2_first, ms2)
                dve.wait_ge(rs2, BASE + t + 1)
                dve.wait_ge(h_out[s], BASE + (t - s) * 8)
                dve.wait_ge(tr, BASE + t * 2 - 2)
                dve.scalar_tensor_tensor(out=h[:, s, :], in0=X2[:, q, :], scalar=st[:, s, 6:7],
                                         in1=gain[:, :], op0=ALU.mult, op1=ALU.mult).then_inc(h_ready, 1)

            split(0, 0)
            for k in range(KC):
                dve.wait_ge(wo_in[k // 2], BASE + 16)
                g = gAB[:, k // 4, k % 4:k % 4 + 1]
                dve.tensor_scalar(wo_hi[:, k, :], wo[:, k, :], g, None, ALU.mult).then_inc(w_rounded, 1)
                dve.wait_ge(w_rounded, BASE + k + 1)
                dve.scalar_tensor_tensor(out=wo_lo[:, k, :], in0=wo[:, k, :], scalar=g, in1=wo_hi[:, k, :].bitcast(F32),
                                         op0=ALU.mult, op1=ALU.subtract).then_inc(w_ready, 1)
            dve.wait_ge(w_in_, BASE + 16 * N_W)
            in_rounds(dve, step)
            for t in (NT - 2, NT - 1):
                add_bias(t)
            dve.wait_ge(lg_ready, BASE + NT)


def route(nc, dram, LG, gates, slots, idx, nblk, ident):
    NL = N_GROUPS + N_EXP
    FAR = 99.0
    with ExitStack() as ctx:
        sb = lambda name, shape, dt=F32: ctx.enter_context(nc.sbuf_tensor(name, shape, dt))
        sem = PhaseSemaphores(nc, ctx)
        tri, ones = sb("tri", [P, P]), sb("ones6", [P, P])
        pos8 = sb("pos8", [P, PER_GROUP])
        thr = sb("thr", [P, NT - 1])
        tok = sb("tok", [P, NT], I32)
        zero = sb("zero6", [P, IDX_COLS], I32)
        m4, c4, o4 = sb("m4", [P, NT]), sb("c4", [P, NT, 4]), sb("o4", [P, NT, 4])
        e4, gp = sb("e4", [P, NT, 4]), sb("gp", [P, NT])
        t32, sel = sb("t32", [P, NT, N_GROUPS, PER_GROUP]), sb("sel", [P, NT, PER_GROUP])
        m1, m2, c8 = sb("m1", [P, NT]), sb("m2", [P, NT]), sb("c8", [P, NT, PER_GROUP])
        o1, o2 = sb("o1", [P, NT, PER_GROUP]), sb("o2", [P, NT, PER_GROUP])
        M = [sb(f"M{i}", [P, NT, N_GROUPS, PER_GROUP]) for i in range(2)]
        Ms = sb("Ms", [P, NT, N_EXP])
        base = sb("base", [P, NT + 1, N_EXP])
        over = sb("over", [P, N_EXP, NT - 1])
        nb, cum = sb("nb", [P, N_EXP]), sb("cum", [P, N_EXP])
        pos = sb("pos", [P, NT, N_EXP])
        sl = sb("sl", [P, 2, NT])
        ex, one1 = sb("ex", [P, NT]), sb("one1", [P, NT])
        rows_i, rows_f = sb("rows_i", [IDX_COLS, P], I32), sb("rows_f", [P, P])
        pp, pt = ctx.enter_context(nc.psum_tensor("pp", [P, 512], F32)), ctx.enter_context(nc.psum_tensor("ptot", [P, 512], F32))
        pr = ctx.enter_context(nc.psum_tensor("prows", [P, 512], F32))
        c_in, steps, e_ready, exp_done, M_ready, counted = (sem(n) for n in ("c_in", "r_steps", "e_ready", "exp_done", "M_ready", "counted"))
        filled, slots_ready, zeroed, rows_in, rows_ready, rows_t = (sem(n) for n in ("filled", "slots_ready", "zeroed6", "rows_in", "rows_ready", "rows_t"))
        scattered = sem("scattered", 0)
        block = sem.begin()

        @block.sync
        def _(sp):
            for dst, name in ((tri, "tri"), (ones, "ones"), (pos8, "pos8"), (thr, "thr"), (tok, "tok")):
                sp.dma_start(dst[:, :], dram[name]).then_inc(c_in, 16)
            sp.wait_ge(zeroed, BASE + 1)
            sp.dma_start(dram["slot_tok"].rearrange("(p b) o -> p (b o)", p=P), zero[:, :]).then_inc(filled, 16)
            sp.wait_ge(scattered, 16 * 2 * NT)
            sp.dma_start(rows_i[:, :], dram["slot_tok"].rearrange("(b p) o -> b (p o)", p=P)).then_inc(rows_in, 16)

        @block.gpsimd
        def _(pool):
            pool.memset(zero[:, :], 0).then_inc(zeroed, 1)
            pool.wait_ge(filled, BASE + 16)
            pool.wait_ge(slots_ready, BASE + 1)
            pool.wait_ge(c_in, BASE + 16 * 5)
            for c in range(2):
                for t in range(NT):
                    pool.indirect_dma_start(out=dram["slot_tok"], out_offset=bass.IndirectOffsetOnAxis(ap=slots[:, c, t:t + 1], axis=0),
                                            in_=tok[:, t:t + 1], in_offset=None).then_inc(scattered, 16)
            pool.wait_ge(scattered, 16 * 2 * NT)

        @block.tensor
        def _(pe):
            pe.wait_ge(c_in, BASE + 16 * 5)
            pe.wait_ge(M_ready, BASE + 1)
            rhs = Ms.rearrange("p t e -> p (t e)")
            pe.matmul(pp[:, :], tri[:, :], rhs, start=True, stop=True)
            pe.matmul(pt[:, :], ones[:, :], rhs, start=True, stop=True).then_inc(counted, 1)
            pe.wait_ge(rows_ready, BASE + 2)
            pe.transpose(pr[:, 0:P], rows_f[:, :], ident[:, :]).then_inc(rows_t, 1)

        @block.scalar
        def _(act):
            act.wait_ge(e_ready, BASE + 1)
            act.activation(e4[:, :, :], e4[:, :, :], ACT.Exp).then_inc(exp_done, 1)
            act.wait_ge(e_ready, BASE + 2)
            act.activation(ex[:, :], ex[:, :], ACT.Exp).then_inc(exp_done, 1)

        @block.vector
        def _(dve):
            step = Steps(dve, steps)
            tt = lambda out, a, b, op: step(dve.tensor_tensor(out, a, b, op))
            over_last = lambda a, n: a.unsqueeze(len(a.shape)).broadcast_to([*a.shape, n])

            def first_max(x, m, c, onehot, n):
                place = pos8[:, 0:n].unsqueeze(1).broadcast_to([P, NT, n])
                step(dve.tensor_reduce(m[:, :], x, AX.X, ALU.max))
                tt(c, x, over_last(m[:, :], n), ALU.is_equal)
                tt(c, c, place, ALU.mult)
                step(dve.tensor_reduce(one1[:, :], c, AX.X, ALU.min))
                tt(onehot, place, over_last(one1[:, :], n), ALU.is_equal)

            dve.wait_ge(c_in, BASE + 16 * 5)
            lg, le = LG[:, :, 0:N_GROUPS], LG[:, :, N_GROUPS:NL].rearrange("p t (g e) -> p t g e", g=N_GROUPS)
            first_max(lg, m4, c4[:, :, :], o4[:, :, :], N_GROUPS)
            dve.tensor_tensor(e4[:, :, :], lg, over_last(m4[:, :], 4), ALU.subtract).then_inc(e_ready, 1)
            tt(t32[:, :, :, :], le, over_last(o4[:, :, :], PER_GROUP), ALU.mult)
            step(dve.tensor_reduce(sel[:, :, :], t32.rearrange("p t g e -> p t e g"), AX.X, ALU.add))
            first_max(sel[:, :, :], m1, c8[:, :, :], o1[:, :, :], PER_GROUP)
            step(dve.scalar_tensor_tensor(out=sel[:, :, :], in0=o1[:, :, :], scalar=-1e30, in1=sel[:, :, :], op0=ALU.mult, op1=ALU.add))
            first_max(sel[:, :, :], m2, c8[:, :, :], o2[:, :, :], PER_GROUP)
            dve.tensor_tensor(ex[:, :], m2[:, :], m1[:, :], ALU.subtract).then_inc(e_ready, 1)
            for i, o in enumerate((o1, o2)):
                tt(M[i][:, :, :, :], over_last(o4[:, :, :], PER_GROUP), o[:, :, :].unsqueeze(2).broadcast_to([P, NT, N_GROUPS, PER_GROUP]), ALU.mult)
            flat = [m.rearrange("p t g e -> p t (g e)") for m in M]
            dve.tensor_tensor(Ms[:, :, :], flat[0], flat[1], ALU.add).then_inc(M_ready, 1)
            dve.wait_ge(exp_done, BASE + 2)
            step(dve.tensor_reduce(gp[:, :], e4[:, :, :], AX.X, ALU.add))
            step(dve.tensor_scalar(one1[:, :], ex[:, :], 1.0, None, ALU.add))
            tt(gp[:, :], gp[:, :], one1[:, :], ALU.mult)
            step(dve.reciprocal(gates[:, 0, :], gp[:, :]))
            tt(gates[:, 1, :], gates[:, 0, :], ex[:, :], ALU.mult)
            dve.wait_ge(counted, BASE + 1)
            step(dve.memset(base[:, 0, :], 0.0))
            for t in range(NT):
                tt(base[:, t + 1, :], base[:, t, :], pt[:, t * N_EXP:(t + 1) * N_EXP], ALU.add)
            tt(over[:, :, :], over_last(base[:, NT, :], NT - 1), thr[:, :].unsqueeze(1).broadcast_to([P, N_EXP, NT - 1]), ALU.is_gt)
            step(dve.tensor_reduce(nb[:, :], over[:, :, :], AX.X, ALU.add))
            step(dve.tensor_scalar(nb[:, :], nb[:, :], 1.0, None, ALU.add))
            step(dve.memset(over[:, :, 0], 1.0))
            step(dve.tensor_tensor_scan(cum[:, :], over[:, :, 0], nb[:, :], 0.0, ALU.mult, ALU.add))
            step(dve.tensor_copy(nblk[:, 0, :], nb[:, :]))
            step(dve.tensor_copy(nblk[:, 1, :], cum[:, :]))
            tt(cum[:, :], cum[:, :], nb[:, :], ALU.subtract)
            step(dve.tensor_scalar(cum[:, :], cum[:, :], float(P), float(LEAD * P), ALU.mult, ALU.add))
            tt(pos[:, :, :], pp.rearrange("p (t e) -> p t e", t=NT), base[:, 0:NT, :], ALU.add)
            tt(pos[:, :, :], pos[:, :, :], cum[:, :].unsqueeze(1).broadcast_to([P, NT, N_EXP]), ALU.add)
            for i in range(2):
                tt(flat[i], flat[i], pos[:, :, :], ALU.mult)
                step(dve.tensor_reduce(sl[:, i, :], flat[i], AX.X, ALU.add))
            dve.tensor_copy(slots[:, :, :], sl[:, :, :]).then_inc(slots_ready, 1)
            step(dve.memset(rows_f[:, :], 0.0))
            dve.wait_ge(rows_in, BASE + 16)
            dve.tensor_copy(rows_f[0:IDX_COLS, :], rows_i[:, :]).then_inc(rows_ready, 2)
            dve.wait_ge(rows_t, BASE + 1)
            step(dve.tensor_copy(idx[:, :], pr[:, 0:IDX_COLS]))


def experts(nc, dram, nblk, idx, ident):
    with ExitStack() as ctx:
        sb = lambda name, shape, dt=F32: ctx.enter_context(nc.sbuf_tensor(name, shape, dt))
        sem = PhaseSemaphores(nc, ctx)
        FT = D_EXP // P
        SLABS = KC + FT
        PAIRS, H_PAIRS = SLABS // 2, KC // 2
        raw = sb("w_raw", [P, SLABS, D])
        wh = [sb("wh_hi", [P, KC, D], F32R), sb("wh_lo", [P, KC, D], F32R)]
        wy = [sb("wy_hi", [P, 2 * FT, D], F32R), sb("wy_lo", [P, 2 * FT, D], F32R)]
        cur = sb("curidx", [P, 1], I32)
        xg = sb("xg", [P, D])
        x_hi, x_lo = sb("x_hi", [P, KC, P], F32R), sb("x_lo", [P, KC, P], F32R)
        s1, a = sb("s1", [P, D_EXP]), sb("a", [P, D_EXP])
        a_hi, a_lo = sb("a_hi", [P, FT, P], F32R), sb("a_lo", [P, FT, P], F32R)
        yb = sb("yb", [P, D])
        bank = lambda name: ctx.enter_context(nc.psum_tensor(name, [P, 512], F32))
        p1, p3, pta = bank("p1"), bank("p3"), bank("pta")
        px, py = [bank("px0"), bank("px1")], [bank("pyy0"), bank("pyy1")]
        raw_in = [sem(f"raw_in{r}") for r in range(SLABS)]
        pool_passed, act_passed = sem("pool_passed"), sem("act_passed")
        xg_in, y_out = sem("xg_in", 0), sem("ye_out")
        rounded, lowered, used = sem("w_rnd"), sem("w_low"), sem("w_used")
        idx_ready, trx, xhi_ready, xlo_ready = sem("idx_ready"), sem("trx"), sem("xhi_ready"), sem("xlo_ready")
        s_ready, a_ready, tra, ahi_ready, alo_ready, y_done, y_evac = (
            sem(n) for n in ("s_ready", "a_ready", "tra", "ahi_ready", "alo_ready", "y_done", "y_evac"))

        def per_block(eng, name, body, start=None, on=lambda e, r: None):
            B = eng.alloc_register(f"block_{name}")
            eng.reg_mov(B, 0)
            with eng.Fori(0, N_EXP // 2) as e2:
                for r in range(2):
                    e = e2 * 2 + r
                    if start:
                        start(e, eng.snap(B), r)
                    n = eng.value_load(nblk[0:1, 0, ds(e, 1)], min_val=1, max_val=NT)
                    with eng.Fori(0, n):
                        body(e, eng.snap(B))
                        on(e, r)
                        eng.reg_add(B, B, 1)
            return eng.snap(B)

        block = sem.begin()

        @block.sync
        def _(sp):
            with sp.Fori(0, N_EXP) as e:
                for j in range(SLABS):
                    sp.wait_ge(lowered, BASE + (e - 1) * PAIRS + j // 2 + 1)
                    parts = [("exp_w1", 0, j), ("exp_w3", 1, j)] if j < KC else [("exp_w2", 0, j - KC)]
                    width = D // len(parts)
                    for name, c, k in parts:
                        src = dram[name].rearrange("o e (k p) f -> p (o e) k f", p=P)[:, ds(e, 1), k]
                        sp.dma_start(raw[:, j, c * width:(c + 1) * width], src.rearrange("p a f -> p (a f)")).then_inc(raw_in[j], 16)

        @block.gpsimd
        def _(pool):
            def gather(B):
                pool.tensor_copy(cur[:, :], idx[:, ds(B + LEAD, 1)]).then_inc(idx_ready, 1)
                pool.wait_ge(idx_ready, BASE + B + 1)
                pool.sem_inc(pool_passed, 1)
                pool.indirect_dma_start(out=xg[:, :], out_offset=None, in_=dram["H2"],
                                        in_offset=bass.IndirectOffsetOnAxis(ap=cur[:, :], axis=0)).then_inc(xg_in, 16)

            def gather_after(B):
                pool.wait_ge(trx, BASE + B * 2 + 2)
                pool.wait_ge(xg_in, B * 16 + 16)
                gather(B + 1)

            gather(0)
            gather_after(0)

            def body(e, B):
                gather_after(B + 1)

            B = per_block(pool, "pool", body)
            pool.wait_ge(xg_in, B * 16 + 32)
            pool.sem_inc(pool_passed, 1)

        @block.tensor
        def _(pe):
            e1, place1 = pe.alloc_register("expert1"), pe.alloc_register("place1")
            pe.reg_mov(e1, 0)
            pe.reg_mov(place1, 0)

            def products(acc, hi, lo, k, whi, wlo, n):
                for i, (x, w) in enumerate(((hi, whi), (hi, wlo), (lo, whi))):
                    mm = pe.matmul(acc[:, :], x[:, k, :], w, start=(k == 0 and i == 0), stop=(k == n - 1 and i == 2))
                return mm

            def transpose_x(B):
                pe.wait_ge(xg_in, B * 16 + 16)
                for h in range(2):
                    pe.wait_ge(xlo_ready, BASE + B * 2 + h - 1)
                    for k in range(4 * h, 4 * h + 4):
                        last = pe.transpose(px[h][:, (k % 4) * P:(k % 4 + 1) * P], xg[:, k * P:(k + 1) * P], ident[:, :])
                    last.then_inc(trx, 1)

            def transpose_a():
                for k in range(FT):
                    last = pe.transpose(pta[:, k * P:(k + 1) * P], a[:, k * P:(k + 1) * P], ident[:, :])
                last.then_inc(tra, 1)

            def y(B):
                e, place = pe.snap(e1), pe.snap(place1)
                pe.wait_ge(alo_ready, BASE + B + 1)
                pe.wait_ge(y_evac, BASE + B + 1)
                for k in range(FT):
                    if k % 2 == 0:
                        pe.wait_ge(lowered, BASE + e * PAIRS + H_PAIRS + k // 2 + 1)
                    for c in range(2):
                        whi, wlo = (w[:, ds(place + k, 1), c * 512:(c + 1) * 512].rearrange("p a n -> p (a n)") for w in wy)
                        mm = products(py[c], a_hi, a_lo, k, whi, wlo, FT)
                mm.then_inc(y_done, 1)

            pe.wait_ge(a_ready, BASE + 1)
            transpose_a()
            transpose_x(0)

            def body(e, B):
                pe.wait_ge(a_ready, BASE + B + 1)
                for k in range(KC):
                    if k % 4 == 0:
                        pe.wait_ge(xlo_ready, BASE + B * 2 + k // 4 + 1)
                    if k % 2 == 0:
                        pe.wait_ge(lowered, BASE + e * PAIRS + k // 2 + 1)
                    for acc, cols in ((p1, slice(0, D_EXP)), (p3, slice(D_EXP, 2 * D_EXP))):
                        mm = products(acc, x_hi, x_lo, k, wh[0][:, k, cols], wh[1][:, k, cols], KC)
                    mm.then_inc(used, 1)
                transpose_x(B + 1)
                y(B)
                pe.wait_ge(a_ready, BASE + B + 2)
                transpose_a()

            def on(e, r):
                pe.reg_mov(e1, e)
                pe.reg_mov(place1, r * FT)

            y(per_block(pe, "pe", body, on=on))

        @block.scalar
        def _(act):
            def split_x(B):
                for h in range(2):
                    act.wait_ge(trx, BASE + B * 2 + h + 1)
                    act.activation(x_hi[:, 4 * h:4 * h + 4, :], px[h].rearrange("p (k n) -> p k n", k=4), ACT.Copy).then_inc(xhi_ready, 1)

            def split_a(B):
                act.wait_ge(tra, BASE + B + 1)
                act.activation(a_hi[:, :, :], pta.rearrange("p (k n) -> p k n", k=FT), ACT.Copy).then_inc(ahi_ready, 1)

            def store_y(B):
                act.wait_ge(y_done, BASE + B + 1)
                act.wait_ge(y_out, BASE + B * 16)
                for c in range(2):
                    copy = act.activation(yb[:, c * 512:(c + 1) * 512], py[c][:, :], ACT.Copy)
                copy.then_inc(y_evac, 1)
                act.wait_ge(y_evac, BASE + B + 1)
                act.dma_start(dram["YB"][ds(B * P, P), :], yb[:, :]).then_inc(y_out, 16)

            def split_w(e, B, r):
                for pair in range(PAIRS):
                    j = 2 * pair
                    for slab in (j, j + 1):
                        act.wait_ge(raw_in[slab], BASE + (e + 1) * (32 if slab < KC else 16))
                    if pair < H_PAIRS:
                        act.wait_ge(used, BASE + B * KC + j + 2 - KC)
                        place = wh[0][:, j:j + 2, :]
                    else:
                        act.wait_ge(y_done, BASE + B + 1)
                        place = wy[0][:, r * FT + j - KC:r * FT + j - KC + 2, :]
                    act.activation(place, raw[:, j:j + 2, :], ACT.Copy).then_inc(rounded, 1)

            split_x(0)

            def body(e, B):
                split_a(B)
                store_y(B)
                act.wait_ge(used, BASE + B * KC + KC)
                act.wait_ge(a_ready, BASE + B + 1)
                act.activation(s1[:, :], p1[:, :], ACT.Silu).then_inc(s_ready, 1)
                split_x(B + 1)

            B = per_block(act, "act", body, split_w)
            split_a(B)
            for last in range(2):
                store_y(B + last)
            act.wait_ge(y_out, BASE + B * 16 + 32)
            act.sem_inc(act_passed, 1)

        @block.vector
        def _(dve):
            def split_x(B):
                for h in range(2):
                    dve.wait_ge(xhi_ready, BASE + B * 2 + h + 1)
                    dve.tensor_tensor(x_lo[:, 4 * h:4 * h + 4, :], px[h].rearrange("p (k n) -> p k n", k=4),
                                      x_hi[:, 4 * h:4 * h + 4, :].bitcast(F32), ALU.subtract).then_inc(xlo_ready, 1)

            def split_a(B):
                dve.wait_ge(ahi_ready, BASE + B + 1)
                dve.tensor_tensor(a_lo[:, :, :], pta.rearrange("p (k n) -> p k n", k=FT), a_hi[:, :, :].bitcast(F32), ALU.subtract).then_inc(alo_ready, 1)

            def split_w(e, B, r):
                for pair in range(PAIRS):
                    j = 2 * pair
                    dve.wait_ge(rounded, BASE + e * PAIRS + pair + 1)
                    hi, lo = (w[:, j:j + 2, :] if pair < H_PAIRS else v[:, r * FT + j - KC:r * FT + j - KC + 2, :] for w, v in zip(wh, wy))
                    dve.tensor_tensor(lo, raw[:, j:j + 2, :], hi.bitcast(F32), ALU.subtract).then_inc(lowered, 1)

            dve.memset(py[0][:, :], 0.0)
            dve.memset(py[1][:, :], 0.0).then_inc(y_done, 1)
            dve.memset(a[:, :], 0.0).then_inc(a_ready, 1)
            split_x(0)

            def body(e, B):
                split_a(B)
                dve.wait_ge(s_ready, BASE + B + 1)
                dve.wait_ge(tra, BASE + B + 1)
                dve.tensor_tensor(a[:, :], p3[:, :], s1[:, :], ALU.mult).then_inc(a_ready, 1)
                split_x(B + 1)

            split_a(per_block(dve, "dve", body, split_w))


def combine(nc, dram, gates, slots):
    with ExitStack() as ctx:
        sb = lambda name, shape, dt=F32: ctx.enter_context(nc.sbuf_tensor(name, shape, dt))
        sem = PhaseSemaphores(nc, ctx)
        y = sb("ycomb", [P, 4, 2, D])
        x = sb("xcomb", [P, 4, D])
        out = sb("outt", [P, 2, D])
        gain = sb("gain_fin", [P, D])
        st = sb("st8", [P, 2, 4])
        gain_in, y_in = sem("gain8_in"), [sem(f"yc_in{s}", 0) for s in range(4)]
        x_in = [sem(f"xc_in{s}") for s in range(4)]
        s1, s2, sqd, m1, m2, rs, o_ready = (sem(n) for n in ("c_s1", "c_s2", "c_sq", "c_m1", "c_m2", "c_rs", "c_out"))
        o_out = [sem(f"o_out{s}") for s in range(2)]
        out_t = dram["out"].rearrange("o (p l) d -> l p (o d)", l=NT)
        block = sem.begin()

        @block.sync
        def _(sp):
            sp.dma_start(gain[:, :], dram["norm_final_g"].partition_broadcast(P)).then_inc(gain_in, 16)
            def load(t, q):
                sp.dma_start(x[:, q, :], dram["X2"][ds(t, 1)].rearrange("a p d -> (a p) d")).then_inc(x_in[q], 16)

            for q in range(4):
                load(q, q)
            def store(t, q):
                sp.wait_ge(o_ready, BASE + t + 1)
                sp.dma_start(out_t[ds(t, 1)].rearrange("a p d -> (a p) d"), out[:, q % 2, :]).then_inc(o_out[q % 2], 16)

            with sp.Fori(0, NT // 4 - 1) as it:
                for q in range(4):
                    store(it * 4 + q, q)
                    load(it * 4 + q + 4, q)
            for q in range(4):
                store(NT - 4 + q, q)
            for s in range(2):
                sp.wait_ge(o_out[s], BASE + 16 * (NT // 2))

        @block.gpsimd
        def _(pool):
            for t in range(NT):
                if t >= 4:
                    pool.wait_ge(s2, BASE + t - 3)
                for c in range(2):
                    pool.indirect_dma_start(out=y[:, t % 4, c, :], out_offset=None, in_=dram["YB"],
                                            in_offset=bass.IndirectOffsetOnAxis(ap=slots[:, c, t:t + 1], axis=0)).then_inc(y_in[t % 4], 16)

        @block.scalar
        def _(act):
            with act.Fori(0, NT // 4) as it:
                for q in range(4):
                    t, s = it * 4 + q, q % 2
                    act.wait_ge(s2, BASE + t + 1)
                    act.wait_ge(o_out[s], BASE + (t - s) * 8)
                    act.activation(out[:, s, :], x[:, q, :], ACT.Square, accum_out=st[:, s, 0:1]).then_inc(sqd, 1)
                    act.wait_ge(m2, BASE + t + 1)
                    act.activation(st[:, s, 3:4], st[:, s, 2:3], ACT.Sqrt).then_inc(rs, 1)

        @block.vector
        def _(dve):
            dve.wait_ge(gain_in, BASE + 16)

            def add_expert(t, q, c):
                done = (s1, s2)[c]
                if c == 0:
                    dve.wait_ge(x_in[q], BASE + (t - q) * 4 + 16)
                    dve.wait_ge(y_in[q], (t - q) * 8 + 32)
                else:
                    dve.wait_ge(s1, BASE + t + 1)
                dve.scalar_tensor_tensor(out=x[:, q, :], in0=y[:, q, c, :], scalar=gates[:, c, ds(t, 1)], in1=x[:, q, :],
                                         op0=ALU.mult, op1=ALU.add).then_inc(done, 1)

            def root(t, q):
                s = q % 2
                dve.wait_ge(sqd, BASE + t + 1)
                dve.tensor_scalar(st[:, s, 1:2], st[:, s, 0:1], 1.0 / D, EPS, ALU.mult, ALU.add).then_inc(m1, 1)
                dve.wait_ge(m1, BASE + t + 1)
                dve.reciprocal(st[:, s, 2:3], st[:, s, 1:2]).then_inc(m2, 1)

            def scale(t, q):
                s = q % 2
                dve.wait_ge(rs, BASE + t + 1)
                dve.scalar_tensor_tensor(out=out[:, s, :], in0=x[:, q, :], scalar=st[:, s, 3:4], in1=gain[:, :],
                                         op0=ALU.mult, op1=ALU.mult).then_inc(o_ready, 1)

            def step(t, q, ahead=True):
                if ahead:
                    add_expert(t + 1, (q + 1) % 4, 0)
                root(t, q)
                if ahead:
                    add_expert(t + 1, (q + 1) % 4, 1)
                scale(t, q)

            for c in range(2):
                add_expert(0, 0, c)
            with dve.Fori(0, NT // 4 - 1) as it:
                for q in range(4):
                    step(it * 4 + q, q)
            for q in range(4):
                step(NT - 4 + q, q, ahead=q < 3)


def routing_tables():
    tau, p = np.arange(NT), np.arange(P)
    return dict(tri=np.triu(np.ones((P, P), np.float32), 1), ones=np.ones((P, P), np.float32),
                pos8=np.broadcast_to(np.arange(8, dtype=np.float32) - 99, (P, 8)).copy(),
                thr=np.broadcast_to(P * np.arange(1, NT, dtype=np.float32), (P, NT - 1)).copy(),
                tok=(tau[None] * P + p[:, None]).astype(np.int32))


def build(nc, dram):
    for name, shape, dt in (("L", [3, P, NT, CH], F32), ("YT", [NT, P, KC, P], F32), ("KA", [2, P, R // 2, CH], F32),
                            ("SA", [P, 2, NT, CH], F32), ("SI", [P, 2, NT, CH], F32), ("H2", [SEQ, D], F32), ("ZZ", [P, SEQ], F32), ("X2", [NT, P, D], F32),
                            ("YB", [N_SLOTS, D], F32), ("slot_tok", [(IDX_COLS) * P, 1], I32)):
        dram[name] = nc.dram_tensor(f"scratch_{name}", shape, dt, kind="Internal").ap()
    with ExitStack() as ctx:
        sb = lambda stack, name, shape, dt=F32: stack.enter_context(nc.sbuf_tensor(name, shape, dt))
        ident = sb(ctx, "ident", [P, P])
        dram["gAB"] = gAB = sb(ctx, "gAB", [P, 2, CT])
        with ExitStack() as phase:
            hT = sb(phase, "hT", [P, KC, SEQ])
            load_and_norm(nc, dram, hT, ident)
            project_and_lru(nc, dram, hT, ident)
        rB = sb(ctx, "rB", [P, NT])
        with ExitStack() as phase:
            invn = sb(phase, "invn", [P, 2, CH])
            cur = sb(phase, "cur", [P, NT, CH])
            filters(nc, dram, invn, cur)
            skip = sb(phase, "skip", [P, CH])
            stage = sb(phase, "stage", [P, 2, NT, CH])
            gate = sb(phase, "gate", [P, NT, CH])
            for o in range(2):
                conv_forward(nc, dram, o, cur, skip, stage)
                conv_blocks(nc, dram, o, gate)
                conv_inverse(nc, dram, o, cur, stage, gate, invn, rB, ident)
        LG = sb(ctx, "LG", [P, NT, N_GROUPS + N_EXP])
        gates, slots = sb(ctx, "gates", [P, 2, NT]), sb(ctx, "slots", [P, 2, NT], I32)
        idx = sb(ctx, "idx", [P, IDX_COLS], I32)
        nblk = sb(ctx, "nblk", [P, 2, N_EXP], I32)
        output_projection(nc, dram, LG, gAB, rB, ident)
        route(nc, dram, LG, gates, slots, idx, nblk, ident)
        experts(nc, dram, nblk, idx, ident)
        combine(nc, dram, gates, slots)


_INS = ["x", "norm_mix_g", "w_in", "lru_conv_w", "lru_conv_b", "lru_wr_f", "lru_br_f", "lru_wi_f", "lru_bi_f", "lru_lambda_f",
        "lru_wr_b", "lru_br_b", "lru_wi_b", "lru_bi_b", "lru_lambda_b", "hy_conv_w", "hy_conv_b",
        "hy_filt_w1", "hy_filt_b1", "hy_filt_freq1", "hy_filt_w2", "hy_filt_b2", "hy_filt_freq2", "hy_filt_w3", "hy_skip",
        "grp_norm_lru_g", "grp_norm_hy_g", "w_out", "norm_ffn_g", "router_group_w", "router_group_b",
        "router_expert_w", "router_expert_b", "exp_w1", "exp_w3", "exp_w2", "norm_final_g"]


def kernel(**inputs):
    import numpy as _np
    import concourse.bacc as _bacc
    from concourse import mybir as _mybir
    from concourse.bass_utils import run_bass_kernel_spmd as _run

    nc = _bacc.Bacc("TRN2", target_bir_lowering=False, num_devices=1)
    arrays, dram = {}, {}
    tables = {**transform_tables(), **routing_tables()}
    for name, a in [*((n, inputs[n]) for n in _INS), *tables.items()]:
        a = _np.ascontiguousarray(a)
        arrays[f"in_{name}_dram"] = a
        dram[name] = nc.dram_tensor(f"in_{name}_dram", a.shape, _mybir.dt.from_np(a.dtype), kind="ExternalInput").ap()
    dram["out"] = nc.dram_tensor("out_0_dram", (1, SEQ, D), F32, kind="ExternalOutput").ap()
    build(nc, dram)
    r = _run(nc, [arrays], core_ids=[0])
    return r.results[0]["out_0_dram"]
```
